# Optimizing a Trainium2 kernel written in Bass

```python
import jax, jax.numpy as jnp
from jax import lax
import numpy as np

D_MODEL = 1024
BATCH = 1
SEQ = 256
DEPTH = 4

N_MIXERS = 3
A_DILATIONS = (1, 4, 16)
A_WINDOWS = (128, 512, 2048)
A_GROUPS = 3
A_HEADS_PER_GROUP = 8
A_HEAD_DIM = 64
A_GROUP_WIDTH = A_HEADS_PER_GROUP * A_HEAD_DIM
A_STEPS = 128
A_BLOCK = 128
A_HEADS_TOTAL = A_GROUPS * A_HEADS_PER_GROUP
REL_BUCKETS = 32
REL_MAX_EXACT = REL_BUCKETS // 2
REL_MAX_DIST = 2048
B_WINDOWS = (2, 4, 8, 16)
B_GROUPS = 4
B_GROUP_WIDTH = D_MODEL // B_GROUPS
C_CHUNK = 128
C_GROUPS = 4
C_GROUP_WIDTH = D_MODEL // C_GROUPS
FFN_HIDDEN = -(-8 * D_MODEL // (3 * 256)) * 256
PLE_DIM = 256
N_A = (DEPTH + 2) // 3
N_B = (DEPTH + 1) // 3
N_C = DEPTH // 3
EPS = 1e-6
NEG = -1e30

kernel_name = "hybrid_dilated_pool_sgu_trunk"

def rmsnorm(x, g):
    xf = x.astype(jnp.float32)
    y = xf * lax.rsqrt(jnp.mean(xf * xf, axis=-1, keepdims=True) + EPS)
    return (y * g.astype(jnp.float32)).astype(x.dtype)

def t5_bucket(n):
    nf = np.maximum(n, 1).astype(np.float32)
    large = REL_MAX_EXACT + (np.log(nf / REL_MAX_EXACT) / np.log(REL_MAX_DIST / REL_MAX_EXACT)
                             * (REL_BUCKETS - REL_MAX_EXACT)).astype(np.int32)
    large = np.minimum(large, REL_BUCKETS - 1)
    return np.where(n < REL_MAX_EXACT, n, large).astype(np.int32)

def rel_bias_block(table_g, d):
    i = np.arange(A_BLOCK)[:, None]
    j = np.arange(2 * A_BLOCK)[None, :]
    rel = A_BLOCK + i - j
    valid = (rel >= 0) & (rel <= A_STEPS)
    bucket = t5_bucket(np.where(valid, rel, 0) * d)
    bias = jnp.transpose(table_g[bucket], (2, 0, 1))
    return bias, valid

def banded_branch(q, k, v, bias, valid):
    N, L, H, Dh = q.shape
    nb = -(-L // A_BLOCK)
    Lp = nb * A_BLOCK
    pad = ((0, 0), (0, Lp - L), (0, 0), (0, 0))
    qb, kb, vb = [jnp.pad(t, pad).reshape(N, nb, A_BLOCK, H, Dh) for t in (q, k, v)]

    def with_prev(t):
        prev = jnp.pad(t, ((0, 0), (1, 0), (0, 0), (0, 0), (0, 0)))[:, :-1]
        return jnp.concatenate([prev, t], axis=2)

    kk, vv = with_prev(kb), with_prev(vb)
    s = jnp.einsum('nbqhd,nbkhd->nhbqk', qb, kk).astype(jnp.float32) * (Dh ** -0.5)
    s = s + bias[:, None].astype(jnp.float32)
    key_pos = (np.arange(nb)[:, None, None] * A_BLOCK + np.arange(2 * A_BLOCK)[None, None, :] - A_BLOCK)
    mask = valid[None] & (key_pos >= 0)
    s = jnp.where(mask, s, NEG)
    m = jnp.max(s, axis=-1, keepdims=True)
    e = jnp.exp(s - m)
    den = jnp.sum(e, axis=-1, keepdims=True)
    o = jnp.einsum('nhbqk,nbkhd->nbqhd', (e / den).astype(v.dtype), vv)
    lse = (m + jnp.log(den))[..., 0]
    o = o.reshape(N, Lp, H, Dh)[:, :L]
    lse = jnp.transpose(lse, (0, 2, 3, 1)).reshape(N, Lp, H)[:, :L]
    return o, lse

def mixer_dilated(h, w_qkv, w_o, rel_table):
    B, S, _ = h.shape
    H, Dh = A_HEADS_PER_GROUP, A_HEAD_DIM
    qkv = (h @ w_qkv).reshape(B, S, 3, A_GROUPS, H, Dh)
    outs, lses = [], []
    for g, d in enumerate(A_DILATIONS):
        L = S // d

        def to_phase(t):
            return t.reshape(B, L, d, H, Dh).transpose(0, 2, 1, 3, 4).reshape(B * d, L, H, Dh)

        q, k, v = (to_phase(qkv[:, :, c, g]) for c in range(3))
        bias, valid = rel_bias_block(rel_table[:, g * H:(g + 1) * H], d)
        o, lse = banded_branch(q, k, v, bias, valid)
        outs.append(o.reshape(B, d, L, H, Dh).transpose(0, 2, 1, 3, 4).reshape(B, S, H, Dh))
        lses.append(lse.reshape(B, d, L, H).transpose(0, 2, 1, 3).reshape(B, S, H))
    w = jax.nn.softmax(jnp.stack(lses), axis=0)
    o = jnp.einsum('gbsh,gbshd->bshd', w, jnp.stack(outs).astype(jnp.float32))
    return o.reshape(B, S, A_GROUP_WIDTH).astype(h.dtype) @ w_o

def mixer_pool(h, w_in, w_grp, scale, w_out):
    B, S, _ = h.shape
    y = (h @ w_in).reshape(B, S, B_GROUPS, B_GROUP_WIDTH)
    pos = jnp.arange(1, S + 1, dtype=jnp.float32)[:, None]
    pooled = []
    for g, win in enumerate(B_WINDOWS):
        yg = y[:, :, g].astype(jnp.float32)
        c = jnp.cumsum(yg, axis=1)
        c_prev = jnp.pad(c, ((0, 0), (win, 0), (0, 0)))[:, :S]
        mean = (c - c_prev) / jnp.minimum(pos, win)
        pooled.append(mean - yg)
    z = jnp.stack(pooled, axis=2).astype(h.dtype)
    z = jnp.einsum('bsgc,gce->bsge', z, w_grp).reshape(B, S, D_MODEL) * scale
    return z @ w_out

def mixer_sgu(h, w_in, v_gain, w_s, b_s, w_out):
    B, S, _ = h.shape
    z = jax.nn.gelu(h @ w_in)
    u, v = jnp.split(z, 2, axis=-1)
    vf = v.astype(jnp.float32)
    mu = jnp.mean(vf, axis=-1, keepdims=True)
    var = jnp.mean(jnp.square(vf - mu), axis=-1, keepdims=True)
    vn = ((vf - mu) * lax.rsqrt(var + EPS) * v_gain.astype(jnp.float32)).astype(h.dtype)
    vn = vn.reshape(B, S // C_CHUNK, C_CHUNK, C_GROUPS, C_GROUP_WIDTH)
    wm = w_s * jnp.tril(jnp.ones((C_CHUNK, C_CHUNK), w_s.dtype))
    sp = jnp.einsum('gts,bnsgc->bntgc', wm, vn) + jnp.transpose(b_s)[:, :, None]
    out = u * sp.reshape(B, S, D_MODEL)
    return out @ w_out

def swiglu(h, w_gate, w_up, w_down):
    return (jax.nn.silu(h @ w_gate) * (h @ w_up)) @ w_down

def setup_inputs(seed: int = 0) -> dict:
    key = jax.random.key(seed)
    ks = jax.random.split(key, 24)
    f32 = jnp.float32

    def w(k, shape, fan_in):
        return jax.random.normal(k, shape, f32) * (fan_in ** -0.5)

    def gain(k, shape):
        return 1.0 + 0.1 * jax.random.normal(k, shape, f32)

    return {
        'x': jax.random.normal(ks[0], (BATCH, SEQ, D_MODEL), f32),
        'p': jax.random.normal(ks[1], (DEPTH, BATCH, SEQ, PLE_DIM), f32),
        'rel_table': 0.3 * jax.random.normal(ks[2], (REL_BUCKETS, A_HEADS_TOTAL), f32),
        'norm_mix': gain(ks[3], (DEPTH, D_MODEL)),
        'norm_ffn': gain(ks[4], (DEPTH, D_MODEL)),
        'norm_ple': gain(ks[5], (DEPTH, D_MODEL)),
        'final_norm': gain(ks[6], (D_MODEL,)),
        'a_w_qkv': w(ks[7], (N_A, D_MODEL, 3 * A_GROUPS * A_GROUP_WIDTH), D_MODEL),
        'a_w_o': w(ks[8], (N_A, A_GROUP_WIDTH, D_MODEL), A_GROUP_WIDTH),
        'b_w_in': w(ks[9], (N_B, D_MODEL, D_MODEL), D_MODEL),
        'b_w_grp': w(ks[10], (N_B, B_GROUPS, B_GROUP_WIDTH, B_GROUP_WIDTH), B_GROUP_WIDTH),
        'b_scale': gain(ks[11], (N_B, D_MODEL)),
        'b_w_out': w(ks[12], (N_B, D_MODEL, D_MODEL), D_MODEL),
        'c_w_in': w(ks[13], (N_C, D_MODEL, 2 * D_MODEL), D_MODEL),
        'c_v_gain': gain(ks[14], (N_C, D_MODEL)),
        'c_w_s': w(ks[15], (N_C, C_GROUPS, C_CHUNK, C_CHUNK), C_CHUNK),
        'c_b_s': gain(ks[16], (N_C, C_GROUPS, C_CHUNK)),
        'c_w_out': w(ks[17], (N_C, D_MODEL, D_MODEL), D_MODEL),
        'ffn_w_gate': w(ks[18], (DEPTH, D_MODEL, FFN_HIDDEN), D_MODEL),
        'ffn_w_up': w(ks[19], (DEPTH, D_MODEL, FFN_HIDDEN), D_MODEL),
        'ffn_w_down': w(ks[20], (DEPTH, FFN_HIDDEN, D_MODEL), FFN_HIDDEN),
        'ple_w_gate': w(ks[21], (DEPTH, D_MODEL, D_MODEL), D_MODEL),
        'ple_w_proj': w(ks[22], (DEPTH, PLE_DIM, D_MODEL), PLE_DIM),
    }

def reference(x, p, rel_table, norm_mix, norm_ffn, norm_ple, final_norm,
              a_w_qkv, a_w_o, b_w_in, b_w_grp, b_scale, b_w_out,
              c_w_in, c_v_gain, c_w_s, c_b_s, c_w_out,
              ffn_w_gate, ffn_w_up, ffn_w_down, ple_w_gate, ple_w_proj):
    h = x
    for i in range(DEPTH):
        hn = rmsnorm(h, norm_mix[i])
        kind, j = i % N_MIXERS, i // N_MIXERS
        if kind == 0:
            y = mixer_dilated(hn, a_w_qkv[j], a_w_o[j], rel_table)
        elif kind == 1:
            y = mixer_pool(hn, b_w_in[j], b_w_grp[j], b_scale[j], b_w_out[j])
        else:
            y = mixer_sgu(hn, c_w_in[j], c_v_gain[j], c_w_s[j], c_b_s[j], c_w_out[j])
        h = h + y
        h = h + swiglu(rmsnorm(h, norm_ffn[i]), ffn_w_gate[i], ffn_w_up[i], ffn_w_down[i])
        gate = jax.nn.sigmoid(rmsnorm(h, norm_ple[i]) @ ple_w_gate[i])
        h = h + (p[i] @ ple_w_proj[i]) * gate
    return rmsnorm(h, final_norm)


_drawn_inputs = setup_inputs


def setup_inputs(seed=0):
    import zlib

    import numpy as np

    out = dict(_drawn_inputs(seed))
    spreads = {}
    factors = {}
    for name, (base, spread) in spreads.items():
        noise = np.random.default_rng([zlib.crc32(name.encode()), seed]).standard_normal(out[name].shape)
        drawn = base * np.exp(spread * noise) if base else spread * noise
        out[name] = __import__('jax').numpy.asarray(drawn.astype(out[name].dtype))
    for name, factor in factors.items():
        out[name] = (out[name] * factor).astype(out[name].dtype)
    return out
```

```python
from contextlib import ExitStack

import numpy as np

import concourse.bass as bass
from concourse import mybir

F32 = mybir.dt.float32
F32R = mybir.dt.float32r
BF16 = mybir.dt.bfloat16
ALU = mybir.AluOpType
ACT = mybir.ActivationFunctionType

P = 128
SEQ = 256
D = 1024
KT = D // P
DEPTH = 4
GROUPS = 3
HEADS = 8
DH = 64
PAIRS = HEADS // 2
GW = HEADS * DH
QW = GROUPS * P
HIDDEN = 2816
HB = HIDDEN // SEQ
HKT = HIDDEN // P
PLE = 256
EPS = 1e-6
NEG = -1e30
SKEW = 3 * P
HALF = 4 * 512
MIXERS = [i % 3 for i in range(DEPTH)]

A_PANELS, B_PANELS, C_PANELS = 4 * PAIRS, 5, 6
F_PANELS, D_PANELS, G_PANELS = HB, 6, 3


def at(base, i, step):
    return base if i is None else base + i * step


class Counts:

    def __init__(self):
        n = 0
        t = 8
        hi = 4
        h = 4
        x = 4
        hid = 2
        dmas = []
        half = []
        self.n, self.t, self.hi, self.h, self.x, self.hid = {}, {}, {}, {}, {}, {}
        for layer, kind in enumerate(MIXERS):
            def mark(part):
                key = (layer, part)
                self.n[key], self.t[key], self.hi[key] = n, t, hi
                self.h[key], self.x[key], self.hid[key] = h, x, hid
            mark("mix")
            dmas += ([3] * 3 + ([3] * 3 + [1]) * (PAIRS - 1) + [3], [1] * B_PANELS, [1] * C_PANELS)[kind]
            dmas += [2] * (F_PANELS + 1) + [1] * (D_PANELS - 1 + G_PANELS)
            half += ([4 * QW] * 3 + ([4 * QW] * 3 + [512]) * (PAIRS - 1) + [4 * QW],
                     [HALF, HALF, 4 * SEQ, HALF, HALF], [HALF] * C_PANELS)[kind]
            half += [HALF] * F_PANELS + [HALF, HALF, 3 * 512] * 2 + [D, HALF, HALF]
            n += (A_PANELS, B_PANELS, C_PANELS)[kind]
            t += (4, 4, 9)[kind]
            hi += (4, 4, 8)[kind]
            h += (16, 4, 4)[kind]
            x += 4
            mark("ffn")
            n += F_PANELS
            t += HB
            hi += HB
            hid += 2 * HB
            mark("down")
            n += D_PANELS
            t += 5
            hi += 5
            h += 4
            x += 4
            mark("ple")
            n += G_PANELS
            h += 4
            if layer < DEPTH - 1:
                t += 4
                hi += 4
                x += 4
        self.panels = n
        self.half = half
        self.landed = [sum(dmas[i % 2:i + 1:2]) for i in range(n)]


def trunk(nc, x, p, rel_table, norm_mix, norm_ffn, norm_ple, final_norm, a_w_qkv, a_w_o,
          b_w_in, b_w_grp, b_scale, b_w_out, c_w_in, c_v_gain, c_w_s, c_b_s, c_w_out,
          ffn_w_gate, ffn_w_up, ffn_w_down, ple_w_gate, ple_w_proj,
          identity, bucket_of, pool_of, lower, out):
    cnt = Counts()
    last_layer = DEPTH - 1

    with ExitStack() as ctx:
        def sb(name, shape, dt=F32, scope=ctx):
            return scope.enter_context(nc.sbuf_tensor(name, shape, dt))

        def sem(name):
            return ctx.enter_context(nc.semaphore(name))

        raw = sb("raw", [P, 4, HALF])
        w_hi = sb("w_hi", [P, 2, 2 * HALF], F32R)
        w_lo = sb("w_lo", [P, 2, 2 * HALF], F32R)
        x_hi = sb("x_hi", [P, 2, KT, SEQ], F32R)
        x_lo = sb("x_lo", [P, 2, KT, SEQ], F32R)
        h = sb("h", [P, 2, D])
        ident = sb("ident", [P, P])
        rows = sb("rows", [12 * KT + KT + 4, P])
        cols = sb("cols", [P, 12 * KT + KT + 4])
        xf = sb("xf", [P, 2, 512])
        squares = sb("squares", [P, D], BF16)
        ssq = sb("ssq", [P, 26])
        mean_sq = sb("mean_sq", [P, 28])
        rinv = sb("rinv", [P, 28])
        rinv8 = sb("rinv8", [P, 2])
        half_r = sb("half_r", [P, 2])
        expo = sb("expo", [P, 1])
        gated = sb("gated", [P, 2, 512])
        prod = sb("prod", [P, 2, 512])
        p_rows = sb("p_rows", [P, 2, PLE])
        p_hi = sb("p_hi", [P, 2, SEQ], F32R)
        p_lo = sb("p_lo", [P, 2, SEQ], F32R)

        with ExitStack() as part:
            hid_hi = sb("hid_hi", [P, HKT, SEQ], F32R, part)
            hid_lo = sb("hid_lo", [P, HKT, SEQ], F32R, part)
        with ExitStack() as part:
            qk = sb("qk", [P, 2, 2, QW], F32, part)
            q_t = sb("q_t", [P, GROUPS, SEQ], F32, part)
            k_t = sb("k_t", [P, GROUPS, SEQ], F32, part)
            v = sb("v", [P, 2, GROUPS, P], F32, part)
            e = sb("e", [P, 2, GROUPS * SEQ], F32, part)
            e_t = sb("e_t", [P, 2, GROUPS * SEQ], F32, part)
            o = sb("o", [P, 2, P], F32, part)
            o_hi = sb("o_hi", [P, SEQ], F32R, part)
            o_lo = sb("o_lo", [P, SEQ], F32R, part)
            bias = sb("bias", [P, 2, GROUPS, SEQ], F32, part)
            tops = sb("tops", [P, 4, 2], F32, part)
            neg_top = sb("neg_top", [P, 4], F32, part)
            waited = sb("waited", [P, 1], F32, part)
            den = sb("den", [P, 4], F32, part)
            rden = sb("rden", [P, 4], F32, part)
            table = sb("table", [33, GROUPS * HEADS], F32, part)
            buckets = sb("buckets", [33, GROUPS, SKEW], F32, part)
            offsets = sb("offsets", [HEADS, GROUPS, SKEW], F32, part)
        with ExitStack() as part:
            y = sb("y", [P, 2, D], F32, part)
            pool_w = sb("pool_w", [P, 4, 3 * P], F32, part)
            z_hi = sb("z_hi", [P, KT, SEQ], F32R, part)
            z_lo = sb("z_lo", [P, KT, SEQ], F32R, part)
            u_hi = sb("u_hi", [P, KT, SEQ], F32R, part)
            u_lo = sb("u_lo", [P, KT, SEQ], F32R, part)
        with ExitStack() as part:
            gv = sb("gv", [P, 2, D], F32, part)
            gu = sb("gu", [P, 2, D], F32, part)
            gain_v = sb("gain_v", [P, D], F32, part)
            w_s = sb("w_s", [P, 4, P], F32, part)
            w_st = sb("w_st", [P, 4, P], F32, part)
            tril = sb("tril", [P, P], F32, part)
            stats = sb("stats", [P, 2, 2, 6], F32, part)
            mv = sb("mv", [P, 2, 2], F32, part)
            c_hi = sb("c_hi", [P, KT, SEQ], F32R, part)
            c_lo = sb("c_lo", [P, KT, SEQ], F32R, part)
        with ExitStack() as part:
            gain_f = sb("gain_f", [P, D], F32, part)
            result = sb("result", [P, 2, D], F32, part)

        def bank(name):
            return ctx.enter_context(nc.psum_tensor(name, [P, 512], F32))

        acc = [[bank(f"acc{j}{t}") for t in range(2)] for j in range(2)]
        tbank = [bank("tbank0"), bank("tbank1")]
        sbank = [bank("sbank0"), bank("sbank1")]
        pv_bank, qkt_bank = acc[1]

        bias_rows = nc.dram_tensor("bias_rows", (GROUPS * HEADS, SKEW), F32).ap()
        bias_skew = nc.dram_tensor("bias_skew", (GROUPS * HEADS, P, SKEW), F32).ap()

        raw_in = [sem(f"raw_in{i}") for i in range(4)]
        x_in = sem("x_in")
        id_in = sem("id_in")
        rows_in = sem("rows_in")
        table_in = sem("table_in")
        p_in = sem("p_in")
        part_in = sem("part_in")
        bias_in = sem("bias_in")
        out_in = sem("out_in")
        hi_done = sem("hi_done")
        lo_done = sem("lo_done")
        blk = sem("blk")
        t_done = sem("t_done")
        t_free = sem("t_free")
        t_hi = sem("t_hi")
        h_done = sem("h_done")
        x_done = sem("x_done")
        ssq_done = sem("ssq_done")
        r_step = sem("r_step")
        r_done = sem("r_done")
        expo_set = sem("expo_set")
        gate_done = sem("gate_done")
        hid_done = sem("hid_done")
        dve_step = sem("dve_step")
        qkv_out = sem("qkv_out")
        qkt_done = sem("qkt_done")
        qkt_out = sem("qkt_out")
        s_done = sem("s_done")
        embed_step = sem("embed_step")
        max_done = sem("max_done")
        rden_done = sem("rden_done")
        top_done = sem("top_done")
        exp_done = sem("exp_done")
        et_done = sem("et_done")
        et_out = sem("et_out")
        pv_done = sem("pv_done")
        o_done = sem("o_done")
        ot_done = sem("ot_done")
        ot_hi = sem("ot_hi")
        ot_lo = sem("ot_lo")
        table_one = sem("table_one")
        y_out = sem("y_out")
        z_done = sem("z_done")
        z_hi_done = sem("z_hi_done")
        z_lo_done = sem("z_lo_done")
        ln_stat = sem("ln_stat")
        v_done = sem("v_done")
        sp_done = sem("sp_done")
        result_done = sem("result_done")
        rows_out = sem("rows_out")
        masked = sem("masked")
        gate_out = sem("gate_out")

        def kt_slice(par, k, kt, width, buf):
            s = (k // (kt // 2)) * HALF + (k % (kt // 2)) * width
            return buf[:, par, s:s + width]

        def quarters(layer, part):
            by_half = [(0, 0), (1, 0), (0, 1), (1, 1)]
            if part == "ffn" and MIXERS[layer] == 0:
                return [(0, 0), (0, 1), (1, 0), (1, 1)], [cnt.t[layer, "mix"] + q for q in range(4)], cnt.h[layer, "ffn"] - 4
            if part == "ffn":
                return by_half, [cnt.t[layer, "ffn"] - 4 + q for q in range(4)], cnt.h[layer, "ffn"] - 4
            if part == "ple":
                t = cnt.t[layer, "down"]
                return by_half, [t, t + 1, t + 3, t + 4], cnt.h[layer, "down"]
            if layer == 0:
                return by_half, [1, 2, 3, 4], 0
            return by_half, [cnt.t[layer - 1, "ple"] + q for q in range(4)], cnt.h[layer - 1, "ple"]

        def gain_col(i, k):
            return (i % 3) * DEPTH * KT + (i // 3) * KT + k

        BSCALE = 12 * KT
        BSP = 13 * KT

        qkv_src = a_w_qkv.rearrange("a (f k p) (c g n x) -> a c n f g p k x",
                                    f=2, p=P, c=3, g=GROUPS, x=P)
        wo_src = a_w_o.rearrange("a (n p) (j x) -> a n j p x", p=P, j=2)

        def square(w):
            return w.rearrange("(f k p) (j x) -> j f p k x", f=2, p=P, x=512)

        block = ctx.enter_context(nc.Block())


        @block.sync
        def _(sp):
            def slot_free(n, half, i=None, m=0):
                if n >= 2:
                    sp.wait_ge(lo_done, at(4 * (n - 2) + 2 * half + 2, i, 4 * m))

            def half_slot(n, half, **dims):
                length = 1
                for size in dims.values():
                    length *= size
                names = " ".join(dims)
                return raw[:, 2 * (n % 2) + half, 0:length].rearrange(f"p ({names}) -> p {names}", **dims)

            def load_qkv(n, a, c, pair, i=None):
                for f in range(2):
                    slot_free(n, f, i, 4)
                    for g in range(GROUPS):
                        sp.dma_start(half_slot(n, f, k=4, g=GROUPS, x=P)[:, :, g, :],
                                     qkv_src[a, c, pair, f, g]).then_inc(raw_in[2 * (n % 2) + f], 16)

            def load_wo(n, a, pair, i=None):
                for j in range(2):
                    slot_free(n, j, i, 4)
                    sp.dma_start(half_slot(n, j, k=1, x=512)[:, 0, :],
                                 wo_src[a, pair, j]).then_inc(raw_in[2 * (n % 2) + j], 16)

            def load_square(n, w, j):
                for f in range(2):
                    slot_free(n, f)
                    sp.dma_start(half_slot(n, f, k=4, x=512), square(w)[j, f]).then_inc(raw_in[2 * (n % 2) + f], 16)

            def load_hidden(n, layer, b, i=None):
                for f in range(2):
                    slot_free(n, f, i, 2)
                    dst = half_slot(n, f, k=4, s=2, x=SEQ)
                    for s, w in ((0, ffn_w_gate), (1, ffn_w_up)):
                        src = w[layer].rearrange("(f k p) (b x) -> b f p k x", f=2, p=P, x=SEQ)[b, f]
                        sp.dma_start(dst[:, :, s, :], src).then_inc(raw_in[2 * (n % 2) + f], 16)

            def mixer_a(layer, a):
                n = cnt.n[layer, "mix"]
                for c in range(3):
                    load_qkv(n + c, a, c, 0)
                with sp.Fori(0, PAIRS - 1, 1) as i:
                    for c in range(3):
                        load_qkv(n + 3 + c, a, c, i + 1, i)
                    load_wo(n + 6, a, i, i)
                m = n + A_PANELS - 1
                for j in range(2):
                    slot_free(m, j)
                    for c0, c1 in ((0, P), (P, 2 * P), (2 * P, 4 * P)):
                        sp.dma_start(half_slot(m, j, k=1, x=512)[:, 0, c0:c1], wo_src[a, PAIRS - 1, j][:, c0:c1]
                                     ).then_inc(raw_in[2 * (m % 2) + j], 16)

            def mixer_b(layer):
                n = cnt.n[layer, "mix"]
                sp.wait_ge(blk, 2 * cnt.n[layer - 1, "ple"])
                sp.dma_start(pool_w[:, :, :], pool_of).then_inc(part_in, 16)
                for j in range(2):
                    load_square(n + j, b_w_in[0], j)
                for f in range(2):
                    slot_free(n + 2, f)
                    src = b_w_grp[0].rearrange("(f g) (c p) x -> f p (g c) x", f=2, p=P)[f]
                    sp.dma_start(half_slot(n + 2, f, k=4, x=SEQ), src).then_inc(raw_in[2 * (n % 2) + f], 16)
                for j in range(2):
                    load_square(n + 3 + j, b_w_out[0], j)

            def mixer_c(layer):
                n = cnt.n[layer, "mix"]
                for j in (0, 1):
                    load_square(n + j, c_w_in[0], 2 + j)
                sp.wait_ge(blk, 2 * cnt.n[layer - 1, "ple"])
                sp.dma_start(gain_v[:, :], bass.AP(tensor=c_v_gain.tensor, offset=0, ap=[[0, P], [1, D]])
                             ).then_inc(part_in, 16)
                sp.dma_start(w_s[:, :, :], c_w_s[0].rearrange("g t s -> t g s")).then_inc(part_in, 16)
                sp.dma_start(tril[:, :], lower).then_inc(part_in, 16)
                for j in (0, 1):
                    load_square(n + 2 + j, c_w_in[0], j)
                for j in (0, 1):
                    load_square(n + 4 + j, c_w_out[0], j)

            def ffn(layer):
                n = cnt.n[layer, "ffn"]
                load_hidden(n, layer, 0)
                with sp.Fori(0, (HB - 1) // 2, 1) as i:
                    for s in range(2):
                        load_hidden(n + 1 + s, layer, i * 2 + (s + 1), i)
                n = cnt.n[layer, "down"]
                w = ffn_w_down[layer].rearrange("(k p) (j x) -> j p k x", p=P, x=512)
                for j in range(2):
                    for t, (k0, kh) in enumerate(((0, 4), (8, 4), (16, 3))):
                        for f in range(2):
                            slot_free(n, f)
                            for k1, k2 in ((0, 2), (2, 4)) if (j, t) == (0, 0) else ((0, kh),):
                                sp.dma_start(half_slot(n, f, k=kh, x=512)[:, k1:k2, :],
                                             w[j][:, k0 + f * kh + k1:k0 + f * kh + k2, :]
                                             ).then_inc(raw_in[2 * (n % 2) + f], 16)
                        n += 1
                    if j == 0:
                        sp.dma_start(p_rows[:, :, :], p[layer, 0].rearrange("(t p) d -> p t d", p=P)).then_inc(p_in, 16)
                n = cnt.n[layer, "ple"]
                for f in range(2):
                    slot_free(n, f)
                    sp.dma_start(half_slot(n, f, k=1, x=D)[:, 0, :], ple_w_proj[layer][f * P:(f + 1) * P, :]
                                 ).then_inc(raw_in[2 * (n % 2) + f], 16)
                for j in range(2):
                    load_square(n + 1 + j, ple_w_gate[layer], j)

            sp.dma_start(h[:, :, :], x[0].rearrange("(t p) d -> p t d", p=P)).then_inc(x_in, 16)
            sp.dma_start(ident[:, :], identity).then_inc(id_in, 16)
            for b, g in enumerate((norm_mix, norm_ffn, norm_ple)):
                sp.dma_start(rows[b * DEPTH * KT:(b + 1) * DEPTH * KT, :], g.rearrange("l (k x) -> (l k) x", x=P)
                             ).then_inc(rows_in, 16)
            sp.dma_start(rows[BSCALE:BSCALE + KT, :], b_scale.rearrange("l (k x) -> (l k) x", x=P)).then_inc(rows_in, 16)
            sp.dma_start(rows[BSP:BSP + 4, :], c_b_s[0]).then_inc(rows_in, 16)
            sp.dma_start(table[0:32, :], rel_table).then_inc(table_in, 16)
            sp.dma_start(buckets[:, :, :], bucket_of).then_inc(table_in, 16)
            for layer, kind in enumerate(MIXERS):
                if kind == 0:
                    mixer_a(layer, layer // 3)
                elif kind == 1:
                    mixer_b(layer)
                else:
                    mixer_c(layer)
                ffn(layer)
            sp.wait_ge(blk, 2 * cnt.n[last_layer, "ple"])
            sp.dma_start(gain_f[:, :], bass.AP(tensor=final_norm.tensor, offset=0, ap=[[0, P], [1, D]])).then_inc(part_in, 16)
            for tok in range(2):
                sp.wait_ge(result_done, tok + 1)
                sp.dma_start(out[0][tok * P:(tok + 1) * P, :], result[:, tok, :]).then_inc(out_in, 16)
            sp.wait_ge(out_in, 32)

        @block.tensor
        def _(pe):
            def passes(out_, st, st_lo, mv_, mv_lo, start, stop):
                nc.tensor.matmul(out_, st, mv_, start=start, stop=False)
                nc.tensor.matmul(out_, st_lo, mv_, start=False, stop=False)
                return nc.tensor.matmul(out_, st, mv_lo, start=False, stop=stop)

            def xt(norm):
                return x_hi[:, norm % 2], x_lo[:, norm % 2]

            def product(n, tok, kt, width, act, k0, out_, i=None, m=0, waits={}, mid=None,
                        start=True, stop=True):
                for k in range(kt):
                    if tok == 0 and k == 0:
                        pe.wait_ge(lo_done, at(4 * n + 2, i, 4 * m))
                    if tok == 0 and k == kt // 2:
                        pe.wait_ge(lo_done, at(4 * n + 4, i, 4 * m))
                    if k in waits:
                        pe.wait_ge(*waits[k])
                    if mid and k == mid[0]:
                        mid[1]()
                    last = passes(out_, act[0][:, k0 + k, tok * P:(tok + 1) * P], act[1][:, k0 + k, tok * P:(tok + 1) * P],
                                  kt_slice(n % 2, k, kt, width, w_hi), kt_slice(n % 2, k, kt, width, w_lo),
                                  start=start and k == 0, stop=stop and k == kt - 1)
                last.then_inc(blk, 1)

            def quarter(layer, part, q):
                order, uses, h0 = quarters(layer, part)
                (tok, j), t = order[q], uses[q]
                pe.wait_ge(h_done, 4 if h0 == 0 else h0 + q + 1)
                pe.wait_ge(t_free, t - 1 if t > 1 else 1)
                for c in range(4):
                    last = nc.tensor.transpose(tbank[t % 2][:, c * P:(c + 1) * P],
                                               h[:, tok, (4 * j + c) * P:(4 * j + c + 1) * P], ident[:, :])
                last.then_inc(t_done, 1)

            def x_waits(layer, part, tok):
                order, _, _ = quarters(layer, part)
                x0 = {"mix": cnt.x[layer, "mix"], "ffn": cnt.x[layer, "ffn"], "ple": cnt.x[layer, "ple"]}[part] - 4
                return {4 * j: (x_done, x0 + order.index((tok, j)) + 1) for j in range(2)}

            def scores(u, pair, i):
                hd, qt = u // 2, u % 2
                if u == 0:
                    pe.wait_ge(qkt_out, at(4 * pair + 4, i, 4))
                if u or pair:
                    pe.wait_ge(top_done, at(4 * pair + u, i, 4))
                keys = (qt + 1) * P
                for g in range(GROUPS):
                    dst = sbank[0][:, g * keys:(g + 1) * keys] if qt == 0 or g < 2 else sbank[1][:, 0:keys]
                    last = nc.tensor.matmul(dst, q_t[hd * DH:(hd + 1) * DH, g, qt * P:(qt + 1) * P],
                                            k_t[hd * DH:(hd + 1) * DH, g, 0:keys], start=True, stop=True)
                last.then_inc(s_done, 1)

            def exp_transposes(u, pair, i):
                pe.wait_ge(exp_done, at(4 * pair + u + 1, i, 4))
                if u:
                    pe.wait_ge(et_out, at(4 * pair + u, i, 4))
                for b in range(GROUPS * (u % 2 + 1)):
                    last = nc.tensor.transpose(tbank[b // 4][:, (b % 4) * P:(b % 4 + 1) * P],
                                               e[:, u % 2, b * P:(b + 1) * P], ident[:, :])
                last.then_inc(et_done, 1)

            def weighted_values(u, pair, h0, i):
                hd, qt = u // 2, u % 2
                pe.wait_ge(et_out, at(4 * pair + u + 1, i, 4))
                if u:
                    pe.wait_ge(o_done, at(4 * pair + u, i, 4))
                else:
                    pe.wait_ge(h_done, at(h0, i, 4))
                    pe.wait_ge(qkv_out, at(6 * pair + 6, i, 6))
                blocks = [(g, t) for g in range(GROUPS) for t in range(qt + 1)]
                for b, (g, t) in enumerate(blocks):
                    last = nc.tensor.matmul(pv_bank[:, 0:DH], e_t[:, u % 2, b * P:(b + 1) * P],
                                            v[:, t, g, hd * DH:(hd + 1) * DH],
                                            start=(b == 0), stop=(b == len(blocks) - 1))
                last.then_inc(pv_done, 1)

            def qk_transposes(c, tok, pair, i):
                pe.wait_ge(qkv_out, at(6 * pair + 2 * c + tok + 1, i, 6))
                if c or tok:
                    pe.wait_ge(qkt_out, at(4 * pair + 2 * c + tok, i, 4))
                if i is not None and (c, tok) == (1, 1):
                    pe.wait_ge(ot_lo, at(pair, i, 1))
                for g in range(GROUPS):
                    last = nc.tensor.transpose(qkt_bank[:, g * P:(g + 1) * P],
                                               qk[:, c, tok, g * P:(g + 1) * P], ident[:, :])
                last.then_inc(qkt_done, 1)

            def out_transposes(pair, i):
                pe.wait_ge(o_done, at(4 * pair + 4, i, 4))
                if i is not None:
                    pe.wait_ge(qkt_out, at(4 * pair + 7, i, 4))
                for tok in range(2):
                    last = nc.tensor.transpose(qkt_bank[:, tok * P:(tok + 1) * P], o[:, tok, :], ident[:, :])
                last.then_inc(ot_done, 1)

            def wo_blocks(n, pair, i):
                pe.wait_ge(lo_done, at(4 * n + 4, i, 16))
                pe.wait_ge(ot_lo, at(pair + 1, i, 1))
                for tok in range(2):
                    if i is not None:
                        pe.wait_ge(qkv_out, at(6 * pair + 11 + tok, i, 6))
                    for j in range(2):
                        if i is not None and (tok, j) == (1, 1):
                            pe.wait_ge(qkt_out, at(4 * pair + 8, i, 4))
                        last = passes(acc[j][tok][:, :], o_hi[:, tok * P:(tok + 1) * P], o_lo[:, tok * P:(tok + 1) * P],
                                      kt_slice(n % 2, j, 2, 512, w_hi), kt_slice(n % 2, j, 2, 512, w_lo),
                                      start=True, stop=True)
                    last.then_inc(blk, 1)

            def mixer_a(layer, pair):
                n, h0, norm = cnt.n[layer, "mix"], cnt.h[layer, "mix"], 3 * layer
                quarter(layer, "mix", 2)
                if layer == 0:
                    quarter(layer, "mix", 3)
                    bias_vectors()
                for c in range(3):
                    for tok in range(2):
                        if c:
                            pe.wait_ge(qkv_out, 6 * pair + 2 * c + tok - 1)
                        product(n + c, tok, KT, QW, xt(norm), 0, acc[0][tok][:, 0:QW],
                                waits=x_waits(layer, "mix", tok) if c == 0 else {},
                                mid=(6, lambda: quarter(layer, "mix", 3)) if c == tok == 0 and layer else None)
                    if c:
                        qk_transposes(c - 1, 0, pair, None)
                        qk_transposes(c - 1, 1, pair, None)
                with pe.Fori(0, PAIRS - 1, 1) as i:
                    def qkv(c, tok, mid=None):
                        pe.wait_ge(qkv_out, at(6 * pair + 6 + 2 * c + tok - 1, i, 6))
                        if c == 0:
                            pe.wait_ge(h_done, at(h0 - 3 + 2 * tok, i, 4))
                        product(n + 3 + c, tok, KT, QW, xt(norm), 0, acc[0][tok][:, 0:QW], i, 4, mid=mid)
                    scores(0, pair, i)
                    qkv(0, 0)
                    exp_transposes(0, pair, i)
                    scores(1, pair, i)
                    qkv(0, 1)
                    weighted_values(0, pair, h0, i)
                    exp_transposes(1, pair, i)
                    scores(2, pair, i)
                    qkv(1, 0)
                    weighted_values(1, pair, h0, i)
                    exp_transposes(2, pair, i)
                    scores(3, pair, i)
                    qkv(1, 1)
                    weighted_values(2, pair, h0, i)
                    exp_transposes(3, pair, i)
                    qk_transposes(0, 0, pair + 1, i)
                    qkv(2, 0, mid=(3, lambda: qk_transposes(0, 1, pair + 1, i)))
                    weighted_values(3, pair, h0, i)
                    qk_transposes(1, 0, pair + 1, i)
                    qkv(2, 1, mid=(4, lambda: out_transposes(pair, i)))
                    qk_transposes(1, 1, pair + 1, i)
                    wo_blocks(n + 6, pair, i)
                last_pair = pair + PAIRS - 1
                scores(0, last_pair, None)
                for u in range(4):
                    exp_transposes(u, last_pair, None)
                    if u < 3:
                        scores(u + 1, last_pair, None)
                    weighted_values(u, last_pair, h0 + 4 * (PAIRS - 1), None)
                out_transposes(last_pair, None)
                wo_blocks(n + A_PANELS - 1, last_pair, None)
                for q in range(3):
                    quarter(layer, "ffn", q)

            def bias_vectors():
                pe.wait_ge(table_in, 32)
                pe.wait_ge(table_one, 1)
                for g in range(GROUPS):
                    t = 5 + g
                    pe.wait_ge(t_free, t - 1)
                    nc.tensor.matmul(tbank[t % 2][0:HEADS, 0:SKEW], table[:, g * HEADS:(g + 1) * HEADS],
                                     buckets[:, g, :], start=True, stop=True).then_inc(t_done, 1)

            def mixer_out(layer, n, act, waits):
                for j in range(2):
                    for tok in range(2):
                        product(n + j, tok, KT, 512, act, 0, acc[j][tok][:, :], waits=waits[tok] if j == 0 else {})
                        if (j, tok) == (1, 0):
                            quarter(layer, "ffn", 0)
                            quarter(layer, "ffn", 1)
                quarter(layer, "ffn", 2)

            def mixer_b(layer):
                n, norm = cnt.n[layer, "mix"], 3 * layer
                quarter(layer, "mix", 2)
                for j in range(2):
                    for tok in range(2):
                        product(n + j, tok, KT, 512, xt(norm), 0, acc[j][tok][:, :],
                                waits=x_waits(layer, "mix", tok) if j == 0 else {},
                                mid=(6, lambda: quarter(layer, "mix", 3)) if j == tok == 0 else None)
                pe.wait_ge(part_in, 16)
                for u in range(4):
                    pe.wait_ge(y_out, 2 if u < 2 else 4)
                    if u >= 2:
                        pe.wait_ge(z_lo_done, u - 1)
                    for c in range(2):
                        f = 2 * u + c
                        dst = sbank[u % 2][:, c * SEQ:(c + 1) * SEQ]
                        nc.tensor.matmul(dst, y[:, 0, f * P:(f + 1) * P], pool_w[:, u, 0:SEQ],
                                         start=True, stop=False)
                        last = nc.tensor.matmul(dst[:, P:SEQ], y[:, 1, f * P:(f + 1) * P], pool_w[:, u, SEQ:SEQ + P],
                                                start=False, stop=True)
                    last.then_inc(z_done, 1)
                for g in range(4):
                    pe.wait_ge(lo_done, 4 * (n + 2) + (2 if g < 2 else 4))
                    pe.wait_ge(z_lo_done, g + 3)
                    for eh in range(2):
                        dst = sbank[g % 2][:, eh * SEQ:(eh + 1) * SEQ]
                        for c in range(2):
                            wg_hi, wg_lo = (kt_slice(n % 2, 2 * g + c, KT, SEQ, b)[:, eh * P:(eh + 1) * P] for b in (w_hi, w_lo))
                            last = passes(dst, wg_hi, wg_lo, z_hi[:, 2 * g + c, :], z_lo[:, 2 * g + c, :],
                                          start=c == 0, stop=c == 1)
                    last.then_inc(blk if g % 2 else z_done, 1)
                by_group = {2 * g: (z_lo_done, 5 + g) for g in range(4)}
                mixer_out(layer, n + 3, (u_hi, u_lo), [by_group, by_group])

            def mixer_c(layer):
                n, t0, norm = cnt.n[layer, "mix"], cnt.t[layer, "mix"], 3 * layer
                quarter(layer, "mix", 2)
                y0 = 4

                def block_in(s, tok):
                    if s >= 2:
                        pe.wait_ge(y_out, y0 + 2 * (s - 2) + tok + 1)
                    product(n + s, tok, KT, 512, xt(norm), 0, acc[s % 2][tok][:, :],
                            waits=x_waits(layer, "mix", tok) if s == 0 else {},
                            mid=(6, lambda: quarter(layer, "mix", 3)) if s == tok == 0 else None)

                def spatial(j, tok):
                    pe.wait_ge(v_done, tok + 1)
                    if j:
                        pe.wait_ge(gate_out, tok + 1)
                    for s in range(2):
                        g = 2 * j + s
                        last = nc.tensor.matmul(sbank[tok][:, s * SEQ:(s + 1) * SEQ], w_st[:, g, :],
                                                gv[:, tok, g * SEQ:(g + 1) * SEQ], start=True, stop=True)
                    last.then_inc(sp_done, 1)

                def gated_quarter(q):
                    tok, j = q % 2, q // 2
                    t = t0 + 1 + q
                    pe.wait_ge(gate_out, q + 1)
                    pe.wait_ge(t_free, t - 1)
                    for c in range(4):
                        last = nc.tensor.transpose(tbank[t % 2][:, c * P:(c + 1) * P],
                                                   gu[:, tok, (4 * j + c) * P:(4 * j + c + 1) * P], ident[:, :])
                    last.then_inc(t_done, 1)

                for s in range(3):
                    for tok in range(2):
                        block_in(s, tok)
                pe.wait_ge(masked, 1)
                pe.wait_ge(t_free, t0 - 1)
                for g in range(4):
                    last = nc.tensor.transpose(tbank[t0 % 2][:, g * P:(g + 1) * P], w_s[:, g, :], ident[:, :])
                last.then_inc(t_done, 1)
                block_in(3, 0)
                pe.wait_ge(t_free, t0 + 1)
                spatial(0, 0)
                spatial(0, 1)
                block_in(3, 1)
                gated_quarter(0)
                gated_quarter(1)
                spatial(1, 0)
                spatial(1, 1)
                gated_quarter(2)
                gated_quarter(3)
                mixer_out(layer, n + 4, (c_hi, c_lo),
                          [{4 * j: (t_free, t0 + 1 + 2 * j + tok + 1) for j in range(2)} for tok in range(2)])

            def ffn(layer):
                n, t0, hid0, norm = cnt.n[layer, "ffn"], cnt.t[layer, "ffn"], cnt.hid[layer, "ffn"], 3 * layer + 1

                def hidden_transposes(b, bank_, i=None):
                    pe.wait_ge(hid_done, at(hid0 + 2 * b + 2, i, 4))
                    pe.wait_ge(t_free, at(t0 + b - 1, i, 2))
                    for c in range(2):
                        for tok in range(2):
                            last = nc.tensor.transpose(tbank[bank_][:, (2 * c + tok) * P:(2 * c + tok + 1) * P],
                                                       prod[:, tok, c * P:(c + 1) * P], ident[:, :])
                    last.then_inc(t_done, 1)

                for tok in range(2):
                    product(n, tok, KT, 512, xt(norm), 0, acc[0][tok][:, :], waits=x_waits(layer, "ffn", tok),
                            mid=(6, lambda: quarter(layer, "ffn", 3)) if tok == 0 else None)
                with pe.Fori(0, (HB - 1) // 2, 1) as i:
                    for s in range(2):
                        for tok in range(2):
                            pe.wait_ge(hid_done, at(hid0 + 2 * (s - 1) + tok + 1, i, 4))
                            product(n + 1 + s, tok, KT, 512, xt(norm), 0, acc[(1 + s) % 2][tok][:, :], i, 2)
                            if tok == 0:
                                hidden_transposes(s, (t0 + s) % 2, i)

                n, hb, td = cnt.n[layer, "down"], cnt.h[layer, "down"], cnt.t[layer, "down"]
                for j in range(2):
                    for s, (k0, kt) in enumerate(((0, 8), (8, 8), (16, 6))):
                        for tok in range(2):
                            if (j, s) == (0, 0):
                                pe.wait_ge(hid_done, hid0 + 2 * (HB - 1) + tok + 1)
                            if (j, s, tok) == (0, 2, 0):
                                pe.wait_ge(t_free, t0 + HB)
                            product(n, tok, kt, 512, (hid_hi, hid_lo), k0, acc[j][tok][:, :], start=s == 0, stop=s == 2)
                            if (j, s, tok) == (0, 0, 0):
                                hidden_transposes(HB - 1, (t0 + HB - 1) % 2)
                            if (j, s, tok) == (1, 0, 0):
                                quarter(layer, "ple", 0)
                                quarter(layer, "ple", 1)
                            if (j, s, tok) == (1, 1, 0):
                                pe.wait_ge(p_in, 16 * (layer + 1))
                                pe.wait_ge(t_free, td + 1)
                                for k in range(2):
                                    for tk in range(2):
                                        last = nc.tensor.transpose(tbank[(td + 2) % 2][:, (2 * k + tk) * P:(2 * k + tk + 1) * P],
                                                                   p_rows[:, tk, k * P:(k + 1) * P], ident[:, :])
                                last.then_inc(t_done, 1)
                        n += 1
                quarter(layer, "ple", 2)

                pe.wait_ge(lo_done, 4 * n + 4)
                pe.wait_ge(t_free, td + 3)
                for tok in range(2):
                    pe.wait_ge(h_done, hb + 2 + tok + 1)
                    for j in range(2):
                        for k in range(2):
                            w_k = [b[:, n % 2, k * HALF + j * 512:k * HALF + (j + 1) * 512] for b in (w_hi, w_lo)]
                            last = passes(acc[j][tok][:, :], p_hi[:, k, tok * P:(tok + 1) * P],
                                          p_lo[:, k, tok * P:(tok + 1) * P], *w_k, start=k == 0, stop=k == 1)
                    last.then_inc(blk, 1)
                    if tok == 0:
                        quarter(layer, "ple", 3)
                for j in range(2):
                    for tok in range(2):
                        if j:
                            pe.wait_ge(gate_done, 26 * layer + 2 * HB + tok + 1)
                        product(n + 1 + j, tok, KT, 512, xt(3 * layer + 2), 0, sbank[tok][:, :],
                                waits=x_waits(layer, "ple", tok) if j == 0 else {})
                        if (j, tok) == (1, 0) and layer < last_layer:
                            quarter(layer + 1, "mix", 0)
                            quarter(layer + 1, "mix", 1)

            pe.wait_ge(id_in, 16)
            pe.wait_ge(rows_in, 16 * 5)
            nc.tensor.transpose(tbank[0][:, 0:13 * KT + 4], rows[:, :], ident[0:13 * KT + 4, 0:13 * KT + 4]).then_inc(t_done, 1)
            quarter(0, "mix", 0)
            quarter(0, "mix", 1)
            pair = 0
            for layer, kind in enumerate(MIXERS):
                if kind == 0:
                    mixer_a(layer, pair)
                    pair += PAIRS
                elif kind == 1:
                    mixer_b(layer)
                else:
                    mixer_c(layer)
                ffn(layer)

        def panel_quarter(n, s):
            q = cnt.half[n] // 2
            a, half = (s % 2) * q, s // 2
            return raw[:, 2 * (n % 2) + half, a:a + q], [b[:, n % 2, half * HALF + a:half * HALF + a + q] for b in (w_hi, w_lo)]

        def hi_index(layer, part, q):
            if part == "mix" and layer == 0:
                return q + 1
            if part == "mix":
                return cnt.hi[layer - 1, "ple"] + q + 1
            if part == "ffn":
                return cnt.hi[layer, "ffn"] - 4 + q + 1
            return cnt.hi[layer, "down"] + (1, 2, 4, 5)[q]

        def norm_of(layer, part):
            return 3 * layer + ("mix", "ffn", "ple").index(part)

        def r_index(norm, tok):
            return 2 * norm + tok + 1 + (2 if norm > 6 else 0)

        def quarter_view(buf, tok, j):
            return buf[:, 4 * j:4 * j + 4, tok * P:(tok + 1) * P]

        def four(ap):
            return ap.rearrange("p (c x) -> p c x", c=4)

        @block.scalar
        def _(act):
            def split(n, i=None, m=0, which=range(4)):
                for s in which:
                    if s == 0 and n >= 2:
                        act.wait_ge(blk, at(2 * n - 2, i, 2 * m))
                    if s % 2 == 0:
                        step = 16 * (cnt.landed[n + m] - cnt.landed[n]) if m else 0
                        act.wait_ge(raw_in[2 * (n % 2) + s // 2], at(16 * cnt.landed[n], i, step))
                    src, (hi, _) = panel_quarter(n, s)
                    nc.scalar.copy(hi, src).then_inc(hi_done, 1)

            def quarter_hi(layer, part, q):
                order, uses, _ = quarters(layer, part)
                tok, j = order[q]
                act.wait_ge(t_free, uses[q] + 1)
                nc.scalar.copy(quarter_view(x_hi[:, norm_of(layer, part) % 2], tok, j), four(xf[:, q % 2, :])
                               ).then_inc(t_hi, 1)

            def sum_squares(norm, tok, ready):
                act.wait_ge(h_done, ready)
                if norm or tok:
                    act.wait_ge(ssq_done, 2 * norm + tok)
                nc.scalar.activation(squares[:, :], h[:, tok, :], ACT.Square,
                                     accum_out=ssq[:, 2 * norm + tok:2 * norm + tok + 1]).then_inc(ssq_done, 1)

            def late_half(layer, part, n):
                norm, (_, _, h0) = norm_of(layer, part), quarters(layer, part)
                split(n, which=(0,))
                quarter_hi(layer, part, 2)
                split(n, which=(1,))
                quarter_hi(layer, part, 3)
                split(n, which=(2, 3))
                sum_squares(norm, 0, 4 if h0 == 0 else h0 + 3)
                sum_squares(norm, 1, h0 + 4)

            def rows_out_of_psum(n, c, tok, pair, i):
                act.wait_ge(blk, at(2 * n + tok + 1, i, 8))
                if c == 2 and i is not None:
                    act.wait_ge(pv_done, at(4 * (pair - 1) + 4, i, 4))
                dst = v[:, tok, :, :].rearrange("p g x -> p (g x)") if c == 2 else qk[:, c, tok, :]
                scale = rinv8[:, tok:tok + 1] if c == 0 else rinv[:, r_col[0] + tok:r_col[0] + tok + 1]
                nc.scalar.activation(dst, acc[0][tok][:, 0:QW], ACT.Copy, scale=scale).then_inc(qkv_out, 1)

            r_col = [0]

            def qk_out_of_psum(c, tok, pair, i):
                act.wait_ge(qkt_done, at(4 * pair + 2 * c + tok + 1, i, 4))
                dst = (q_t, k_t)[c][:, :, tok * P:(tok + 1) * P]
                nc.scalar.copy(dst, qkt_bank[:, 0:QW].rearrange("p (g x) -> p g x", g=GROUPS)).then_inc(qkt_out, 1)

            def exponentials(u, pair, i):
                act.wait_ge(top_done, at(4 * pair + u + 1, i, 4))
                width = QW * (u % 2 + 1)
                nc.scalar.activation(e[:, u % 2, 0:width], e[:, u % 2, 0:width], ACT.Exp,
                                     bias=neg_top[:, u:u + 1], accum_out=den[:, u:u + 1]).then_inc(exp_done, 1)

            def exp_out_of_psum(u, pair, i):
                act.wait_ge(et_done, at(4 * pair + u + 1, i, 4))
                if u >= 2:
                    act.wait_ge(pv_done, at(4 * pair + u - 1, i, 4))
                if u % 2 == 0:
                    nc.scalar.copy(e_t[:, 0, 0:QW], tbank[0][:, 0:QW]).then_inc(et_out, 1)
                else:
                    nc.scalar.copy(e_t[:, 1, 0:512], tbank[0][:, :])
                    nc.scalar.copy(e_t[:, 1, 512:2 * QW], tbank[1][:, 0:2 * QW - 512]).then_inc(et_out, 1)

            def out_hi(pair, i):
                act.wait_ge(ot_done, at(pair + 1, i, 1))
                nc.scalar.copy(o_hi[:, :], qkt_bank[:, 0:SEQ]).then_inc(ot_hi, 1)

            def mixer_a(layer, pair):
                n, norm = cnt.n[layer, "mix"], 3 * layer
                r_col[0] = 2 * norm
                late_half(layer, "mix", n + 1)
                act.wait_ge(r_done, r_index(norm, 1))
                rows_out_of_psum(n, 0, 0, pair, None)
                rows_out_of_psum(n, 0, 1, pair, None)
                split(n + 2)
                rows_out_of_psum(n + 1, 1, 0, pair, None)
                rows_out_of_psum(n + 1, 1, 1, pair, None)
                qk_out_of_psum(0, 0, pair, None)
                qk_out_of_psum(0, 1, pair, None)
                split(n + 3)
                rows_out_of_psum(n + 2, 2, 0, pair, None)
                rows_out_of_psum(n + 2, 2, 1, pair, None)
                qk_out_of_psum(1, 0, pair, None)
                qk_out_of_psum(1, 1, pair, None)
                with act.Fori(0, PAIRS - 1, 1) as i:
                    m, nxt = n + 3, pair + 1
                    exponentials(0, pair, i)
                    split(m + 1, i, 4)
                    rows_out_of_psum(m, 0, 0, nxt, i)
                    exp_out_of_psum(0, pair, i)
                    exponentials(1, pair, i)
                    rows_out_of_psum(m, 0, 1, nxt, i)
                    exp_out_of_psum(1, pair, i)
                    exponentials(2, pair, i)
                    split(m + 2, i, 4)
                    rows_out_of_psum(m + 1, 1, 0, nxt, i)
                    exp_out_of_psum(2, pair, i)
                    exponentials(3, pair, i)
                    rows_out_of_psum(m + 1, 1, 1, nxt, i)
                    exp_out_of_psum(3, pair, i)
                    qk_out_of_psum(0, 0, nxt, i)
                    split(m + 3, i, 4)
                    qk_out_of_psum(0, 1, nxt, i)
                    rows_out_of_psum(m + 2, 2, 0, nxt, i)
                    qk_out_of_psum(1, 0, nxt, i)
                    out_hi(pair, i)
                    rows_out_of_psum(m + 2, 2, 1, nxt, i)
                    qk_out_of_psum(1, 1, nxt, i)
                    split(m + 4, i, 4)
                last_pair = pair + PAIRS - 1
                exponentials(0, last_pair, None)
                split(n + A_PANELS)
                for u in range(4):
                    exp_out_of_psum(u, last_pair, None)
                    if u < 3:
                        exponentials(u + 1, last_pair, None)
                out_hi(last_pair, None)
                quarter_hi(layer, "ffn", 0)
                quarter_hi(layer, "ffn", 1)
                late_half(layer, "ffn", n + A_PANELS + 1)

            def steps_before(layer, part, n, evacuate=lambda tok: None):
                evacuate(1)
                split(n, which=(0, 1))
                quarter_hi(layer, part, 0)
                quarter_hi(layer, part, 1)
                split(n, which=(2, 3))

            def mixer_b(layer):
                n, norm = cnt.n[layer, "mix"], 3 * layer

                def y_rows(j, tok):
                    act.wait_ge(blk, 2 * (n + j) + tok + 1)
                    nc.scalar.activation(y[:, tok, j * 512:(j + 1) * 512], acc[j][tok][:, :], ACT.Copy,
                                         scale=rinv[:, 2 * norm + tok:2 * norm + tok + 1]).then_inc(y_out, 1)

                late_half(layer, "mix", n + 1)
                act.wait_ge(r_done, r_index(norm, 1))
                y_rows(0, 0)
                y_rows(0, 1)
                split(n + 2)
                y_rows(1, 0)
                y_rows(1, 1)
                for u in range(4):
                    act.wait_ge(z_done, u + 1)
                    nc.scalar.copy(z_hi[:, 2 * u:2 * u + 2, :].rearrange("p c x -> p (c x)"), sbank[u % 2][:, :]
                                   ).then_inc(z_hi_done, 1)
                    split(n + 3, which=(u,))
                for g in range(4):
                    act.wait_ge(*((blk, 2 * (n + 2) + g // 2 + 1) if g % 2 else (z_done, 5 + g // 2)))
                    for eh in range(2):
                        k = 2 * g + eh
                        last = nc.scalar.activation(u_hi[:, k, :], sbank[g % 2][:, eh * SEQ:(eh + 1) * SEQ], ACT.Copy,
                                                    scale=cols[:, BSCALE + k:BSCALE + k + 1])
                    last.then_inc(z_hi_done, 1)
                split(n + 4)
                steps_before(layer, "ffn", n + 5)
                late_half(layer, "ffn", n + 6)

            def mixer_c(layer):
                n, norm, t0 = cnt.n[layer, "mix"], 3 * layer, cnt.t[layer, "mix"]

                def gelu_rows(s, tok):
                    act.wait_ge(blk, 2 * (n + s) + tok + 1)
                    dst = (gv, gu)[s // 2][:, tok, (s % 2) * 512:(s % 2 + 1) * 512]
                    nc.scalar.activation(dst, acc[s % 2][tok][:, :], ACT.Gelu_apprx_tanh,
                                         scale=rinv[:, 2 * norm + tok:2 * norm + tok + 1]).then_inc(y_out, 1)

                late_half(layer, "mix", n + 1)
                act.wait_ge(r_done, r_index(norm, 1))
                for s in range(4):
                    gelu_rows(s, 0)
                    gelu_rows(s, 1)
                    if s < 3:
                        split(n + 2 + s)
                for q in range(4):
                    act.wait_ge(t_done, t0 + 1 + q + 1)
                    nc.scalar.copy(quarter_view(c_hi, q % 2, q // 2), four(tbank[(t0 + 1 + q) % 2][:, :])).then_inc(t_hi, 1)
                split(n + 5)
                steps_before(layer, "ffn", n + 6)
                late_half(layer, "ffn", n + 7)

            def ffn(layer):
                n, t0, hid0, norm = cnt.n[layer, "ffn"], cnt.t[layer, "ffn"], cnt.hid[layer, "ffn"], 3 * layer + 1

                def silu(b, s, tok, i=None):
                    act.wait_ge(blk, at(2 * (n + b) + tok + 1, i, 4))
                    if b:
                        act.wait_ge(hid_done, at(hid0 + 2 * (b - 1) + tok + 1, i, 4))
                    nc.scalar.activation(gated[:, tok, 0:SEQ], acc[s][tok][:, 0:SEQ], ACT.Silu,
                                         scale=rinv[:, 2 * norm + tok:2 * norm + tok + 1]).then_inc(gate_done, 1)

                def hidden_hi(b, bank_, i=None):
                    act.wait_ge(t_done, at(t0 + b + 1, i, 2))
                    k0 = 2 * b if i is None else i * 4 + 2 * b
                    nc.scalar.copy(hid_hi[:, bass.ds(k0, 2), :], tbank[bank_][:, :].rearrange("p (c x) -> p c x", c=2)
                                   ).then_inc(t_hi, 1)

                act.wait_ge(r_done, r_index(norm, 1))
                silu(0, 0, 0)
                with act.Fori(0, (HB - 1) // 2, 1) as i:
                    for s in range(2):
                        silu(s, s, 1, i)
                        split(n + 2 + s, i, 2)
                        hidden_hi(s, (t0 + s) % 2, i)
                        silu(s + 1, (s + 1) % 2, 0, i)
                silu(HB - 1, 0, 1)
                d = cnt.n[layer, "down"]
                split(d + 1)
                hidden_hi(HB - 1, (t0 + HB - 1) % 2)
                split(d + 2)
                split(d + 3)
                steps_before(layer, "ple", d + 4)
                split(d + 5, which=(0, 1))
                td = cnt.t[layer, "down"]
                act.wait_ge(t_done, td + 3)
                nc.scalar.copy(p_hi[:, :, :].rearrange("p k x -> p (k x)"), tbank[(td + 2) % 2][:, :]).then_inc(t_hi, 1)
                split(d + 5, which=(2, 3))
                g = cnt.n[layer, "ple"]
                split(g)
                late_half(layer, "ple", g + 1)
                norm += 1

                def tanh(j, tok):
                    act.wait_ge(blk, 2 * (g + 1 + j) + tok + 1)
                    if j:
                        act.wait_ge(h_done, cnt.h[layer, "ple"] + tok + 1)
                    nc.scalar.activation(gated[:, tok, :], sbank[tok][:, :], ACT.Tanh,
                                         scale=half_r[:, tok:tok + 1]).then_inc(gate_done, 1)

                act.wait_ge(r_done, r_index(norm, 1))
                split(g + 2)
                tanh(0, 0)
                if layer < last_layer:
                    steps_before(layer + 1, "mix", g + 3, lambda tok: tanh(0, tok))
                else:
                    tanh(0, 1)
                tanh(1, 0)
                tanh(1, 1)

            split(0)
            quarter_hi(0, "mix", 0)
            quarter_hi(0, "mix", 1)
            pair = 0
            for layer, kind in enumerate(MIXERS):
                if kind == 0:
                    mixer_a(layer, pair)
                    pair += PAIRS
                elif kind == 1:
                    mixer_b(layer)
                else:
                    mixer_c(layer)
                ffn(layer)
            h0 = cnt.h[last_layer, "ple"]
            sum_squares(12, 0, h0 + 3)
            sum_squares(12, 1, h0 + 4)

        @block.vector
        def _(dve):
            TT, TS, STT = nc.vector.tensor_tensor, nc.vector.tensor_scalar, nc.vector.scalar_tensor_tensor

            def split(n, i=None, m=0, which=range(4)):
                for s in which:
                    dve.wait_ge(hi_done, at(4 * n + s + 1, i, 4 * m))
                    src, (hi, lo) = panel_quarter(n, s)
                    TT(lo, src, hi.bitcast(F32), ALU.subtract).then_inc(lo_done, 1)

            def quarter_scale(layer, part, q):
                order, uses, _ = quarters(layer, part)
                (tok, j), t = order[q], uses[q]
                c0 = gain_col(norm_of(layer, part), 4 * j)
                gains = bass.AP(tensor=cols[:, :].tensor, offset=c0, ap=[[13 * KT + 4, P], [1, 4], [0, P]])
                before = cnt.x[layer, part] - 4 + q - 1
                if before >= 1:
                    dve.wait_ge(x_done, before)
                dve.wait_ge(t_done, t + 1)
                TT(four(xf[:, q % 2, :]), four(tbank[t % 2][:, :]), gains, ALU.mult).then_inc(t_free, 1)

            def quarter_lo(layer, part, q):
                tok, j = quarters(layer, part)[0][q]
                par = norm_of(layer, part) % 2
                dve.wait_ge(t_hi, hi_index(layer, part, q))
                TT(quarter_view(x_lo[:, par], tok, j), four(xf[:, q % 2, :]),
                   quarter_view(x_hi[:, par], tok, j).bitcast(F32), ALU.subtract).then_inc(x_done, 1)

            def late_half(layer, part, n, update):
                quarter_scale(layer, part, 2)
                update(1, 1)
                split(n, which=(0,))
                quarter_lo(layer, part, 2)
                split(n, which=(1,))
                quarter_scale(layer, part, 3)
                split(n, which=(2,))
                quarter_lo(layer, part, 3)
                split(n, which=(3,))

            def steps_before(layer, part, n, update):
                update(1, 0)
                split(n, which=(0, 1))
                quarter_scale(layer, part, 0)
                quarter_scale(layer, part, 1)
                quarter_lo(layer, part, 0)
                quarter_lo(layer, part, 1)
                split(n, which=(2, 3))
                update(0, 1)

            def add_product(n, tok, j):
                dve.wait_ge(blk, 2 * n + tok + 1)
                hj = h[:, tok, j * 512:(j + 1) * 512]
                TT(hj, acc[j][tok][:, :], hj, ALU.add).then_inc(h_done, 1)

            def biased_scores(u, pair, i):
                hd, qt = u // 2, u % 2
                dve.wait_ge(s_done, at(4 * pair + u + 1, i, 4))
                if u == 0:
                    dve.wait_ge(bias_in, at(32 * pair + 32, i, 32))
                if u >= 2:
                    dve.wait_ge(et_done, at(4 * pair + u - 1, i, 4))
                if qt == 0:
                    parts = [(sbank[0][:, 0:QW].rearrange("p (g x) -> p g x", g=GROUPS), bias[:, hd, :, P:SEQ],
                              e[:, 0, 0:QW].rearrange("p (g x) -> p g x", g=GROUPS))]
                else:
                    parts = [(sbank[0][:, :], bias[:, hd, 0:2, :].rearrange("p g x -> p (g x)"), e[:, 1, 0:512]),
                             (sbank[1][:, 0:SEQ], bias[:, hd, 2, :], e[:, 1, 512:2 * QW])]
                nc.vector.memset(waited[:, :], 0.0)
                for b, (s_, b_, e_) in enumerate(parts):
                    nc.vector.tensor_tensor_reduce(out=e_, in0=s_, in1=b_, scale=1.0, scalar=-3e38, op0=ALU.add,
                                                   op1=ALU.max, accum_out=tops[:, u, b:b + 1]).then_inc(max_done, 1)
                dve.wait_ge(max_done, at(6 * pair + (1, 3, 4, 6)[u], i, 6))
                TS(neg_top[:, u:u + 1], tops[:, u, 0:1], tops[:, u, qt:qt + 1], -1.0, ALU.max, ALU.mult).then_inc(top_done, 1)

            def normalised(u, pair, i):
                hd, qt = u // 2, u % 2
                dve.wait_ge(pv_done, at(4 * pair + u + 1, i, 4))
                nc.vector.reciprocal(rden[:, u:u + 1], den[:, u:u + 1]).then_inc(rden_done, 1)
                dve.wait_ge(rden_done, at(4 * pair + u + 1, i, 4))
                TS(o[:, qt, hd * DH:(hd + 1) * DH], pv_bank[:, 0:DH], rden[:, u:u + 1], None, ALU.mult).then_inc(o_done, 1)

            def out_lo(pair, i):
                dve.wait_ge(ot_hi, at(pair + 1, i, 1))
                TT(o_lo[:, :], qkt_bank[:, 0:SEQ], o_hi[:, :].bitcast(F32), ALU.subtract).then_inc(ot_lo, 1)

            def add_wo(n, tok, j, i=None):
                dve.wait_ge(blk, at(2 * n + tok + 1, i, 8))
                hj = h[:, tok, j * 512:(j + 1) * 512]
                TT(hj, acc[j][tok][:, :], hj, ALU.add).then_inc(h_done, 1)

            def mixer_a(layer, pair, update):
                n = cnt.n[layer, "mix"]
                late_half(layer, "mix", n + 1, update)
                if layer == 0:
                    for g in range(GROUPS):
                        dve.wait_ge(t_done, 5 + g + 1)
                        nc.vector.tensor_copy(offsets[:, g, :], tbank[(5 + g) % 2][0:HEADS, 0:SKEW]).then_inc(t_free, 1)
                split(n + 2)
                split(n + 3)
                with dve.Fori(0, PAIRS - 1, 1) as i:
                    m = n + 3
                    biased_scores(0, pair, i)
                    split(m + 1, i, 4)
                    biased_scores(1, pair, i)
                    normalised(0, pair, i)
                    biased_scores(2, pair, i)
                    split(m + 2, i, 4)
                    normalised(1, pair, i)
                    biased_scores(3, pair, i)
                    normalised(2, pair, i)
                    split(m + 3, i, 4)
                    normalised(3, pair, i)
                    out_lo(pair, i)
                    split(m + 4, i, 4, (0, 1))
                    add_wo(m + 3, 0, 0, i)
                    add_wo(m + 3, 0, 1, i)
                    split(m + 4, i, 4, (2, 3))
                    add_wo(m + 3, 1, 0, i)
                    add_wo(m + 3, 1, 1, i)
                last_pair, w = pair + PAIRS - 1, n + A_PANELS - 1
                biased_scores(0, last_pair, None)
                split(n + A_PANELS)
                for u in range(4):
                    if u < 3:
                        biased_scores(u + 1, last_pair, None)
                    normalised(u, last_pair, None)
                out_lo(last_pair, None)
                add_wo(w, 0, 0)
                add_wo(w, 0, 1)
                quarter_scale(layer, "ffn", 0)
                add_wo(w, 1, 0)
                quarter_scale(layer, "ffn", 1)
                quarter_lo(layer, "ffn", 0)
                quarter_lo(layer, "ffn", 1)
                add_wo(w, 1, 1)
                late_half(layer, "ffn", w + 2, lambda tok, j: None)

            def mixer_b(layer, update):
                n = cnt.n[layer, "mix"]
                late_half(layer, "mix", n + 1, update)
                split(n + 2)
                for u in range(4):
                    dve.wait_ge(z_hi_done, u + 1)
                    TT(z_lo[:, 2 * u:2 * u + 2, :].rearrange("p c x -> p (c x)"), sbank[u % 2][:, :],
                       z_hi[:, 2 * u:2 * u + 2, :].rearrange("p c x -> p (c x)").bitcast(F32), ALU.subtract
                       ).then_inc(z_lo_done, 1)
                    split(n + 3, which=(u,))
                for g in range(4):
                    dve.wait_ge(z_hi_done, 5 + g)
                    for eh in range(2):
                        k = 2 * g + eh
                        last = STT(u_lo[:, k, :], sbank[g % 2][:, eh * SEQ:(eh + 1) * SEQ], cols[:, BSCALE + k:BSCALE + k + 1],
                                   u_hi[:, k, :].bitcast(F32), ALU.mult, ALU.subtract)
                    last.then_inc(z_lo_done, 1)
                split(n + 4)
                add_product(n + 3, 0, 0)
                steps_before(layer, "ffn", n + 5, lambda tok, j: add_product(n + 3 + j, tok, j))
                late_half(layer, "ffn", n + 6, lambda tok, j: add_product(n + 3 + j, tok, j))

            def mixer_c(layer, update):
                n, t0 = cnt.n[layer, "mix"], cnt.t[layer, "mix"]
                y0, hi0 = 4, cnt.hi[layer, "mix"]
                late_half(layer, "mix", n + 1, update)
                dve.wait_ge(part_in, 64)
                tril4 = bass.AP(tensor=tril[:, :].tensor, offset=0, ap=[[P, P], [0, 4], [1, P]])
                TT(w_s[:, :, :], w_s[:, :, :], tril4, ALU.mult).then_inc(masked, 1)
                split(n + 2)
                split(n + 3)
                step = 0
                for tok in range(2):
                    dve.wait_ge(y_out, y0 + 2 + tok + 1)
                    for j in range(2):
                        nc.vector.bn_stats(stats[:, tok, j, :], gv[:, tok, j * 512:(j + 1) * 512]).then_inc(dve_step, 1)
                    step += 2
                    dve.wait_ge(dve_step, step)
                    nc.vector.bn_aggr(mv[:, tok, :], stats[:, tok, :, :]).then_inc(ln_stat, 1)
                dve.wait_ge(t_done, t0 + 1)
                nc.vector.tensor_copy(w_st[:, :, :].rearrange("p g x -> p (g x)"), tbank[t0 % 2][:, :]).then_inc(t_free, 1)
                for tok in range(2):
                    dve.wait_ge(ln_stat, tok + 1)
                    dve.wait_ge(r_done, 2 * 7 + tok + 1)
                    TS(gv[:, tok, :], gv[:, tok, :], mv[:, tok, 0:1], rinv[:, 26 + tok:27 + tok],
                       ALU.subtract, ALU.mult).then_inc(dve_step, 1)
                    step += 1
                    dve.wait_ge(dve_step, step)
                    TT(gv[:, tok, :], gv[:, tok, :], gain_v[:, :], ALU.mult).then_inc(v_done, 1)
                split(n + 4)
                for half_ in range(2):
                    for q in (2 * half_, 2 * half_ + 1):
                        tok, j = q % 2, q // 2
                        dve.wait_ge(sp_done, q + 1)
                        dve.wait_ge(y_out, y0 + 4 + q + 1)
                        for s in range(2):
                            g = 2 * j + s
                            gu_ = gu[:, tok, g * SEQ:(g + 1) * SEQ]
                            last = STT(gu_, sbank[tok][:, s * SEQ:(s + 1) * SEQ], cols[:, BSP + g:BSP + g + 1], gu_,
                                       ALU.add, ALU.mult)
                        last.then_inc(gate_out, 1)
                    for q in (2 * half_, 2 * half_ + 1):
                        tok, j = q % 2, q // 2
                        dve.wait_ge(t_hi, hi0 + q + 1)
                        TT(quarter_view(c_lo, tok, j), four(tbank[(t0 + 1 + q) % 2][:, :]),
                           quarter_view(c_hi, tok, j).bitcast(F32), ALU.subtract).then_inc(t_free, 1)
                split(n + 5)
                add_product(n + 4, 0, 0)
                steps_before(layer, "ffn", n + 6, lambda tok, j: add_product(n + 4 + j, tok, j))
                late_half(layer, "ffn", n + 7, lambda tok, j: add_product(n + 4 + j, tok, j))

            def ffn(layer):
                n, t0, norm = cnt.n[layer, "ffn"], cnt.t[layer, "ffn"], 3 * layer + 1
                hi0, g0 = cnt.hi[layer, "ffn"], 26 * layer

                def hidden(b, s, tok, i=None):
                    dve.wait_ge(gate_done, at(g0 + 2 * b + tok + 1, i, 4))
                    STT(prod[:, tok, 0:SEQ], acc[s][tok][:, SEQ:512], rinv[:, 2 * norm + tok:2 * norm + tok + 1],
                        gated[:, tok, 0:SEQ], ALU.mult, ALU.mult).then_inc(hid_done, 1)

                def hidden_lo(b, bank_, i=None):
                    dve.wait_ge(t_hi, at(hi0 + b + 1, i, 2))
                    k0 = 2 * b if i is None else i * 4 + 2 * b
                    TT(hid_lo[:, bass.ds(k0, 2), :], tbank[bank_][:, :].rearrange("p (c x) -> p c x", c=2),
                       hid_hi[:, bass.ds(k0, 2), :].bitcast(F32), ALU.subtract).then_inc(t_free, 1)

                hidden(0, 0, 0)
                with dve.Fori(0, (HB - 1) // 2, 1) as i:
                    for s in range(2):
                        hidden(s, s, 1, i)
                        split(n + 2 + s, i, 2)
                        hidden_lo(s, (t0 + s) % 2, i)
                        hidden(s + 1, (s + 1) % 2, 0, i)
                hidden(HB - 1, 0, 1)
                d = cnt.n[layer, "down"]
                split(d + 1)
                hidden_lo(HB - 1, (t0 + HB - 1) % 2)
                split(d + 2)
                split(d + 3)
                add_product(d + 2, 0, 0)

                def down(tok, j):
                    add_product(d + 2 + 3 * j, tok, j)

                update_none = lambda tok, j: down(tok, j) if (tok, j) == (1, 0) else None
                steps_before(layer, "ple", d + 4, update_none)
                split(d + 5, which=(0, 1))
                td = cnt.t[layer, "down"]
                dve.wait_ge(t_hi, cnt.hi[layer, "down"] + 3)
                TT(p_lo[:, :, :].rearrange("p k x -> p (k x)"), tbank[(td + 2) % 2][:, :],
                   p_hi[:, :, :].rearrange("p k x -> p (k x)").bitcast(F32), ALU.subtract).then_inc(t_free, 1)
                split(d + 5, which=(2, 3))
                g = cnt.n[layer, "ple"]
                split(g)
                down(0, 1)
                late_half(layer, "ple", g + 1, down)

                def embed(tok, j):
                    dve.wait_ge(gate_done, g0 + 2 * HB + 2 * j + tok + 1)
                    STT(prod[:, tok, :], gated[:, tok, :], 1.0, acc[j][tok][:, :], ALU.add, ALU.mult).then_inc(embed_step, 1)
                    dve.wait_ge(embed_step, 4 * layer + 2 * j + tok + 1)
                    hj = h[:, tok, j * 512:(j + 1) * 512]
                    STT(hj, prod[:, tok, :], 0.5, hj, ALU.mult, ALU.add).then_inc(h_done, 1)

                split(g + 2)
                embed(0, 0)
                if layer < last_layer:
                    steps_before(layer + 1, "mix", g + 3, embed)
                else:
                    embed(1, 0)
                    embed(0, 1)
                return embed

            dve.wait_ge(x_in, 16)
            dve.sem_inc(h_done, 4)
            dve.sem_inc(hid_done, 2)
            nc.vector.memset(expo[:, :], -0.5).then_inc(expo_set, 1)
            nc.vector.memset(table[32:33, :], 1.0).then_inc(table_one, 1)
            dve.wait_ge(t_done, 1)
            nc.vector.tensor_copy(cols[:, :], tbank[0][:, 0:13 * KT + 4]).then_inc(t_free, 1)
            dve.wait_ge(t_free, 1)
            quarter_scale(0, "mix", 0)
            quarter_scale(0, "mix", 1)
            split(0)
            quarter_lo(0, "mix", 0)
            quarter_lo(0, "mix", 1)
            update = lambda tok, j: None
            pair = 0
            for layer, kind in enumerate(MIXERS):
                if kind == 0:
                    mixer_a(layer, pair, update)
                    pair += PAIRS
                elif kind == 1:
                    mixer_b(layer, update)
                else:
                    mixer_c(layer, update)
                update = ffn(layer)
            update(1, 1)
            dve.wait_ge(part_in, 80)
            for tok in range(2):
                dve.wait_ge(r_done, r_index(12, tok))
                STT(result[:, tok, :], h[:, tok, :], rinv[:, 24 + tok:25 + tok], gain_f[:, :],
                    ALU.mult, ALU.mult).then_inc(result_done, 1)

        @block.gpsimd
        def _(pool):
            steps = [0]

            def chained(ins):
                steps[0] += 1
                ins.then_inc(r_step, 1)
                pool.wait_ge(r_step, steps[0])

            def inverse_root(col, src, scale):
                m = mean_sq[:, col:col + 1]
                chained(nc.gpsimd.tensor_scalar(m, src, scale, EPS, ALU.mult, ALU.add))
                return nc.gpsimd.tensor_tensor(rinv[:, col:col + 1], m, expo[:, :], ALU.pow)

            def inverse_rms(norm):
                for tok in range(2):
                    col = 2 * norm + tok
                    pool.wait_ge(ssq_done, col + 1)
                    ins = inverse_root(col, ssq[:, col:col + 1], 1.0 / D)
                    scaled, by = {0: (rinv8, 1 / 8), 2: (half_r, 0.5)}.get(norm % 3, (None, None))
                    if norm < 12 and scaled is not None:
                        chained(ins)
                        ins = nc.gpsimd.tensor_scalar(scaled[:, tok:tok + 1], rinv[:, col:col + 1], by, None, ALU.mult)
                    ins.then_inc(r_done, 1)

            skewed = bass.AP(tensor=bias_skew.tensor, offset=P - 1,
                             ap=[[2 * P * SKEW, PAIRS], [P * SKEW, 2], [SKEW - 1, P], [HEADS * P * SKEW, GROUPS], [1, SEQ]])

            def load_bias(pair, i=None):
                for hd in range(2):
                    pool.dma_start(bias[:, hd, :, :], skewed[pair if i is None else i + pair, hd]).then_inc(bias_in, 16)

            pool.wait_ge(expo_set, 1)
            done = 0
            for layer, kind in enumerate(MIXERS):
                if layer == 0:
                    inverse_rms(0)
                    pool.wait_ge(t_free, 8)
                    pool.dma_start(bias_rows.rearrange("(g n) u -> n g u", g=GROUPS), offsets[:, :, :]).then_inc(rows_out, 16)
                    pool.wait_ge(rows_out, 16)
                    pool.dma_start(bias_skew, bass.AP(tensor=bias_rows.tensor, offset=0,
                                                      ap=[[SKEW, GROUPS * HEADS], [0, P], [1, SKEW]])).then_inc(rows_out, 16)
                    pool.wait_ge(rows_out, 32)
                else:
                    inverse_rms(3 * layer)
                if kind == 0:
                    load_bias(0)
                    with pool.Fori(0, PAIRS - 1, 1) as i:
                        pool.wait_ge(top_done, at(4 * done + 4, i, 4))
                        load_bias(1, i)
                    done += PAIRS
                if kind == 2:
                    for tok in range(2):
                        pool.wait_ge(ln_stat, tok + 1)
                        inverse_root(26 + tok, mv[:, tok, 1:2], 1.0).then_inc(r_done, 1)
                inverse_rms(3 * layer + 1)
                inverse_rms(3 * layer + 2)
            inverse_rms(12)


_INS = ["x", "p", "rel_table", "norm_mix", "norm_ffn", "norm_ple", "final_norm", "a_w_qkv", "a_w_o",
        "b_w_in", "b_w_grp", "b_scale", "b_w_out", "c_w_in", "c_v_gain", "c_w_s", "c_b_s", "c_w_out",
        "ffn_w_gate", "ffn_w_up", "ffn_w_down", "ple_w_gate", "ple_w_proj"]
_CONSTS = ["identity", "bucket_of", "pool_of", "lower"]
_OUTS = [((1, SEQ, D), "float32")]


def constants():
    f32 = np.float32
    bucket_of = np.zeros((33, GROUPS, SKEW), f32)
    for g, d in enumerate((1, 4, 16)):
        n = SEQ - 1 - np.arange(SKEW)
        near = np.maximum(n, 1).astype(f32)
        large = 16 + (np.log(near / 16) / np.log(2048 / 16) * 16).astype(np.int32)
        bucket = np.where(n < 16, n, np.minimum(large, 31))
        seen = (n >= 0) & (n % d == 0) & (n <= 128 * d)
        bucket_of[bucket[seen], g, np.flatnonzero(seen)] = 1.0
        bucket_of[32, g, ~seen] = NEG
    full = np.zeros((4, SEQ, SEQ), f32)
    for g, win in enumerate((2, 4, 8, 16)):
        for s in range(SEQ):
            full[g, max(0, s - win + 1):s + 1, s] = f32(1.0) / f32(min(s + 1, win))
            full[g, s, s] -= f32(1.0)
    pool_of = np.concatenate([full[:, :P, :], full[:, P:, P:]], axis=2).transpose(1, 0, 2)
    return {"identity": np.eye(P, dtype=f32), "bucket_of": bucket_of,
            "pool_of": np.ascontiguousarray(pool_of), "lower": np.tril(np.ones((P, P), f32))}


def kernel(**inputs):
    import concourse.bacc as _bacc
    from concourse.bass_utils import run_bass_kernel_spmd as _run

    nc = _bacc.Bacc("TRN2", target_bir_lowering=False, num_devices=1)
    const = constants()
    arrays, args = {}, []
    for name in _INS + _CONSTS:
        a = np.ascontiguousarray(inputs[name] if name in _INS else const[name])
        arrays[f"in_{name}_dram"] = a
        args.append(nc.dram_tensor(f"in_{name}_dram", a.shape, mybir.dt.from_np(a.dtype), kind="ExternalInput").ap())
    for i, (shape, dtype) in enumerate(_OUTS):
        args.append(nc.dram_tensor(f"out_{i}_dram", shape, mybir.dt.from_np(np.dtype(dtype)), kind="ExternalOutput").ap())
    trunk(nc, *args)
    r = _run(nc, [arrays], core_ids=[0])
    return r.results[0]["out_0_dram"]
```

```python
from contextlib import ExitStack

import numpy as np

import concourse.bass as bass
from concourse import mybir

F32 = mybir.dt.float32
F32R = mybir.dt.float32r
BF16 = mybir.dt.bfloat16
ALU = mybir.AluOpType
ACT = mybir.ActivationFunctionType

P = 128
SEQ = 256
D = 1024
KT = D // P
DEPTH = 4
GROUPS = 3
HEADS = 8
DH = 64
PAIRS = HEADS // 2
GW = HEADS * DH
QW = GROUPS * P
HIDDEN = 2816
HB = HIDDEN // SEQ
HKT = HIDDEN // P
PLE = 256
EPS = 1e-6
NEG = -1e30
SKEW = 3 * P
HALF = 4 * 512
MIXERS = [i % 3 for i in range(DEPTH)]

A_PANELS, B_PANELS, C_PANELS = 3 * PAIRS + 1, 5, 6
F_PANELS, D_PANELS, G_PANELS = HB, 6, 3


def at(base, i, step):
    return base if i is None else base + i * step


class Counts:

    def __init__(self):
        n = 0
        t = 8
        hi = 4
        h = 4
        x = 4
        hid = 2
        dmas = []
        half = []
        self.n, self.t, self.hi, self.h, self.x, self.hid = {}, {}, {}, {}, {}, {}
        for layer, kind in enumerate(MIXERS):
            def mark(part):
                key = (layer, part)
                self.n[key], self.t[key], self.hi[key] = n, t, hi
                self.h[key], self.x[key], self.hid[key] = h, x, hid
            mark("mix")
            dmas += ([3] * (3 * PAIRS) + [1], [1] * B_PANELS, [1] * C_PANELS)[kind]
            dmas += [2] * (F_PANELS + 1) + [1] * (D_PANELS - 1 + G_PANELS)
            half += ([4 * QW] * (3 * PAIRS) + [HALF],
                     [HALF, HALF, 4 * SEQ, HALF, HALF], [HALF] * C_PANELS)[kind]
            half += [HALF] * F_PANELS + [HALF, HALF, 3 * 512] * 2 + [D, HALF, HALF]
            n += (A_PANELS, B_PANELS, C_PANELS)[kind]
            t += (4, 4, 9)[kind]
            hi += (4, 4, 8)[kind]
            h += 4
            x += 4
            mark("ffn")
            n += F_PANELS
            t += HB
            hi += HB
            hid += 2 * HB
            mark("down")
            n += D_PANELS
            t += 5
            hi += 5
            h += 4
            x += 4
            mark("ple")
            n += G_PANELS
            h += 4
            if layer < DEPTH - 1:
                t += 4
                hi += 4
                x += 4
        self.panels = n
        self.half = half
        self.landed = [sum(dmas[i % 2:i + 1:2]) for i in range(n)]


def trunk(nc, x, p, rel_table, norm_mix, norm_ffn, norm_ple, final_norm, a_w_qkv, a_w_o,
          b_w_in, b_w_grp, b_scale, b_w_out, c_w_in, c_v_gain, c_w_s, c_b_s, c_w_out,
          ffn_w_gate, ffn_w_up, ffn_w_down, ple_w_gate, ple_w_proj,
          identity, bucket_of, pool_of, lower, out):
    cnt = Counts()
    last_layer = DEPTH - 1

    with ExitStack() as ctx:
        def sb(name, shape, dt=F32, scope=ctx):
            return scope.enter_context(nc.sbuf_tensor(name, shape, dt))

        def sem(name):
            return ctx.enter_context(nc.semaphore(name))

        raw = sb("raw", [P, 4, HALF])
        w_hi = sb("w_hi", [P, 2, 2 * HALF], F32R)
        w_lo = sb("w_lo", [P, 2, 2 * HALF], F32R)
        x_hi = sb("x_hi", [P, 2, KT, SEQ], F32R)
        x_lo = sb("x_lo", [P, 2, KT, SEQ], F32R)
        h = sb("h", [P, 2, D])
        ident = sb("ident", [P, P])
        rows = sb("rows", [12 * KT + KT + 4, P])
        cols = sb("cols", [P, 12 * KT + KT + 4])
        xf = sb("xf", [P, 2, 512])
        squares = sb("squares", [P, D], BF16)
        ssq = sb("ssq", [P, 26])
        mean_sq = sb("mean_sq", [P, 28])
        rinv = sb("rinv", [P, 28])
        rinv8 = sb("rinv8", [P, 2])
        half_r = sb("half_r", [P, 2])
        expo = sb("expo", [P, 1])
        gated = sb("gated", [P, 2, 512])
        prod = sb("prod", [P, 2, 512])
        p_rows = sb("p_rows", [P, 2, PLE])
        p_hi = sb("p_hi", [P, 2, SEQ], F32R)
        p_lo = sb("p_lo", [P, 2, SEQ], F32R)

        with ExitStack() as part:
            hid_hi = sb("hid_hi", [P, HKT, SEQ], F32R, part)
            hid_lo = sb("hid_lo", [P, HKT, SEQ], F32R, part)
        with ExitStack() as part:
            qk = sb("qk", [P, 2, 2, QW], F32, part)
            q_t = sb("q_t", [P, GROUPS, SEQ], F32, part)
            k_t = sb("k_t", [P, GROUPS, SEQ], F32, part)
            v = sb("v", [P, 2, GROUPS, P], F32, part)
            e = sb("e", [P, 2, GROUPS * SEQ], F32, part)
            e_t = sb("e_t", [P, 2, GROUPS * SEQ], F32, part)
            o = sb("o", [P, 2, P], F32, part)
            o_hi = sb("o_hi", [P, PAIRS, SEQ], F32R, part)
            o_lo = sb("o_lo", [P, PAIRS, SEQ], F32R, part)
            bias = sb("bias", [P, 2, GROUPS, SEQ], F32, part)
            tops = sb("tops", [P, 4, 2], F32, part)
            neg_top = sb("neg_top", [P, 4], F32, part)
            den = sb("den", [P, 4], F32, part)
            rden = sb("rden", [P, 4], F32, part)
            table = sb("table", [33, GROUPS * HEADS], F32, part)
            buckets = e[0:33].rearrange("p s x -> p (s x)")[:, 0:GROUPS * SKEW].rearrange("p (g x) -> p g x", g=GROUPS)
            offsets = e_t[0:HEADS].rearrange("p s x -> p (s x)")[:, 0:GROUPS * SKEW].rearrange("p (g x) -> p g x", g=GROUPS)
        with ExitStack() as part:
            y = sb("y", [P, 2, D], F32, part)
            pool_w = sb("pool_w", [P, 4, 3 * P], F32, part)
            z_hi = sb("z_hi", [P, KT, SEQ], F32R, part)
            z_lo = sb("z_lo", [P, KT, SEQ], F32R, part)
            u_hi = sb("u_hi", [P, KT, SEQ], F32R, part)
            u_lo = sb("u_lo", [P, KT, SEQ], F32R, part)
        with ExitStack() as part:
            gv = sb("gv", [P, 2, D], F32, part)
            gu = sb("gu", [P, 2, D], F32, part)
            gain_v = sb("gain_v", [P, D], F32, part)
            w_s = sb("w_s", [P, 4, P], F32, part)
            w_st = sb("w_st", [P, 4, P], F32, part)
            tril = sb("tril", [P, P], F32, part)
            stats = sb("stats", [P, 2, 2, 6], F32, part)
            mv = sb("mv", [P, 2, 2], F32, part)
            c_hi = sb("c_hi", [P, KT, SEQ], F32R, part)
            c_lo = sb("c_lo", [P, KT, SEQ], F32R, part)
        with ExitStack() as part:
            gain_f = sb("gain_f", [P, D], F32, part)
            result = sb("result", [P, 2, D], F32, part)

        def bank(name):
            return ctx.enter_context(nc.psum_tensor(name, [P, 512], F32))

        acc = [[bank(f"acc{j}{t}") for t in range(2)] for j in range(2)]
        tbank = [bank("tbank0"), bank("tbank1")]
        sbank = [bank("sbank0"), bank("sbank1")]
        qkt_bank, pv_bank = acc[1]

        bias_rows = nc.dram_tensor("bias_rows", (GROUPS * HEADS, SKEW), F32).ap()
        bias_skew = nc.dram_tensor("bias_skew", (GROUPS * HEADS, P, SKEW), F32).ap()

        raw_in = [sem(f"raw_in{i}") for i in range(4)]
        x_in = sem("x_in")
        id_in = sem("id_in")
        rows_in = sem("rows_in")
        table_in = sem("table_in")
        p_in = sem("p_in")
        part_in = sem("part_in")
        bias_in = sem("bias_in")
        out_in = sem("out_in")
        hi_done = sem("hi_done")
        lo_done = sem("lo_done")
        half_used = sem("half_used")
        blk = sem("blk")
        t_done = sem("t_done")
        t_free = sem("t_free")
        t_hi = sem("t_hi")
        h_done = sem("h_done")
        x_done = sem("x_done")
        ssq_done = sem("ssq_done")
        r_step = sem("r_step")
        r_done = sem("r_done")
        expo_set = sem("expo_set")
        gate_done = sem("gate_done")
        hid_done = sem("hid_done")
        dve_step = sem("dve_step")
        qkv_out = sem("qkv_out")
        qkt_done = sem("qkt_done")
        qkt_out = sem("qkt_out")
        s_done = sem("s_done")
        embed_step = sem("embed_step")
        max_done = sem("max_done")
        rden_done = sem("rden_done")
        top_done = sem("top_done")
        exp_done = sem("exp_done")
        et_done = sem("et_done")
        et_out = sem("et_out")
        pv_done = sem("pv_done")
        o_done = sem("o_done")
        ot_done = sem("ot_done")
        ot_hi = sem("ot_hi")
        ot_lo = sem("ot_lo")
        table_one = sem("table_one")
        y_out = sem("y_out")
        z_done = sem("z_done")
        z_hi_done = sem("z_hi_done")
        z_lo_done = sem("z_lo_done")
        ln_stat = sem("ln_stat")
        v_done = sem("v_done")
        sp_done = sem("sp_done")
        result_done = sem("result_done")
        rows_out = sem("rows_out")
        masked = sem("masked")
        gate_out = sem("gate_out")

        def kt_slice(par, k, kt, width, buf):
            s = (k // (kt // 2)) * HALF + (k % (kt // 2)) * width
            return buf[:, par, s:s + width]

        def quarters(layer, part):
            by_half = [(0, 0), (1, 0), (0, 1), (1, 1)]
            if part == "ffn" and MIXERS[layer] == 0:
                return [(0, 0), (0, 1), (1, 0), (1, 1)], [cnt.t[layer, "mix"] + q for q in range(4)], cnt.h[layer, "ffn"] - 4
            if part == "ffn":
                return by_half, [cnt.t[layer, "ffn"] - 4 + q for q in range(4)], cnt.h[layer, "ffn"] - 4
            if part == "ple":
                t = cnt.t[layer, "down"]
                return by_half, [t, t + 1, t + 3, t + 4], cnt.h[layer, "down"]
            if layer == 0:
                return by_half, [1, 2, 3, 4], 0
            return by_half, [cnt.t[layer - 1, "ple"] + q for q in range(4)], cnt.h[layer - 1, "ple"]

        def gain_col(i, k):
            return (i % 3) * DEPTH * KT + (i // 3) * KT + k

        BSCALE = 12 * KT
        BSP = 13 * KT

        qkv_src = a_w_qkv.rearrange("a (f k p) (c g n x) -> a c n f g p k x",
                                    f=2, p=P, c=3, g=GROUPS, x=P)
        wo_src = a_w_o.rearrange("a (f n p) x -> a f p n x", f=2, p=P)

        def square(w):
            return w.rearrange("(f k p) (j x) -> j f p k x", f=2, p=P, x=512)

        block = ctx.enter_context(nc.Block())


        @block.sync
        def _(sp):
            def slot_free(n, half, i=None, m=0):
                if n >= 2:
                    sp.wait_ge(lo_done, at(4 * (n - 2) + 2 * half + 2, i, 4 * m))

            def half_slot(n, half, **dims):
                length = 1
                for size in dims.values():
                    length *= size
                names = " ".join(dims)
                return raw[:, 2 * (n % 2) + half, 0:length].rearrange(f"p ({names}) -> p {names}", **dims)

            def load_qkv(n, a, c, pair):
                for f in range(2):
                    slot_free(n, f)
                    for g in range(GROUPS):
                        sp.dma_start(half_slot(n, f, k=4, g=GROUPS, x=P)[:, :, g, :],
                                     qkv_src[a, c, pair, f, g]).then_inc(raw_in[2 * (n % 2) + f], 16)

            def load_wo(n, a):
                for f in range(2):
                    slot_free(n, f)
                    sp.dma_start(half_slot(n, f, k=2, x=D), wo_src[a, f]).then_inc(raw_in[2 * (n % 2) + f], 16)

            def load_square(n, w, j):
                for f in range(2):
                    slot_free(n, f)
                    sp.dma_start(half_slot(n, f, k=4, x=512), square(w)[j, f]).then_inc(raw_in[2 * (n % 2) + f], 16)

            def load_hidden(n, layer, b, i=None):
                for f in range(2):
                    slot_free(n, f, i, 2)
                    dst = half_slot(n, f, k=4, s=2, x=SEQ)
                    for s, w in ((0, ffn_w_gate), (1, ffn_w_up)):
                        src = w[layer].rearrange("(f k p) (b x) -> b f p k x", f=2, p=P, x=SEQ)[b, f]
                        sp.dma_start(dst[:, :, s, :], src).then_inc(raw_in[2 * (n % 2) + f], 16)

            def mixer_a(layer, a):
                n = cnt.n[layer, "mix"]
                for pair in range(PAIRS):
                    for c in range(3):
                        load_qkv(n + 3 * pair + c, a, c, pair)
                load_wo(n + 3 * PAIRS, a)

            def mixer_b(layer):
                n = cnt.n[layer, "mix"]
                sp.wait_ge(blk, 2 * cnt.n[layer - 1, "ple"])
                sp.dma_start(pool_w[:, :, :], pool_of).then_inc(part_in, 16)
                for j in range(2):
                    load_square(n + j, b_w_in[0], j)
                for f in range(2):
                    slot_free(n + 2, f)
                    src = b_w_grp[0].rearrange("(f g) (c p) x -> f p (g c) x", f=2, p=P)[f]
                    sp.dma_start(half_slot(n + 2, f, k=4, x=SEQ), src).then_inc(raw_in[2 * (n % 2) + f], 16)
                for j in range(2):
                    load_square(n + 3 + j, b_w_out[0], j)

            def mixer_c(layer):
                n = cnt.n[layer, "mix"]
                for j in (0, 1):
                    load_square(n + j, c_w_in[0], 2 + j)
                sp.wait_ge(blk, 2 * cnt.n[layer - 1, "ple"])
                sp.dma_start(gain_v[:, :], bass.AP(tensor=c_v_gain.tensor, offset=0, ap=[[0, P], [1, D]])
                             ).then_inc(part_in, 16)
                sp.dma_start(w_s[:, :, :], c_w_s[0].rearrange("g t s -> t g s")).then_inc(part_in, 16)
                sp.dma_start(tril[:, :], lower).then_inc(part_in, 16)
                for j in (0, 1):
                    load_square(n + 2 + j, c_w_in[0], j)
                for j in (0, 1):
                    load_square(n + 4 + j, c_w_out[0], j)

            def ffn(layer):
                n = cnt.n[layer, "ffn"]
                load_hidden(n, layer, 0)
                with sp.Fori(0, (HB - 1) // 2, 1) as i:
                    for s in range(2):
                        load_hidden(n + 1 + s, layer, i * 2 + (s + 1), i)
                n = cnt.n[layer, "down"]
                w = ffn_w_down[layer].rearrange("(k p) (j x) -> j p k x", p=P, x=512)
                for j in range(2):
                    for t, (k0, kh) in enumerate(((0, 4), (8, 4), (16, 3))):
                        for f in range(2):
                            slot_free(n, f)
                            for k1, k2 in ((0, 2), (2, 4)) if (j, t) == (0, 0) else ((0, kh),):
                                sp.dma_start(half_slot(n, f, k=kh, x=512)[:, k1:k2, :],
                                             w[j][:, k0 + f * kh + k1:k0 + f * kh + k2, :]
                                             ).then_inc(raw_in[2 * (n % 2) + f], 16)
                        n += 1
                    if j == 0:
                        sp.dma_start(p_rows[:, :, :], p[layer, 0].rearrange("(t p) d -> p t d", p=P)).then_inc(p_in, 16)
                n = cnt.n[layer, "ple"]
                for f in range(2):
                    slot_free(n, f)
                    sp.dma_start(half_slot(n, f, k=1, x=D)[:, 0, :], ple_w_proj[layer][f * P:(f + 1) * P, :]
                                 ).then_inc(raw_in[2 * (n % 2) + f], 16)
                for j in range(2):
                    load_square(n + 1 + j, ple_w_gate[layer], j)

            sp.dma_start(h[:, :, :], x[0].rearrange("(t p) d -> p t d", p=P)).then_inc(x_in, 16)
            sp.dma_start(ident[:, :], identity).then_inc(id_in, 16)
            for b, g in enumerate((norm_mix, norm_ffn, norm_ple)):
                sp.dma_start(rows[b * DEPTH * KT:(b + 1) * DEPTH * KT, :], g.rearrange("l (k x) -> (l k) x", x=P)
                             ).then_inc(rows_in, 16)
            sp.dma_start(rows[BSCALE:BSCALE + KT, :], b_scale.rearrange("l (k x) -> (l k) x", x=P)).then_inc(rows_in, 16)
            sp.dma_start(rows[BSP:BSP + 4, :], c_b_s[0]).then_inc(rows_in, 16)
            sp.dma_start(table[0:32, :], rel_table).then_inc(table_in, 16)
            sp.dma_start(buckets, bucket_of).then_inc(table_in, 16)
            for layer, kind in enumerate(MIXERS):
                if kind == 0:
                    mixer_a(layer, layer // 3)
                elif kind == 1:
                    mixer_b(layer)
                else:
                    mixer_c(layer)
                ffn(layer)
            sp.wait_ge(blk, 2 * cnt.n[last_layer, "ple"])
            sp.dma_start(gain_f[:, :], bass.AP(tensor=final_norm.tensor, offset=0, ap=[[0, P], [1, D]])).then_inc(part_in, 16)
            for tok in range(2):
                sp.wait_ge(result_done, tok + 1)
                sp.dma_start(out[0][tok * P:(tok + 1) * P, :], result[:, tok, :]).then_inc(out_in, 16)
            sp.wait_ge(out_in, 32)

        @block.tensor
        def _(pe):
            def passes(out_, st, st_lo, mv_, mv_lo, start, stop):
                nc.tensor.matmul(out_, st, mv_, start=start, stop=False)
                nc.tensor.matmul(out_, st_lo, mv_, start=False, stop=False)
                return nc.tensor.matmul(out_, st, mv_lo, start=False, stop=stop)

            def xt(norm):
                return x_hi[:, norm % 2], x_lo[:, norm % 2]

            def product(n, tok, kt, width, act, k0, out_, i=None, m=0, waits={}, mid={},
                        start=True, stop=True):
                for k in range(kt):
                    if tok == 0 and k == 0:
                        pe.wait_ge(lo_done, at(4 * n + 2, i, 4 * m))
                    if tok == 0 and k == kt // 2:
                        pe.wait_ge(lo_done, at(4 * n + 4, i, 4 * m))
                    if k in waits:
                        pe.wait_ge(*waits[k])
                    if k in mid:
                        mid[k]()
                    last = passes(out_, act[0][:, k0 + k, tok * P:(tok + 1) * P], act[1][:, k0 + k, tok * P:(tok + 1) * P],
                                  kt_slice(n % 2, k, kt, width, w_hi), kt_slice(n % 2, k, kt, width, w_lo),
                                  start=start and k == 0, stop=stop and k == kt - 1)
                    if tok == 1 and k == kt // 2 - 1:
                        last.then_inc(half_used, 1)
                last.then_inc(blk, 1)

            def quarter(layer, part, q):
                order, uses, h0 = quarters(layer, part)
                (tok, j), t = order[q], uses[q]
                pe.wait_ge(h_done, 4 if h0 == 0 else h0 + q + 1)
                pe.wait_ge(t_free, t - 1 if t > 1 else 1)
                for c in range(4):
                    last = nc.tensor.transpose(tbank[t % 2][:, c * P:(c + 1) * P],
                                               h[:, tok, (4 * j + c) * P:(4 * j + c + 1) * P], ident[:, :])
                last.then_inc(t_done, 1)

            def x_waits(layer, part, tok):
                order, _, _ = quarters(layer, part)
                x0 = {"mix": cnt.x[layer, "mix"], "ffn": cnt.x[layer, "ffn"], "ple": cnt.x[layer, "ple"]}[part] - 4
                return {4 * j: (x_done, x0 + order.index((tok, j)) + 1) for j in range(2)}

            def scores(u, pair):
                qt, hd = u // 2, u % 2
                if u == 0:
                    pe.wait_ge(qkt_out, 4 * pair + 4)
                if pair or u > 1:
                    pe.wait_ge(top_done, 4 * pair + (0, 0, 2, 3)[u])
                for g in range(GROUPS):
                    dst = sbank[hd][:, g * P:(g + 1) * P] if qt == 0 else sbank[g // 2][:, (g % 2) * SEQ:(g % 2 + 1) * SEQ]
                    last = nc.tensor.matmul(dst, q_t[hd * DH:(hd + 1) * DH, g, qt * P:(qt + 1) * P],
                                            k_t[hd * DH:(hd + 1) * DH, g, 0:(qt + 1) * P], start=True, stop=True)
                last.then_inc(s_done, 1)

            def exp_transposes(u, pair):
                qt, hd = u // 2, u % 2
                pe.wait_ge(exp_done, 4 * pair + u + 1)
                if qt:
                    pe.wait_ge(et_out, 4 * pair + u)
                for b in range(GROUPS * (qt + 1)):
                    last = nc.tensor.transpose(tbank[b // 4 if qt else hd][:, (b % 4) * P:(b % 4 + 1) * P],
                                               e[:, hd, b * P:(b + 1) * P], ident[:, :])
                last.then_inc(et_done, 1)

            def weighted_values(qt, pair):
                pe.wait_ge(et_out, 4 * pair + 2 * qt + 2)
                pe.wait_ge(qkv_out, 6 * pair + 5 + qt)
                if pair or qt:
                    pe.wait_ge(ot_lo, 2 * pair + qt)
                blocks = [(g, t) for g in range(GROUPS) for t in range(qt + 1)]
                for hd in range(2):
                    for b, (g, t) in enumerate(blocks):
                        last = nc.tensor.matmul(pv_bank[:, hd * DH:(hd + 1) * DH], e_t[:, hd, b * P:(b + 1) * P],
                                                v[:, t, g, hd * DH:(hd + 1) * DH],
                                                start=(b == 0), stop=(b == len(blocks) - 1))
                last.then_inc(pv_done, 1)

            def qk_transposes(c, tok, pair):
                pe.wait_ge(qkv_out, 6 * pair + 2 * c + tok + 1)
                if pair or c or tok:
                    pe.wait_ge(qkt_out, 4 * pair + 2 * c + tok)
                for g in range(GROUPS):
                    last = nc.tensor.transpose(qkt_bank[:, g * P:(g + 1) * P],
                                               qk[:, c, tok, g * P:(g + 1) * P], ident[:, :])
                last.then_inc(qkt_done, 1)

            def out_transpose(tok, pair):
                pe.wait_ge(o_done, 2 * pair + tok + 1)
                nc.tensor.transpose(pv_bank[:, 0:P], o[:, tok, :], ident[:, :]).then_inc(ot_done, 1)

            def wo_product(n, j, tok, pair):
                s = (pair // 2) * HALF + (pair % 2) * D + j * 512
                return passes(acc[j][tok][:, :], o_hi[:, pair, tok * P:(tok + 1) * P], o_lo[:, pair, tok * P:(tok + 1) * P],
                              w_hi[:, n % 2, s:s + 512], w_lo[:, n % 2, s:s + 512], start=pair == 0, stop=pair == PAIRS - 1)

            def mixer_a(layer, pair):
                n, norm = cnt.n[layer, "mix"], 3 * layer
                quarter(layer, "mix", 2)
                for r in range(PAIRS):
                    this, prev = pair + r, pair + r - 1

                    def attention(step):
                        if r and step == 0:
                            exp_transposes(0, prev)
                            exp_transposes(1, prev)
                            scores(2, prev)
                        if r and step == 2:
                            weighted_values(0, prev)
                            exp_transposes(2, prev)
                            scores(3, prev)
                        if r and step == 3:
                            out_transpose(0, prev)
                        if r and step == 4:
                            exp_transposes(3, prev)
                        if r and step == 6:
                            weighted_values(1, prev)
                        if r and step == 8:
                            out_transpose(1, prev)
                        if step in (5, 7, 9, 10):
                            c, tok = divmod((5, 7, 9, 10).index(step), 2)
                            qk_transposes(c, tok, this)
                        if step == 11:
                            scores(0, this)
                            scores(1, this)
                        if (layer, r, step) == (0, 0, 2):
                            bias_vectors()

                    for b in range(6):
                        c, tok = b // 2, b % 2
                        attention(2 * b)
                        if r or c:
                            pe.wait_ge(qkv_out, 6 * this + b - 1)
                        first = r == 0 and c == 0
                        mid = {KT // 2: lambda: attention(2 * b + 1)}
                        if first and tok == 0:
                            mid[6] = lambda: quarter(layer, "mix", 3)
                        product(n + 3 * r + c, tok, KT, QW, xt(norm), 0, acc[0][tok][:, 0:QW],
                                waits=x_waits(layer, "mix", tok) if first else {}, mid=mid)

                w, last_pair = n + 3 * PAIRS, pair + PAIRS - 1
                filling = iter([(j, tok, k) for j, tok in ((0, 0), (1, 0), (0, 1)) for k in range(PAIRS - 1)])

                def fill(count):
                    for _ in range(count):
                        wo_product(w, *next(filling))

                exp_transposes(0, last_pair)
                exp_transposes(1, last_pair)
                scores(2, last_pair)
                pe.wait_ge(lo_done, 4 * w + 4)
                pe.wait_ge(ot_lo, 2 * last_pair)
                pe.wait_ge(qkv_out, 6 * last_pair + 6)
                pe.wait_ge(qkt_out, 4 * last_pair + 4)
                fill(3)
                scores(3, last_pair)
                weighted_values(0, last_pair)
                exp_transposes(2, last_pair)
                fill(1)
                out_transpose(0, last_pair)
                fill(2)
                exp_transposes(3, last_pair)
                fill(1)
                pe.wait_ge(ot_lo, 2 * last_pair + 1)
                wo_product(w, 0, 0, PAIRS - 1)
                wo_product(w, 1, 0, PAIRS - 1).then_inc(blk, 1)
                fill(2)
                weighted_values(1, last_pair)
                quarter(layer, "ffn", 0)
                out_transpose(1, last_pair)
                quarter(layer, "ffn", 1)
                pe.wait_ge(ot_lo, 2 * last_pair + 2)
                for k in range(PAIRS):
                    last = wo_product(w, 1, 1, k)
                    if k == 1:
                        last.then_inc(half_used, 1)
                wo_product(w, 0, 1, PAIRS - 1).then_inc(blk, 1)

            def bias_vectors():
                pe.wait_ge(table_in, 32)
                pe.wait_ge(table_one, 1)
                for g in range(GROUPS):
                    t = 5 + g
                    pe.wait_ge(t_free, t - 1)
                    nc.tensor.matmul(tbank[t % 2][0:HEADS, 0:SKEW], table[:, g * HEADS:(g + 1) * HEADS],
                                     buckets[:, g, :], start=True, stop=True).then_inc(t_done, 1)

            def mixer_out(layer, n, act, waits):
                for j in range(2):
                    for tok in range(2):
                        product(n + j, tok, KT, 512, act, 0, acc[j][tok][:, :], waits=waits[tok] if j == 0 else {})
                        if (j, tok) == (1, 0):
                            quarter(layer, "ffn", 0)
                            quarter(layer, "ffn", 1)
                quarter(layer, "ffn", 2)

            def mixer_b(layer):
                n, norm = cnt.n[layer, "mix"], 3 * layer
                quarter(layer, "mix", 2)
                for j in range(2):
                    for tok in range(2):
                        product(n + j, tok, KT, 512, xt(norm), 0, acc[j][tok][:, :],
                                waits=x_waits(layer, "mix", tok) if j == 0 else {},
                                mid={6: lambda: quarter(layer, "mix", 3)} if j == tok == 0 else {})
                pe.wait_ge(part_in, 16)
                for u in range(4):
                    pe.wait_ge(y_out, 2 if u < 2 else 4)
                    if u >= 2:
                        pe.wait_ge(z_lo_done, u - 1)
                    for c in range(2):
                        f = 2 * u + c
                        dst = sbank[u % 2][:, c * SEQ:(c + 1) * SEQ]
                        nc.tensor.matmul(dst, y[:, 0, f * P:(f + 1) * P], pool_w[:, u, 0:SEQ],
                                         start=True, stop=False)
                        last = nc.tensor.matmul(dst[:, P:SEQ], y[:, 1, f * P:(f + 1) * P], pool_w[:, u, SEQ:SEQ + P],
                                                start=False, stop=True)
                    last.then_inc(z_done, 1)
                for g in range(4):
                    pe.wait_ge(lo_done, 4 * (n + 2) + (2 if g < 2 else 4))
                    pe.wait_ge(z_lo_done, g + 3)
                    for eh in range(2):
                        dst = sbank[g % 2][:, eh * SEQ:(eh + 1) * SEQ]
                        for c in range(2):
                            wg_hi, wg_lo = (kt_slice(n % 2, 2 * g + c, KT, SEQ, b)[:, eh * P:(eh + 1) * P] for b in (w_hi, w_lo))
                            last = passes(dst, wg_hi, wg_lo, z_hi[:, 2 * g + c, :], z_lo[:, 2 * g + c, :],
                                          start=c == 0, stop=c == 1)
                            if (g, eh, c) == (2, 0, 0):
                                last.then_inc(half_used, 1)
                    last.then_inc(blk if g % 2 else z_done, 1)
                by_group = {2 * g: (z_lo_done, 5 + g) for g in range(4)}
                mixer_out(layer, n + 3, (u_hi, u_lo), [by_group, by_group])

            def mixer_c(layer):
                n, t0, norm = cnt.n[layer, "mix"], cnt.t[layer, "mix"], 3 * layer
                quarter(layer, "mix", 2)
                y0 = 4

                def block_in(s, tok):
                    if s >= 2:
                        pe.wait_ge(y_out, y0 + 2 * (s - 2) + tok + 1)
                    product(n + s, tok, KT, 512, xt(norm), 0, acc[s % 2][tok][:, :],
                            waits=x_waits(layer, "mix", tok) if s == 0 else {},
                            mid={6: lambda: quarter(layer, "mix", 3)} if s == tok == 0 else {})

                def spatial(j, tok):
                    pe.wait_ge(v_done, tok + 1)
                    if j:
                        pe.wait_ge(gate_out, tok + 1)
                    for s in range(2):
                        g = 2 * j + s
                        last = nc.tensor.matmul(sbank[tok][:, s * SEQ:(s + 1) * SEQ], w_st[:, g, :],
                                                gv[:, tok, g * SEQ:(g + 1) * SEQ], start=True, stop=True)
                    last.then_inc(sp_done, 1)

                def gated_quarter(q):
                    tok, j = q % 2, q // 2
                    t = t0 + 1 + q
                    pe.wait_ge(gate_out, q + 1)
                    pe.wait_ge(t_free, t - 1)
                    for c in range(4):
                        last = nc.tensor.transpose(tbank[t % 2][:, c * P:(c + 1) * P],
                                                   gu[:, tok, (4 * j + c) * P:(4 * j + c + 1) * P], ident[:, :])
                    last.then_inc(t_done, 1)

                for s in range(3):
                    for tok in range(2):
                        block_in(s, tok)
                pe.wait_ge(masked, 1)
                pe.wait_ge(t_free, t0 - 1)
                for g in range(4):
                    last = nc.tensor.transpose(tbank[t0 % 2][:, g * P:(g + 1) * P], w_s[:, g, :], ident[:, :])
                last.then_inc(t_done, 1)
                block_in(3, 0)
                pe.wait_ge(t_free, t0 + 1)
                spatial(0, 0)
                spatial(0, 1)
                block_in(3, 1)
                gated_quarter(0)
                gated_quarter(1)
                spatial(1, 0)
                spatial(1, 1)
                gated_quarter(2)
                gated_quarter(3)
                mixer_out(layer, n + 4, (c_hi, c_lo),
                          [{4 * j: (t_free, t0 + 1 + 2 * j + tok + 1) for j in range(2)} for tok in range(2)])

            def ffn(layer):
                n, t0, hid0, norm = cnt.n[layer, "ffn"], cnt.t[layer, "ffn"], cnt.hid[layer, "ffn"], 3 * layer + 1

                def hidden_transposes(b, bank_, i=None):
                    pe.wait_ge(hid_done, at(hid0 + 2 * b + 2, i, 4))
                    pe.wait_ge(t_free, at(t0 + b - 1, i, 2))
                    for c in range(2):
                        for tok in range(2):
                            last = nc.tensor.transpose(tbank[bank_][:, (2 * c + tok) * P:(2 * c + tok + 1) * P],
                                                       prod[:, tok, c * P:(c + 1) * P], ident[:, :])
                    last.then_inc(t_done, 1)

                late = {6: lambda: quarter(layer, "ffn", 3)}
                if MIXERS[layer] == 0:
                    late[2] = lambda: quarter(layer, "ffn", 2)
                for tok in range(2):
                    product(n, tok, KT, 512, xt(norm), 0, acc[0][tok][:, :], waits=x_waits(layer, "ffn", tok),
                            mid={} if tok else late)
                with pe.Fori(0, (HB - 1) // 2, 1) as i:
                    for s in range(2):
                        for tok in range(2):
                            pe.wait_ge(hid_done, at(hid0 + 2 * (s - 1) + tok + 1, i, 4))
                            product(n + 1 + s, tok, KT, 512, xt(norm), 0, acc[(1 + s) % 2][tok][:, :], i, 2)
                            if tok == 0:
                                hidden_transposes(s, (t0 + s) % 2, i)

                n, hb, td = cnt.n[layer, "down"], cnt.h[layer, "down"], cnt.t[layer, "down"]
                for j in range(2):
                    for s, (k0, kt) in enumerate(((0, 8), (8, 8), (16, 6))):
                        for tok in range(2):
                            if (j, s) == (0, 0):
                                pe.wait_ge(hid_done, hid0 + 2 * (HB - 1) + tok + 1)
                            if (j, s, tok) == (0, 2, 0):
                                pe.wait_ge(t_free, t0 + HB)
                            product(n, tok, kt, 512, (hid_hi, hid_lo), k0, acc[j][tok][:, :], start=s == 0, stop=s == 2)
                            if (j, s, tok) == (0, 0, 0):
                                hidden_transposes(HB - 1, (t0 + HB - 1) % 2)
                            if (j, s, tok) == (1, 0, 0):
                                quarter(layer, "ple", 0)
                                quarter(layer, "ple", 1)
                            if (j, s, tok) == (1, 1, 0):
                                pe.wait_ge(p_in, 16 * (layer + 1))
                                pe.wait_ge(t_free, td + 1)
                                for k in range(2):
                                    for tk in range(2):
                                        last = nc.tensor.transpose(tbank[(td + 2) % 2][:, (2 * k + tk) * P:(2 * k + tk + 1) * P],
                                                                   p_rows[:, tk, k * P:(k + 1) * P], ident[:, :])
                                last.then_inc(t_done, 1)
                        n += 1
                quarter(layer, "ple", 2)

                pe.wait_ge(lo_done, 4 * n + 4)
                pe.wait_ge(t_free, td + 3)
                for tok in range(2):
                    pe.wait_ge(h_done, hb + 2 + tok + 1)
                    for j in range(2):
                        for k in range(2):
                            w_k = [b[:, n % 2, k * HALF + j * 512:k * HALF + (j + 1) * 512] for b in (w_hi, w_lo)]
                            last = passes(acc[j][tok][:, :], p_hi[:, k, tok * P:(tok + 1) * P],
                                          p_lo[:, k, tok * P:(tok + 1) * P], *w_k, start=k == 0, stop=k == 1)
                            if (tok, j, k) == (1, 1, 0):
                                last.then_inc(half_used, 1)
                    last.then_inc(blk, 1)
                    if tok == 0:
                        quarter(layer, "ple", 3)
                for j in range(2):
                    for tok in range(2):
                        if j:
                            pe.wait_ge(gate_done, 26 * layer + 2 * HB + tok + 1)
                        product(n + 1 + j, tok, KT, 512, xt(3 * layer + 2), 0, sbank[tok][:, :],
                                waits=x_waits(layer, "ple", tok) if j == 0 else {})
                        if (j, tok) == (1, 0) and layer < last_layer:
                            quarter(layer + 1, "mix", 0)
                            quarter(layer + 1, "mix", 1)

            pe.wait_ge(id_in, 16)
            pe.wait_ge(rows_in, 16 * 5)
            nc.tensor.transpose(tbank[0][:, 0:13 * KT + 4], rows[:, :], ident[0:13 * KT + 4, 0:13 * KT + 4]).then_inc(t_done, 1)
            quarter(0, "mix", 0)
            quarter(0, "mix", 1)
            pair = 0
            for layer, kind in enumerate(MIXERS):
                if kind == 0:
                    mixer_a(layer, pair)
                    pair += PAIRS
                elif kind == 1:
                    mixer_b(layer)
                else:
                    mixer_c(layer)
                ffn(layer)

        def panel_quarter(n, s):
            q = cnt.half[n] // 2
            a, half = (s % 2) * q, s // 2
            return raw[:, 2 * (n % 2) + half, a:a + q], [b[:, n % 2, half * HALF + a:half * HALF + a + q] for b in (w_hi, w_lo)]

        def hi_index(layer, part, q):
            if part == "mix" and layer == 0:
                return q + 1
            if part == "mix":
                return cnt.hi[layer - 1, "ple"] + q + 1
            if part == "ffn":
                return cnt.hi[layer, "ffn"] - 4 + q + 1
            return cnt.hi[layer, "down"] + (1, 2, 4, 5)[q]

        def norm_of(layer, part):
            return 3 * layer + ("mix", "ffn", "ple").index(part)

        def r_index(norm, tok):
            return 2 * norm + tok + 1 + (2 if norm > 6 else 0)

        def quarter_view(buf, tok, j):
            return buf[:, 4 * j:4 * j + 4, tok * P:(tok + 1) * P]

        def four(ap):
            return ap.rearrange("p (c x) -> p c x", c=4)

        @block.scalar
        def _(act):
            def split(n, i=None, m=0, which=range(4)):
                for s in which:
                    if s == 0 and n >= 2:
                        act.wait_ge(half_used, at(n - 1, i, m))
                    if s == 2 and n >= 2:
                        act.wait_ge(blk, at(2 * n - 2, i, 2 * m))
                    if s % 2 == 0:
                        step = 16 * (cnt.landed[n + m] - cnt.landed[n]) if m else 0
                        act.wait_ge(raw_in[2 * (n % 2) + s // 2], at(16 * cnt.landed[n], i, step))
                    src, (hi, _) = panel_quarter(n, s)
                    nc.scalar.copy(hi, src).then_inc(hi_done, 1)

            def quarter_hi(layer, part, q):
                order, uses, _ = quarters(layer, part)
                tok, j = order[q]
                act.wait_ge(t_free, uses[q] + 1)
                nc.scalar.copy(quarter_view(x_hi[:, norm_of(layer, part) % 2], tok, j), four(xf[:, q % 2, :])
                               ).then_inc(t_hi, 1)

            def sum_squares(norm, tok, ready):
                act.wait_ge(h_done, ready)
                if norm or tok:
                    act.wait_ge(ssq_done, 2 * norm + tok)
                nc.scalar.activation(squares[:, :], h[:, tok, :], ACT.Square,
                                     accum_out=ssq[:, 2 * norm + tok:2 * norm + tok + 1]).then_inc(ssq_done, 1)

            def late_half(layer, part, n):
                norm, (_, _, h0) = norm_of(layer, part), quarters(layer, part)
                split(n, which=(0,))
                quarter_hi(layer, part, 2)
                split(n, which=(1,))
                quarter_hi(layer, part, 3)
                split(n, which=(2, 3))
                sum_squares(norm, 0, 4 if h0 == 0 else h0 + 3)
                sum_squares(norm, 1, h0 + 4)

            def rows_out_of_psum(layer, n, c, tok, pair):
                act.wait_ge(blk, 2 * (n + c) + tok + 1)
                if c == 2 and pair:
                    act.wait_ge(pv_done, 2 * pair)
                dst = v[:, tok, :, :].rearrange("p g x -> p (g x)") if c == 2 else qk[:, c, tok, :]
                scale = rinv8[:, tok:tok + 1] if c == 0 else rinv[:, 6 * layer + tok:6 * layer + tok + 1]
                nc.scalar.activation(dst, acc[0][tok][:, 0:QW], ACT.Copy, scale=scale).then_inc(qkv_out, 1)

            def qk_out_of_psum(c, tok, pair):
                act.wait_ge(qkt_done, 4 * pair + 2 * c + tok + 1)
                dst = (q_t, k_t)[c][:, :, tok * P:(tok + 1) * P]
                nc.scalar.copy(dst, qkt_bank[:, 0:QW].rearrange("p (g x) -> p g x", g=GROUPS)).then_inc(qkt_out, 1)

            def exponentials(u, pair):
                act.wait_ge(top_done, 4 * pair + u + 1)
                width = QW * (u // 2 + 1)
                nc.scalar.activation(e[:, u % 2, 0:width], e[:, u % 2, 0:width], ACT.Exp,
                                     bias=neg_top[:, u:u + 1], accum_out=den[:, u:u + 1]).then_inc(exp_done, 1)

            def exp_out_of_psum(u, pair):
                qt, hd = u // 2, u % 2
                act.wait_ge(et_done, 4 * pair + u + 1)
                if pair or qt:
                    act.wait_ge(pv_done, 2 * pair + qt)
                if qt == 0:
                    nc.scalar.copy(e_t[:, hd, 0:QW], tbank[hd][:, 0:QW]).then_inc(et_out, 1)
                else:
                    nc.scalar.copy(e_t[:, hd, 0:512], tbank[0][:, :])
                    nc.scalar.copy(e_t[:, hd, 512:2 * QW], tbank[1][:, 0:2 * QW - 512]).then_inc(et_out, 1)

            def out_hi(tok, r, pair):
                act.wait_ge(ot_done, 2 * pair + tok + 1)
                nc.scalar.copy(o_hi[:, r, tok * P:(tok + 1) * P], pv_bank[:, 0:P]).then_inc(ot_hi, 1)

            def mixer_a(layer, pair):
                norm = 3 * layer
                late_half(layer, "mix", cnt.n[layer, "mix"] + 1)
                act.wait_ge(r_done, r_index(norm, 1))
                for r in range(PAIRS):
                    n, this, prev = cnt.n[layer, "mix"] + 3 * r, pair + r, pair + r - 1
                    if r:
                        rows_out_of_psum(layer, n - 3, 2, 1, prev)
                        exp_out_of_psum(0, prev)
                        exp_out_of_psum(1, prev)
                        split(n + 1, which=(0, 1))
                        exponentials(2, prev)
                    rows_out_of_psum(layer, n, 0, 0, this)
                    if r:
                        exp_out_of_psum(2, prev)
                        exponentials(3, prev)
                        split(n + 1, which=(2,))
                        out_hi(0, r - 1, prev)
                        split(n + 1, which=(3,))
                    rows_out_of_psum(layer, n, 0, 1, this)
                    if r:
                        exp_out_of_psum(3, prev)
                    split(n + 2, which=(0,))
                    qk_out_of_psum(0, 0, this)
                    split(n + 2, which=(1,))
                    rows_out_of_psum(layer, n, 1, 0, this)
                    split(n + 2, which=(2,))
                    qk_out_of_psum(0, 1, this)
                    split(n + 2, which=(3,))
                    rows_out_of_psum(layer, n, 1, 1, this)
                    if r:
                        out_hi(1, r - 1, prev)
                    split(n + 3, which=(0,))
                    qk_out_of_psum(1, 0, this)
                    rows_out_of_psum(layer, n, 2, 0, this)
                    qk_out_of_psum(1, 1, this)
                    split(n + 3, which=(1, 2))
                    exponentials(0, this)
                    exponentials(1, this)
                    split(n + 3, which=(3,))
                f, last_pair = n + 4, this
                rows_out_of_psum(layer, n, 2, 1, last_pair)
                exp_out_of_psum(0, last_pair)
                exp_out_of_psum(1, last_pair)
                split(f, which=(0,))
                exponentials(2, last_pair)
                split(f, which=(1,))
                exponentials(3, last_pair)
                exp_out_of_psum(2, last_pair)
                out_hi(0, PAIRS - 1, last_pair)
                exp_out_of_psum(3, last_pair)
                split(f, which=(2, 3))
                quarter_hi(layer, "ffn", 0)
                out_hi(1, PAIRS - 1, last_pair)
                quarter_hi(layer, "ffn", 1)
                late_half(layer, "ffn", f + 1)

            def steps_before(layer, part, n, evacuate=lambda tok: None):
                evacuate(1)
                split(n, which=(0, 1))
                quarter_hi(layer, part, 0)
                quarter_hi(layer, part, 1)
                split(n, which=(2, 3))

            def mixer_b(layer):
                n, norm = cnt.n[layer, "mix"], 3 * layer

                def y_rows(j, tok):
                    act.wait_ge(blk, 2 * (n + j) + tok + 1)
                    nc.scalar.activation(y[:, tok, j * 512:(j + 1) * 512], acc[j][tok][:, :], ACT.Copy,
                                         scale=rinv[:, 2 * norm + tok:2 * norm + tok + 1]).then_inc(y_out, 1)

                late_half(layer, "mix", n + 1)
                act.wait_ge(r_done, r_index(norm, 1))
                y_rows(0, 0)
                y_rows(0, 1)
                split(n + 2)
                y_rows(1, 0)
                y_rows(1, 1)
                for u in range(4):
                    act.wait_ge(z_done, u + 1)
                    nc.scalar.copy(z_hi[:, 2 * u:2 * u + 2, :].rearrange("p c x -> p (c x)"), sbank[u % 2][:, :]
                                   ).then_inc(z_hi_done, 1)
                    split(n + 3, which=(u,))
                for g in range(4):
                    act.wait_ge(*((blk, 2 * (n + 2) + g // 2 + 1) if g % 2 else (z_done, 5 + g // 2)))
                    for eh in range(2):
                        k = 2 * g + eh
                        last = nc.scalar.activation(u_hi[:, k, :], sbank[g % 2][:, eh * SEQ:(eh + 1) * SEQ], ACT.Copy,
                                                    scale=cols[:, BSCALE + k:BSCALE + k + 1])
                    last.then_inc(z_hi_done, 1)
                split(n + 4)
                steps_before(layer, "ffn", n + 5)
                late_half(layer, "ffn", n + 6)

            def mixer_c(layer):
                n, norm, t0 = cnt.n[layer, "mix"], 3 * layer, cnt.t[layer, "mix"]

                def gelu_rows(s, tok):
                    act.wait_ge(blk, 2 * (n + s) + tok + 1)
                    dst = (gv, gu)[s // 2][:, tok, (s % 2) * 512:(s % 2 + 1) * 512]
                    nc.scalar.activation(dst, acc[s % 2][tok][:, :], ACT.Gelu_apprx_tanh,
                                         scale=rinv[:, 2 * norm + tok:2 * norm + tok + 1]).then_inc(y_out, 1)

                late_half(layer, "mix", n + 1)
                act.wait_ge(r_done, r_index(norm, 1))
                for s in range(4):
                    gelu_rows(s, 0)
                    gelu_rows(s, 1)
                    if s < 3:
                        split(n + 2 + s)
                for q in range(4):
                    act.wait_ge(t_done, t0 + 1 + q + 1)
                    nc.scalar.copy(quarter_view(c_hi, q % 2, q // 2), four(tbank[(t0 + 1 + q) % 2][:, :])).then_inc(t_hi, 1)
                split(n + 5)
                steps_before(layer, "ffn", n + 6)
                late_half(layer, "ffn", n + 7)

            def ffn(layer):
                n, t0, hid0, norm = cnt.n[layer, "ffn"], cnt.t[layer, "ffn"], cnt.hid[layer, "ffn"], 3 * layer + 1

                def silu(b, s, tok, i=None):
                    act.wait_ge(blk, at(2 * (n + b) + tok + 1, i, 4))
                    if b:
                        act.wait_ge(hid_done, at(hid0 + 2 * (b - 1) + tok + 1, i, 4))
                    nc.scalar.activation(gated[:, tok, 0:SEQ], acc[s][tok][:, 0:SEQ], ACT.Silu,
                                         scale=rinv[:, 2 * norm + tok:2 * norm + tok + 1]).then_inc(gate_done, 1)

                def hidden_hi(b, bank_, i=None):
                    act.wait_ge(t_done, at(t0 + b + 1, i, 2))
                    k0 = 2 * b if i is None else i * 4 + 2 * b
                    nc.scalar.copy(hid_hi[:, bass.ds(k0, 2), :], tbank[bank_][:, :].rearrange("p (c x) -> p c x", c=2)
                                   ).then_inc(t_hi, 1)

                act.wait_ge(r_done, r_index(norm, 1))
                silu(0, 0, 0)
                with act.Fori(0, (HB - 1) // 2, 1) as i:
                    for s in range(2):
                        silu(s, s, 1, i)
                        split(n + 2 + s, i, 2)
                        hidden_hi(s, (t0 + s) % 2, i)
                        silu(s + 1, (s + 1) % 2, 0, i)
                silu(HB - 1, 0, 1)
                d = cnt.n[layer, "down"]
                split(d + 1)
                hidden_hi(HB - 1, (t0 + HB - 1) % 2)
                split(d + 2)
                split(d + 3)
                steps_before(layer, "ple", d + 4)
                split(d + 5, which=(0, 1))
                td = cnt.t[layer, "down"]
                act.wait_ge(t_done, td + 3)
                nc.scalar.copy(p_hi[:, :, :].rearrange("p k x -> p (k x)"), tbank[(td + 2) % 2][:, :]).then_inc(t_hi, 1)
                split(d + 5, which=(2, 3))
                g = cnt.n[layer, "ple"]
                split(g)
                late_half(layer, "ple", g + 1)
                norm += 1

                def tanh(j, tok):
                    act.wait_ge(blk, 2 * (g + 1 + j) + tok + 1)
                    if j:
                        act.wait_ge(h_done, cnt.h[layer, "ple"] + tok + 1)
                    nc.scalar.activation(gated[:, tok, :], sbank[tok][:, :], ACT.Tanh,
                                         scale=half_r[:, tok:tok + 1]).then_inc(gate_done, 1)

                act.wait_ge(r_done, r_index(norm, 1))
                split(g + 2)
                tanh(0, 0)
                if layer < last_layer:
                    steps_before(layer + 1, "mix", g + 3, lambda tok: tanh(0, tok))
                else:
                    tanh(0, 1)
                tanh(1, 0)
                tanh(1, 1)

            split(0)
            quarter_hi(0, "mix", 0)
            quarter_hi(0, "mix", 1)
            pair = 0
            for layer, kind in enumerate(MIXERS):
                if kind == 0:
                    mixer_a(layer, pair)
                    pair += PAIRS
                elif kind == 1:
                    mixer_b(layer)
                else:
                    mixer_c(layer)
                ffn(layer)
            h0 = cnt.h[last_layer, "ple"]
            sum_squares(12, 0, h0 + 3)
            sum_squares(12, 1, h0 + 4)

        @block.vector
        def _(dve):
            TT, TS, STT = nc.vector.tensor_tensor, nc.vector.tensor_scalar, nc.vector.scalar_tensor_tensor

            def split(n, i=None, m=0, which=range(4)):
                for s in which:
                    dve.wait_ge(hi_done, at(4 * n + s + 1, i, 4 * m))
                    src, (hi, lo) = panel_quarter(n, s)
                    TT(lo, src, hi.bitcast(F32), ALU.subtract).then_inc(lo_done, 1)

            def quarter_scale(layer, part, q):
                order, uses, _ = quarters(layer, part)
                (tok, j), t = order[q], uses[q]
                c0 = gain_col(norm_of(layer, part), 4 * j)
                gains = bass.AP(tensor=cols[:, :].tensor, offset=c0, ap=[[13 * KT + 4, P], [1, 4], [0, P]])
                before = cnt.x[layer, part] - 4 + q - 1
                if before >= 1:
                    dve.wait_ge(x_done, before)
                dve.wait_ge(t_done, t + 1)
                TT(four(xf[:, q % 2, :]), four(tbank[t % 2][:, :]), gains, ALU.mult).then_inc(t_free, 1)

            def quarter_lo(layer, part, q):
                tok, j = quarters(layer, part)[0][q]
                par = norm_of(layer, part) % 2
                dve.wait_ge(t_hi, hi_index(layer, part, q))
                TT(quarter_view(x_lo[:, par], tok, j), four(xf[:, q % 2, :]),
                   quarter_view(x_hi[:, par], tok, j).bitcast(F32), ALU.subtract).then_inc(x_done, 1)

            def late_half(layer, part, n, update):
                quarter_scale(layer, part, 2)
                update(1, 1)
                split(n, which=(0,))
                quarter_lo(layer, part, 2)
                split(n, which=(1,))
                quarter_scale(layer, part, 3)
                split(n, which=(2,))
                quarter_lo(layer, part, 3)
                split(n, which=(3,))

            def steps_before(layer, part, n, update):
                update(1, 0)
                split(n, which=(0, 1))
                quarter_scale(layer, part, 0)
                quarter_scale(layer, part, 1)
                quarter_lo(layer, part, 0)
                quarter_lo(layer, part, 1)
                split(n, which=(2, 3))
                update(0, 1)

            def add_product(n, tok, j):
                dve.wait_ge(blk, 2 * n + tok + 1)
                hj = h[:, tok, j * 512:(j + 1) * 512]
                TT(hj, acc[j][tok][:, :], hj, ALU.add).then_inc(h_done, 1)

            def biased_scores(u, pair):
                qt, hd = u // 2, u % 2
                dve.wait_ge(s_done, 4 * pair + u + 1)
                if u == 0:
                    dve.wait_ge(bias_in, 32 * pair + 32)
                if pair or qt:
                    dve.wait_ge(et_done, 4 * pair + 2 * qt)
                if qt == 0:
                    parts = [(sbank[hd][:, 0:QW].rearrange("p (g x) -> p g x", g=GROUPS), bias[:, hd, :, P:SEQ],
                              e[:, hd, 0:QW].rearrange("p (g x) -> p g x", g=GROUPS))]
                else:
                    parts = [(sbank[0][:, :], bias[:, hd, 0:2, :].rearrange("p g x -> p (g x)"), e[:, hd, 0:512]),
                             (sbank[1][:, 0:SEQ], bias[:, hd, 2, :], e[:, hd, 512:2 * QW])]
                for b, (s_, b_, e_) in enumerate(parts):
                    nc.vector.tensor_tensor_reduce(out=e_, in0=s_, in1=b_, scale=1.0, scalar=-3e38, op0=ALU.add,
                                                   op1=ALU.max, accum_out=tops[:, u, b:b + 1]).then_inc(max_done, 1)
                dve.wait_ge(max_done, 6 * pair + (1, 2, 4, 6)[u])
                TS(neg_top[:, u:u + 1], tops[:, u, 0:1], tops[:, u, qt:qt + 1], -1.0, ALU.max, ALU.mult).then_inc(top_done, 1)

            def normalised(qt, pair):
                dve.wait_ge(pv_done, 2 * pair + qt + 1)
                nc.vector.reciprocal(rden[:, 2 * qt:2 * qt + 2], den[:, 2 * qt:2 * qt + 2]).then_inc(rden_done, 1)
                dve.wait_ge(rden_done, 2 * pair + qt + 1)
                for hd in range(2):
                    last = TS(o[:, qt, hd * DH:(hd + 1) * DH], pv_bank[:, hd * DH:(hd + 1) * DH],
                              rden[:, 2 * qt + hd:2 * qt + hd + 1], None, ALU.mult)
                last.then_inc(o_done, 1)

            def out_lo(tok, r, pair):
                dve.wait_ge(ot_hi, 2 * pair + tok + 1)
                TT(o_lo[:, r, tok * P:(tok + 1) * P], pv_bank[:, 0:P], o_hi[:, r, tok * P:(tok + 1) * P].bitcast(F32),
                   ALU.subtract).then_inc(ot_lo, 1)

            def mixer_a(layer, pair, update):
                late_half(layer, "mix", cnt.n[layer, "mix"] + 1, update)
                if layer == 0:
                    for g in range(GROUPS):
                        dve.wait_ge(t_done, 5 + g + 1)
                        nc.vector.tensor_copy(offsets[:, g, :], tbank[(5 + g) % 2][0:HEADS, 0:SKEW]).then_inc(t_free, 1)
                for r in range(PAIRS):
                    n, this, prev = cnt.n[layer, "mix"] + 3 * r, pair + r, pair + r - 1
                    if r:
                        split(n + 1, which=(0,))
                        biased_scores(2, prev)
                        split(n + 1, which=(1,))
                        normalised(0, prev)
                        biased_scores(3, prev)
                        split(n + 1, which=(2,))
                        out_lo(0, r - 1, prev)
                        split(n + 1, which=(3,))
                    split(n + 2, which=(0, 1))
                    if r:
                        normalised(1, prev)
                    split(n + 2, which=(2, 3))
                    if r:
                        out_lo(1, r - 1, prev)
                    split(n + 3, which=(0, 1, 2))
                    biased_scores(0, this)
                    biased_scores(1, this)
                    split(n + 3, which=(3,))
                w, f, last_pair = n + 3, n + 4, this
                split(f, which=(0,))
                biased_scores(2, last_pair)
                split(f, which=(1,))
                biased_scores(3, last_pair)
                normalised(0, last_pair)
                out_lo(0, PAIRS - 1, last_pair)
                add_product(w, 0, 0)
                normalised(1, last_pair)
                add_product(w, 0, 1)
                quarter_scale(layer, "ffn", 0)
                split(f, which=(2,))
                quarter_scale(layer, "ffn", 1)
                quarter_lo(layer, "ffn", 0)
                out_lo(1, PAIRS - 1, last_pair)
                quarter_lo(layer, "ffn", 1)
                split(f, which=(3,))
                add_product(w, 1, 0)
                add_product(w, 1, 1)
                late_half(layer, "ffn", f + 1, lambda tok, j: None)

            def mixer_b(layer, update):
                n = cnt.n[layer, "mix"]
                late_half(layer, "mix", n + 1, update)
                split(n + 2)
                for u in range(4):
                    dve.wait_ge(z_hi_done, u + 1)
                    TT(z_lo[:, 2 * u:2 * u + 2, :].rearrange("p c x -> p (c x)"), sbank[u % 2][:, :],
                       z_hi[:, 2 * u:2 * u + 2, :].rearrange("p c x -> p (c x)").bitcast(F32), ALU.subtract
                       ).then_inc(z_lo_done, 1)
                    split(n + 3, which=(u,))
                for g in range(4):
                    dve.wait_ge(z_hi_done, 5 + g)
                    for eh in range(2):
                        k = 2 * g + eh
                        last = STT(u_lo[:, k, :], sbank[g % 2][:, eh * SEQ:(eh + 1) * SEQ], cols[:, BSCALE + k:BSCALE + k + 1],
                                   u_hi[:, k, :].bitcast(F32), ALU.mult, ALU.subtract)
                    last.then_inc(z_lo_done, 1)
                split(n + 4)
                add_product(n + 3, 0, 0)
                steps_before(layer, "ffn", n + 5, lambda tok, j: add_product(n + 3 + j, tok, j))
                late_half(layer, "ffn", n + 6, lambda tok, j: add_product(n + 3 + j, tok, j))

            def mixer_c(layer, update):
                n, t0 = cnt.n[layer, "mix"], cnt.t[layer, "mix"]
                y0, hi0 = 4, cnt.hi[layer, "mix"]
                late_half(layer, "mix", n + 1, update)
                dve.wait_ge(part_in, 64)
                tril4 = bass.AP(tensor=tril[:, :].tensor, offset=0, ap=[[P, P], [0, 4], [1, P]])
                TT(w_s[:, :, :], w_s[:, :, :], tril4, ALU.mult).then_inc(masked, 1)
                split(n + 2)
                split(n + 3)
                step = 0
                for tok in range(2):
                    dve.wait_ge(y_out, y0 + 2 + tok + 1)
                    for j in range(2):
                        nc.vector.bn_stats(stats[:, tok, j, :], gv[:, tok, j * 512:(j + 1) * 512]).then_inc(dve_step, 1)
                    step += 2
                    dve.wait_ge(dve_step, step)
                    nc.vector.bn_aggr(mv[:, tok, :], stats[:, tok, :, :]).then_inc(ln_stat, 1)
                dve.wait_ge(t_done, t0 + 1)
                nc.vector.tensor_copy(w_st[:, :, :].rearrange("p g x -> p (g x)"), tbank[t0 % 2][:, :]).then_inc(t_free, 1)
                for tok in range(2):
                    dve.wait_ge(ln_stat, tok + 1)
                    dve.wait_ge(r_done, 2 * 7 + tok + 1)
                    TS(gv[:, tok, :], gv[:, tok, :], mv[:, tok, 0:1], rinv[:, 26 + tok:27 + tok],
                       ALU.subtract, ALU.mult).then_inc(dve_step, 1)
                    step += 1
                    dve.wait_ge(dve_step, step)
                    TT(gv[:, tok, :], gv[:, tok, :], gain_v[:, :], ALU.mult).then_inc(v_done, 1)
                split(n + 4)
                for half_ in range(2):
                    for q in (2 * half_, 2 * half_ + 1):
                        tok, j = q % 2, q // 2
                        dve.wait_ge(sp_done, q + 1)
                        dve.wait_ge(y_out, y0 + 4 + q + 1)
                        for s in range(2):
                            g = 2 * j + s
                            gu_ = gu[:, tok, g * SEQ:(g + 1) * SEQ]
                            last = STT(gu_, sbank[tok][:, s * SEQ:(s + 1) * SEQ], cols[:, BSP + g:BSP + g + 1], gu_,
                                       ALU.add, ALU.mult)
                        last.then_inc(gate_out, 1)
                    for q in (2 * half_, 2 * half_ + 1):
                        tok, j = q % 2, q // 2
                        dve.wait_ge(t_hi, hi0 + q + 1)
                        TT(quarter_view(c_lo, tok, j), four(tbank[(t0 + 1 + q) % 2][:, :]),
                           quarter_view(c_hi, tok, j).bitcast(F32), ALU.subtract).then_inc(t_free, 1)
                split(n + 5)
                add_product(n + 4, 0, 0)
                steps_before(layer, "ffn", n + 6, lambda tok, j: add_product(n + 4 + j, tok, j))
                late_half(layer, "ffn", n + 7, lambda tok, j: add_product(n + 4 + j, tok, j))

            def ffn(layer):
                n, t0, norm = cnt.n[layer, "ffn"], cnt.t[layer, "ffn"], 3 * layer + 1
                hi0, g0 = cnt.hi[layer, "ffn"], 26 * layer

                def hidden(b, s, tok, i=None):
                    dve.wait_ge(gate_done, at(g0 + 2 * b + tok + 1, i, 4))
                    STT(prod[:, tok, 0:SEQ], acc[s][tok][:, SEQ:512], rinv[:, 2 * norm + tok:2 * norm + tok + 1],
                        gated[:, tok, 0:SEQ], ALU.mult, ALU.mult).then_inc(hid_done, 1)

                def hidden_lo(b, bank_, i=None):
                    dve.wait_ge(t_hi, at(hi0 + b + 1, i, 2))
                    k0 = 2 * b if i is None else i * 4 + 2 * b
                    TT(hid_lo[:, bass.ds(k0, 2), :], tbank[bank_][:, :].rearrange("p (c x) -> p c x", c=2),
                       hid_hi[:, bass.ds(k0, 2), :].bitcast(F32), ALU.subtract).then_inc(t_free, 1)

                hidden(0, 0, 0)
                with dve.Fori(0, (HB - 1) // 2, 1) as i:
                    for s in range(2):
                        hidden(s, s, 1, i)
                        split(n + 2 + s, i, 2)
                        hidden_lo(s, (t0 + s) % 2, i)
                        hidden(s + 1, (s + 1) % 2, 0, i)
                hidden(HB - 1, 0, 1)
                d = cnt.n[layer, "down"]
                split(d + 1)
                hidden_lo(HB - 1, (t0 + HB - 1) % 2)
                split(d + 2)
                split(d + 3)
                add_product(d + 2, 0, 0)

                def down(tok, j):
                    add_product(d + 2 + 3 * j, tok, j)

                update_none = lambda tok, j: down(tok, j) if (tok, j) == (1, 0) else None
                steps_before(layer, "ple", d + 4, update_none)
                split(d + 5, which=(0, 1))
                td = cnt.t[layer, "down"]
                dve.wait_ge(t_hi, cnt.hi[layer, "down"] + 3)
                TT(p_lo[:, :, :].rearrange("p k x -> p (k x)"), tbank[(td + 2) % 2][:, :],
                   p_hi[:, :, :].rearrange("p k x -> p (k x)").bitcast(F32), ALU.subtract).then_inc(t_free, 1)
                split(d + 5, which=(2, 3))
                g = cnt.n[layer, "ple"]
                split(g)
                down(0, 1)
                late_half(layer, "ple", g + 1, down)

                def embed(tok, j):
                    dve.wait_ge(gate_done, g0 + 2 * HB + 2 * j + tok + 1)
                    STT(prod[:, tok, :], gated[:, tok, :], 1.0, acc[j][tok][:, :], ALU.add, ALU.mult).then_inc(embed_step, 1)
                    dve.wait_ge(embed_step, 4 * layer + 2 * j + tok + 1)
                    hj = h[:, tok, j * 512:(j + 1) * 512]
                    STT(hj, prod[:, tok, :], 0.5, hj, ALU.mult, ALU.add).then_inc(h_done, 1)

                split(g + 2)
                embed(0, 0)
                if layer < last_layer:
                    steps_before(layer + 1, "mix", g + 3, embed)
                else:
                    embed(1, 0)
                    embed(0, 1)
                return embed

            dve.wait_ge(x_in, 16)
            dve.sem_inc(h_done, 4)
            dve.sem_inc(hid_done, 2)
            nc.vector.memset(expo[:, :], -0.5).then_inc(expo_set, 1)
            nc.vector.memset(table[32:33, :], 1.0).then_inc(table_one, 1)
            dve.wait_ge(t_done, 1)
            nc.vector.tensor_copy(cols[:, :], tbank[0][:, 0:13 * KT + 4]).then_inc(t_free, 1)
            dve.wait_ge(t_free, 1)
            quarter_scale(0, "mix", 0)
            quarter_scale(0, "mix", 1)
            split(0)
            quarter_lo(0, "mix", 0)
            quarter_lo(0, "mix", 1)
            update = lambda tok, j: None
            pair = 0
            for layer, kind in enumerate(MIXERS):
                if kind == 0:
                    mixer_a(layer, pair, update)
                    pair += PAIRS
                elif kind == 1:
                    mixer_b(layer, update)
                else:
                    mixer_c(layer, update)
                update = ffn(layer)
            update(1, 1)
            dve.wait_ge(part_in, 80)
            for tok in range(2):
                dve.wait_ge(r_done, r_index(12, tok))
                STT(result[:, tok, :], h[:, tok, :], rinv[:, 24 + tok:25 + tok], gain_f[:, :],
                    ALU.mult, ALU.mult).then_inc(result_done, 1)

        @block.gpsimd
        def _(pool):
            steps = [0]

            def chained(ins):
                steps[0] += 1
                ins.then_inc(r_step, 1)
                pool.wait_ge(r_step, steps[0])

            def inverse_root(col, src, scale):
                m = mean_sq[:, col:col + 1]
                chained(nc.gpsimd.tensor_scalar(m, src, scale, EPS, ALU.mult, ALU.add))
                return nc.gpsimd.tensor_tensor(rinv[:, col:col + 1], m, expo[:, :], ALU.pow)

            def inverse_rms(norm):
                for tok in range(2):
                    col = 2 * norm + tok
                    pool.wait_ge(ssq_done, col + 1)
                    ins = inverse_root(col, ssq[:, col:col + 1], 1.0 / D)
                    scaled, by = {0: (rinv8, 1 / 8), 2: (half_r, 0.5)}.get(norm % 3, (None, None))
                    if norm < 12 and scaled is not None:
                        chained(ins)
                        ins = nc.gpsimd.tensor_scalar(scaled[:, tok:tok + 1], rinv[:, col:col + 1], by, None, ALU.mult)
                    ins.then_inc(r_done, 1)

            skewed = bass.AP(tensor=bias_skew.tensor, offset=P - 1,
                             ap=[[2 * P * SKEW, PAIRS], [P * SKEW, 2], [SKEW - 1, P], [HEADS * P * SKEW, GROUPS], [1, SEQ]])

            def load_bias(pair, i=None):
                for hd in range(2):
                    pool.dma_start(bias[:, hd, :, :], skewed[pair if i is None else i + pair, hd]).then_inc(bias_in, 16)

            pool.wait_ge(expo_set, 1)
            done = 0
            for layer, kind in enumerate(MIXERS):
                if layer == 0:
                    inverse_rms(0)
                    pool.wait_ge(t_free, 8)
                    pool.dma_start(bias_rows.rearrange("(g n) u -> n g u", g=GROUPS), offsets).then_inc(rows_out, 16)
                    pool.wait_ge(rows_out, 16)
                    pool.dma_start(bias_skew, bass.AP(tensor=bias_rows.tensor, offset=0,
                                                      ap=[[SKEW, GROUPS * HEADS], [0, P], [1, SKEW]])).then_inc(rows_out, 16)
                    pool.wait_ge(rows_out, 32)
                else:
                    inverse_rms(3 * layer)
                if kind == 0:
                    load_bias(0)
                    with pool.Fori(0, PAIRS - 1, 1) as i:
                        pool.wait_ge(top_done, at(4 * done + 4, i, 4))
                        load_bias(1, i)
                    done += PAIRS
                if kind == 2:
                    for tok in range(2):
                        pool.wait_ge(ln_stat, tok + 1)
                        inverse_root(26 + tok, mv[:, tok, 1:2], 1.0).then_inc(r_done, 1)
                inverse_rms(3 * layer + 1)
                inverse_rms(3 * layer + 2)
            inverse_rms(12)


_INS = ["x", "p", "rel_table", "norm_mix", "norm_ffn", "norm_ple", "final_norm", "a_w_qkv", "a_w_o",
        "b_w_in", "b_w_grp", "b_scale", "b_w_out", "c_w_in", "c_v_gain", "c_w_s", "c_b_s", "c_w_out",
        "ffn_w_gate", "ffn_w_up", "ffn_w_down", "ple_w_gate", "ple_w_proj"]
_CONSTS = ["identity", "bucket_of", "pool_of", "lower"]
_OUTS = [((1, SEQ, D), "float32")]


def constants():
    f32 = np.float32
    bucket_of = np.zeros((33, GROUPS, SKEW), f32)
    for g, d in enumerate((1, 4, 16)):
        n = SEQ - 1 - np.arange(SKEW)
        near = np.maximum(n, 1).astype(f32)
        large = 16 + (np.log(near / 16) / np.log(2048 / 16) * 16).astype(np.int32)
        bucket = np.where(n < 16, n, np.minimum(large, 31))
        seen = (n >= 0) & (n % d == 0) & (n <= 128 * d)
        bucket_of[bucket[seen], g, np.flatnonzero(seen)] = 1.0
        bucket_of[32, g, ~seen] = NEG
    full = np.zeros((4, SEQ, SEQ), f32)
    for g, win in enumerate((2, 4, 8, 16)):
        for s in range(SEQ):
            full[g, max(0, s - win + 1):s + 1, s] = f32(1.0) / f32(min(s + 1, win))
            full[g, s, s] -= f32(1.0)
    pool_of = np.concatenate([full[:, :P, :], full[:, P:, P:]], axis=2).transpose(1, 0, 2)
    return {"identity": np.eye(P, dtype=f32), "bucket_of": bucket_of,
            "pool_of": np.ascontiguousarray(pool_of), "lower": np.tril(np.ones((P, P), f32))}


def kernel(**inputs):
    import concourse.bacc as _bacc
    from concourse.bass_utils import run_bass_kernel_spmd as _run

    nc = _bacc.Bacc("TRN2", target_bir_lowering=False, num_devices=1)
    const = constants()
    arrays, args = {}, []
    for name in _INS + _CONSTS:
        a = np.ascontiguousarray(inputs[name] if name in _INS else const[name])
        arrays[f"in_{name}_dram"] = a
        args.append(nc.dram_tensor(f"in_{name}_dram", a.shape, mybir.dt.from_np(a.dtype), kind="ExternalInput").ap())
    for i, (shape, dtype) in enumerate(_OUTS):
        args.append(nc.dram_tensor(f"out_{i}_dram", shape, mybir.dt.from_np(np.dtype(dtype)), kind="ExternalOutput").ap())
    trunk(nc, *args)
    r = _run(nc, [arrays], core_ids=[0])
    return r.results[0]["out_0_dram"]
```

```python
from contextlib import ExitStack

import numpy as np

import concourse.bass as bass
from concourse import mybir

F32 = mybir.dt.float32
F32R = mybir.dt.float32r
BF16 = mybir.dt.bfloat16
ALU = mybir.AluOpType
ACT = mybir.ActivationFunctionType

P = 128
SEQ = 256
D = 1024
KT = D // P
DEPTH = 4
GROUPS = 3
HEADS = 8
DH = 64
PAIRS = HEADS // 2
QW = GROUPS * P
HIDDEN = 2816
HB = HIDDEN // SEQ
HKT = HIDDEN // P
PLE = 256
EPS = 1e-6
NEG = -1e30
SKEW = 3 * P
HALF = 4 * 512
MIXERS = [i % 3 for i in range(DEPTH)]

A_PANELS, B_PANELS, C_PANELS = 3 * PAIRS + 1, 5, 6
F_PANELS, D_PANELS, G_PANELS = HB, 6, 3


def at(base, i, step):
    return base if i is None else base + i * step


class Counts:

    def __init__(self):
        n = 0
        t = 8
        hi = 4
        h = 4
        x = 4
        hid = 2
        dmas = []
        half = []
        self.n, self.t, self.hi, self.h, self.x, self.hid = {}, {}, {}, {}, {}, {}
        for layer, kind in enumerate(MIXERS):
            def mark(part):
                key = (layer, part)
                self.n[key], self.t[key], self.hi[key] = n, t, hi
                self.h[key], self.x[key], self.hid[key] = h, x, hid
            mark("mix")
            dmas += ([3] * (3 * PAIRS) + [1], [1] * B_PANELS, [1] * C_PANELS)[kind]
            dmas += [2] * (F_PANELS + 1) + [1] * (D_PANELS - 1 + G_PANELS)
            half += ([4 * QW] * (3 * PAIRS) + [HALF],
                     [HALF, HALF, 4 * SEQ, HALF, HALF], [HALF] * C_PANELS)[kind]
            half += [HALF] * F_PANELS + [HALF, HALF, 3 * 512] * 2 + [D, HALF, HALF]
            n += (A_PANELS, B_PANELS, C_PANELS)[kind]
            t += (4, 4, 9)[kind]
            hi += (4, 4, 8)[kind]
            h += 4
            x += 4
            mark("ffn")
            n += F_PANELS
            t += HB
            hi += HB
            hid += 2 * HB
            mark("down")
            n += D_PANELS
            t += 5
            hi += 5
            h += 4
            x += 4
            mark("ple")
            n += G_PANELS
            h += 4
            if layer < DEPTH - 1:
                t += 4
                hi += 4
                x += 4
        self.panels = n
        self.half = half
        self.landed = [sum(dmas[i % 2:i + 1:2]) for i in range(n)]


def trunk(nc, x, p, rel_table, final_norm, a_w_qkv, a_w_o,
          b_w_in, b_w_grp, b_w_out, c_w_in, c_v_gain, c_w_s, c_w_out, vectors,
          ffn_w_gate, ffn_w_up, ffn_w_down, ple_w_gate, ple_w_proj,
          identity, bucket_of, pool_of, lower, out):
    cnt = Counts()
    last_layer = DEPTH - 1

    with ExitStack() as ctx:
        def sb(name, shape, dt=F32, scope=ctx):
            return scope.enter_context(nc.sbuf_tensor(name, shape, dt))

        def sem(name):
            return ctx.enter_context(nc.semaphore(name))

        raw = sb("raw", [P, 4, HALF])
        w_hi = sb("w_hi", [P, 2, 2 * HALF], F32R)
        w_lo = sb("w_lo", [P, 2, 2 * HALF], F32R)
        x_hi = sb("x_hi", [P, 2, KT, SEQ], F32R)
        x_lo = sb("x_lo", [P, 2, KT, SEQ], F32R)
        h = sb("h", [P, 2, D])
        ident = sb("ident", [P, P])
        rows = sb("rows", [12 * KT + KT + 4, P])
        cols = sb("cols", [P, 12 * KT + KT + 4])
        xf = sb("xf", [P, 2, 512])
        squares = sb("squares", [P, D], BF16)
        ssq = sb("ssq", [P, 26])
        mean_sq = sb("mean_sq", [P, 28])
        rinv = sb("rinv", [P, 28])
        rinv8 = sb("rinv8", [P, 2])
        half_r = sb("half_r", [P, 2])
        expo = sb("expo", [P, 1])
        gated = sb("gated", [P, 2, 512])
        prod = sb("prod", [P, 2, 512])
        v = gated[:, :, :].rearrange("p t x -> p (t x)")[:, 0:2 * QW].rearrange("p (t g x) -> p t g x", t=2, g=GROUPS)
        p_rows = sb("p_rows", [P, 2, PLE])
        p_split = sb("p_split", [P, 2, 2, SEQ], F32R)
        p_hi, p_lo = p_split[:, 0], p_split[:, 1]
        k_lo = p_split[:, :, :, :].rearrange("p s k x -> p (s k x)")[:, 0:GROUPS * SEQ]
        k_lo = k_lo.rearrange("p (g x) -> p g x", g=GROUPS)

        with ExitStack() as part:
            hid_hi = sb("hid_hi", [P, HKT, SEQ], F32R, part)
            hid_lo = sb("hid_lo", [P, HKT, SEQ], F32R, part)
        with ExitStack() as part:
            qk = sb("qk", [P, 2, 2, QW], F32, part)
            q2 = sb("q2", [P, 2, GROUPS, SEQ], F32R, part)
            k2 = sb("k2", [P, 2, GROUPS, SEQ], F32R, part)
            e = sb("e", [P, 2, GROUPS * SEQ], F32, part)
            e_t = sb("e_t", [P, 2, GROUPS * SEQ], F32, part)
            o = sb("o", [P, 2, P], F32, part)
            o_hi = sb("o_hi", [P, PAIRS, SEQ], F32R, part)
            o_lo = sb("o_lo", [P, PAIRS, SEQ], F32R, part)
            bias = sb("bias", [P, 2, GROUPS, SEQ], F32, part)
            tops = sb("tops", [P, 4, 2], F32, part)
            neg_top = sb("neg_top", [P, 4], F32, part)
            den = sb("den", [P, 4], F32, part)
            rden = sb("rden", [P, 4], F32, part)
            table = sb("table", [33, GROUPS * HEADS], F32, part)
            buckets = e[0:33].rearrange("p s x -> p (s x)")[:, 0:GROUPS * SKEW].rearrange("p (g x) -> p g x", g=GROUPS)
            offsets = e_t[0:HEADS].rearrange("p s x -> p (s x)")[:, 0:GROUPS * SKEW].rearrange("p (g x) -> p g x", g=GROUPS)
        with ExitStack() as part:
            y = sb("y", [P, 2, D], F32, part)
            pool_w = sb("pool_w", [P, 4, 3 * P], F32, part)
            z_hi = sb("z_hi", [P, KT, SEQ], F32R, part)
            z_lo = sb("z_lo", [P, KT, SEQ], F32R, part)
            u_hi = sb("u_hi", [P, KT, SEQ], F32R, part)
            u_lo = sb("u_lo", [P, KT, SEQ], F32R, part)
        with ExitStack() as part:
            gv = sb("gv", [P, 2, D], F32, part)
            gu = sb("gu", [P, 2, D], F32, part)
            gain_v = sb("gain_v", [P, D], F32, part)
            w_s = sb("w_s", [P, 4, P], F32, part)
            w_st = sb("w_st", [P, 4, P], F32, part)
            tril = sb("tril", [P, P], F32, part)
            stats = sb("stats", [P, 2, 2, 6], F32, part)
            mv = sb("mv", [P, 2, 2], F32, part)
            c_hi = sb("c_hi", [P, KT, SEQ], F32R, part)
            c_lo = sb("c_lo", [P, KT, SEQ], F32R, part)
        with ExitStack() as part:
            gain_f = sb("gain_f", [P, D], F32, part)
            result = sb("result", [P, 2, D], F32, part)

        def bank(name):
            return ctx.enter_context(nc.psum_tensor(name, [P, 512], F32))

        acc = [[bank(f"acc{j}{t}") for t in range(2)] for j in range(2)]
        tbank = [bank("tbank0"), bank("tbank1")]
        sbank = [bank("sbank0"), bank("sbank1")]
        zbank = sbank + tbank
        qkt_bank, pv_bank = acc[1]

        bias_rows = nc.dram_tensor("bias_rows", (GROUPS * HEADS, SKEW), F32).ap()
        bias_skew = nc.dram_tensor("bias_skew", (GROUPS * HEADS, P, SKEW), F32).ap()

        raw_in = [sem(f"raw_in{i}") for i in range(4)]
        x_in = [sem("x_in0"), sem("x_in1")]
        id_in = sem("id_in")
        rows_in = sem("rows_in")
        table_in = sem("table_in")
        p_in = sem("p_in")
        part_in = sem("part_in")
        bias_in = sem("bias_in")
        out_in = sem("out_in")
        hi_done = sem("hi_done")
        lo_done = sem("lo_done")
        half_used = sem("half_used")
        blk = sem("blk")
        t_done = sem("t_done")
        t_free = sem("t_free")
        t_hi = sem("t_hi")
        h_done = sem("h_done")
        x_done = sem("x_done")
        ssq_done = sem("ssq_done")
        r_step = sem("r_step")
        r_done = sem("r_done")
        expo_set = sem("expo_set")
        gate_done = sem("gate_done")
        hid_done = sem("hid_done")
        dve_step = sem("dve_step")
        qkv_out = sem("qkv_out")
        qkt_done = sem("qkt_done")
        qkt_hi = sem("qkt_hi")
        qkt_out = sem("qkt_out")
        s_done = sem("s_done")
        embed_step = sem("embed_step")
        max_done = sem("max_done")
        rden_done = sem("rden_done")
        top_done = sem("top_done")
        exp_done = sem("exp_done")
        et_done = sem("et_done")
        et_out = sem("et_out")
        pv_done = sem("pv_done")
        o_done = sem("o_done")
        ot_done = sem("ot_done")
        ot_hi = sem("ot_hi")
        ot_lo = sem("ot_lo")
        table_one = sem("table_one")
        y_out = sem("y_out")
        z_done = sem("z_done")
        z_hi_done = sem("z_hi_done")
        z_lo_done = sem("z_lo_done")
        ln_stat = sem("ln_stat")
        v_done = sem("v_done")
        sp_done = sem("sp_done")
        result_done = sem("result_done")
        rows_out = sem("rows_out")
        masked = sem("masked")
        gate_out = sem("gate_out")

        def kt_slice(par, k, kt, width, buf):
            s = (k // (kt // 2)) * HALF + (k % (kt // 2)) * width
            return buf[:, par, s:s + width]

        def quarters(layer, part):
            by_half = [(0, 0), (1, 0), (0, 1), (1, 1)]
            by_tile = [(0, 0), (0, 1), (1, 0), (1, 1)]
            if part == "ffn" and MIXERS[layer] == 0:
                return by_tile, [cnt.t[layer, "mix"] + q for q in range(4)], cnt.h[layer, "ffn"] - 4
            if part == "ffn":
                return by_half, [cnt.t[layer, "ffn"] - 4 + q for q in range(4)], cnt.h[layer, "ffn"] - 4
            if part == "ple":
                t = cnt.t[layer, "down"]
                return by_half, [t, t + 1, t + 3, t + 4], cnt.h[layer, "down"]
            if layer == 0:
                return by_tile, [1, 2, 3, 4], 0
            return by_half, [cnt.t[layer - 1, "ple"] + q for q in range(4)], cnt.h[layer - 1, "ple"]

        def gain_col(i, k):
            return (i % 3) * DEPTH * KT + (i // 3) * KT + k

        BSCALE = 12 * KT
        BSP = 13 * KT

        qkv_src = a_w_qkv.rearrange("a (f k p) (c g n x) -> a c n f g p k x",
                                    f=2, p=P, c=3, g=GROUPS, x=P)
        wo_src = a_w_o.rearrange("a (f n p) x -> a f p n x", f=2, p=P)

        def square(w):
            return w.rearrange("(f k p) (j x) -> j f p k x", f=2, p=P, x=512)

        block = ctx.enter_context(nc.Block())


        @block.sync
        def _(sp):
            def slot_free(n, half, i=None, m=0):
                if n >= 2:
                    sp.wait_ge(lo_done, at(4 * (n - 2) + 2 * half + 2, i, 4 * m))

            def half_slot(n, half, **dims):
                length = 1
                for size in dims.values():
                    length *= size
                names = " ".join(dims)
                return raw[:, 2 * (n % 2) + half, 0:length].rearrange(f"p ({names}) -> p {names}", **dims)

            def load_qkv(n, a, c, pair):
                for f in range(2):
                    slot_free(n, f)
                    for g in range(GROUPS):
                        sp.dma_start(half_slot(n, f, k=4, g=GROUPS, x=P)[:, :, g, :],
                                     qkv_src[a, c, pair, f, g]).then_inc(raw_in[2 * (n % 2) + f], 16)

            def load_wo(n, a):
                for f in range(2):
                    slot_free(n, f)
                    sp.dma_start(half_slot(n, f, k=2, x=D), wo_src[a, f]).then_inc(raw_in[2 * (n % 2) + f], 16)

            def load_square(n, w, j):
                for f in range(2):
                    slot_free(n, f)
                    sp.dma_start(half_slot(n, f, k=4, x=512), square(w)[j, f]).then_inc(raw_in[2 * (n % 2) + f], 16)

            def load_hidden(n, layer, b, i=None):
                for f in range(2):
                    slot_free(n, f, i, 2)
                    dst = half_slot(n, f, k=4, s=2, x=SEQ)
                    for s, w in ((0, ffn_w_gate), (1, ffn_w_up)):
                        src = w[layer].rearrange("(f k p) (b x) -> b f p k x", f=2, p=P, x=SEQ)[b, f]
                        sp.dma_start(dst[:, :, s, :], src).then_inc(raw_in[2 * (n % 2) + f], 16)

            def mixer_a(layer, a):
                n = cnt.n[layer, "mix"]
                for pair in range(PAIRS):
                    for c in range(3):
                        if n or pair or c:
                            load_qkv(n + 3 * pair + c, a, c, pair)
                load_wo(n + 3 * PAIRS, a)

            def mixer_b(layer):
                n = cnt.n[layer, "mix"]
                sp.wait_ge(blk, 2 * cnt.n[layer - 1, "ple"])
                sp.dma_start(pool_w[:, :, :], pool_of).then_inc(part_in, 16)
                for j in range(2):
                    load_square(n + j, b_w_in[0], j)
                for f in range(2):
                    slot_free(n + 2, f)
                    src = b_w_grp[0].rearrange("(f g) (c p) x -> f p (g c) x", f=2, p=P)[f]
                    sp.dma_start(half_slot(n + 2, f, k=4, x=SEQ), src).then_inc(raw_in[2 * (n % 2) + f], 16)
                for j in range(2):
                    load_square(n + 3 + j, b_w_out[0], j)

            def mixer_c(layer):
                n = cnt.n[layer, "mix"]
                for j in (0, 1):
                    load_square(n + j, c_w_in[0], 2 + j)
                sp.wait_ge(blk, 2 * cnt.n[layer - 1, "ple"])
                sp.dma_start(gain_v[:, :], bass.AP(tensor=c_v_gain.tensor, offset=0, ap=[[0, P], [1, D]])
                             ).then_inc(part_in, 16)
                sp.dma_start(w_s[:, :, :], c_w_s[0].rearrange("g t s -> t g s")).then_inc(part_in, 16)
                sp.dma_start(tril[:, :], lower).then_inc(part_in, 16)
                for j in (0, 1):
                    load_square(n + 2 + j, c_w_in[0], j)
                for j in (0, 1):
                    load_square(n + 4 + j, c_w_out[0], j)

            def ffn(layer):
                n = cnt.n[layer, "ffn"]
                load_hidden(n, layer, 0)
                with sp.Fori(0, (HB - 1) // 2, 1) as i:
                    for s in range(2):
                        load_hidden(n + 1 + s, layer, i * 2 + (s + 1), i)
                n = cnt.n[layer, "down"]
                w = ffn_w_down[layer].rearrange("(k p) (j x) -> j p k x", p=P, x=512)
                for j in range(2):
                    for t, (k0, kh) in enumerate(((0, 4), (8, 4), (16, 3))):
                        for f in range(2):
                            slot_free(n, f)
                            for k1, k2 in ((0, 2), (2, 4)) if (j, t) == (0, 0) else ((0, kh),):
                                sp.dma_start(half_slot(n, f, k=kh, x=512)[:, k1:k2, :],
                                             w[j][:, k0 + f * kh + k1:k0 + f * kh + k2, :]
                                             ).then_inc(raw_in[2 * (n % 2) + f], 16)
                        n += 1
                    if j == 0:
                        sp.dma_start(p_rows[:, :, :], p[layer, 0].rearrange("(t p) d -> p t d", p=P)).then_inc(p_in, 16)
                n = cnt.n[layer, "ple"]
                for f in range(2):
                    slot_free(n, f)
                    sp.dma_start(half_slot(n, f, k=1, x=D)[:, 0, :], ple_w_proj[layer][f * P:(f + 1) * P, :]
                                 ).then_inc(raw_in[2 * (n % 2) + f], 16)
                for j in range(2):
                    load_square(n + 1 + j, ple_w_gate[layer], j)

            sp.dma_start(ident[:, :], identity).then_inc(id_in, 16)
            sp.dma_start(rows[:, :], vectors).then_inc(rows_in, 16)
            sp.dma_start(h[:, 0, :], x[0, 0:P, :]).then_inc(x_in[0], 16)
            load_qkv(0, 0, 0, 0)
            sp.dma_start(h[:, 1, :], x[0, P:SEQ, :]).then_inc(x_in[1], 16)
            sp.dma_start(table[0:32, :], rel_table).then_inc(table_in, 16)
            sp.dma_start(buckets, bucket_of).then_inc(table_in, 16)
            for layer, kind in enumerate(MIXERS):
                if kind == 0:
                    mixer_a(layer, layer // 3)
                elif kind == 1:
                    mixer_b(layer)
                else:
                    mixer_c(layer)
                ffn(layer)
            sp.wait_ge(blk, 2 * cnt.n[last_layer, "ple"])
            sp.dma_start(gain_f[:, :], bass.AP(tensor=final_norm.tensor, offset=0, ap=[[0, P], [1, D]])).then_inc(part_in, 16)
            for q in range(4):
                tok, c = q // 2, slice(q % 2 * 512, (q % 2 + 1) * 512)
                sp.wait_ge(result_done, q + 1)
                sp.dma_start(out[0][tok * P:(tok + 1) * P, c], result[:, tok, c]).then_inc(out_in, 16)
            sp.wait_ge(out_in, 64)

        @block.tensor
        def _(pe):
            def passes(out_, st, st_lo, mv_, mv_lo, start, stop):
                nc.tensor.matmul(out_, st, mv_, start=start, stop=False)
                nc.tensor.matmul(out_, st, mv_lo, start=False, stop=False)
                return nc.tensor.matmul(out_, st_lo, mv_, start=False, stop=stop)

            def xt(norm):
                return x_hi[:, norm % 2], x_lo[:, norm % 2]

            def product(n, tok, kt, width, act, k0, out_, i=None, m=0, waits={}, mid={},
                        start=True, stop=True):
                for k in range(kt):
                    if tok == 0 and k == 0:
                        pe.wait_ge(lo_done, at(4 * n + 2, i, 4 * m))
                    if tok == 0 and k == kt // 2:
                        pe.wait_ge(lo_done, at(4 * n + 4, i, 4 * m))
                    if k in waits:
                        pe.wait_ge(*waits[k])
                    if k in mid:
                        mid[k]()
                    last = passes(out_, act[0][:, k0 + k, tok * P:(tok + 1) * P], act[1][:, k0 + k, tok * P:(tok + 1) * P],
                                  kt_slice(n % 2, k, kt, width, w_hi), kt_slice(n % 2, k, kt, width, w_lo),
                                  start=start and k == 0, stop=stop and k == kt - 1)
                    if tok == 1 and k == kt // 2 - 1:
                        last.then_inc(half_used, 1)
                last.then_inc(blk, 1)

            def quarter(layer, part, q):
                order, uses, h0 = quarters(layer, part)
                (tok, j), t = order[q], uses[q]
                pe.wait_ge(h_done, 2 * tok + 2 if h0 == 0 else h0 + q + 1)
                pe.wait_ge(t_free, t - 1 if t > 1 else 1)
                for c in range(4):
                    last = nc.tensor.transpose(tbank[t % 2][:, c * P:(c + 1) * P],
                                               h[:, tok, (4 * j + c) * P:(4 * j + c + 1) * P], ident[:, :])
                last.then_inc(t_done, 1)

            def early_quarters(layer, part, tok):
                return ({2: lambda: quarter(layer, part, 0), 5: lambda: quarter(layer, part, 1)},
                        {5: lambda: quarter(layer, part, 2)})[tok]

            def x_waits(layer, part, tok):
                order, _, _ = quarters(layer, part)
                x0 = {"mix": cnt.x[layer, "mix"], "ffn": cnt.x[layer, "ffn"], "ple": cnt.x[layer, "ple"]}[part] - 4
                return {4 * j: (x_done, x0 + order.index((tok, j)) + 1) for j in range(2)}

            def scores(u, pair):
                qt, hd = u // 2, u % 2
                if u == 0:
                    pe.wait_ge(qkt_out, 4 * pair + 4)
                if pair or u > 1:
                    pe.wait_ge(top_done, 4 * pair + (0, 0, 2, 3)[u])
                for g in range(GROUPS):
                    dst = sbank[hd][:, g * P:(g + 1) * P] if qt == 0 else sbank[g // 2][:, (g % 2) * SEQ:(g % 2 + 1) * SEQ]
                    keys, queries, rows_ = slice(0, (qt + 1) * P), slice(qt * P, (qt + 1) * P), slice(hd * DH, (hd + 1) * DH)
                    nc.tensor.matmul(dst, q2[:, hd, g, queries], k2[:, hd, g, keys], start=True, stop=False)
                    last = nc.tensor.matmul(dst, q2[rows_, hd, g, queries], k_lo[rows_, g, keys], start=False, stop=True)
                last.then_inc(s_done, 1)

            def exp_transposes(u, pair):
                qt, hd = u // 2, u % 2
                pe.wait_ge(exp_done, 4 * pair + u + 1)
                if qt:
                    pe.wait_ge(et_out, 4 * pair + u)
                for b in range(GROUPS * (qt + 1)):
                    last = nc.tensor.transpose(tbank[b // 4 if qt else hd][:, (b % 4) * P:(b % 4 + 1) * P],
                                               e[:, hd, b * P:(b + 1) * P], ident[:, :])
                last.then_inc(et_done, 1)

            def weighted_values(qt, pair):
                pe.wait_ge(et_out, 4 * pair + 2 * qt + 2)
                pe.wait_ge(qkv_out, 6 * pair + 5 + qt)
                if pair or qt:
                    pe.wait_ge(ot_lo, 2 * pair + qt)
                blocks = [(g, t) for g in range(GROUPS) for t in range(qt + 1)]
                for hd in range(2):
                    for b, (g, t) in enumerate(blocks):
                        last = nc.tensor.matmul(pv_bank[:, hd * DH:(hd + 1) * DH], e_t[:, hd, b * P:(b + 1) * P],
                                                v[:, t, g, hd * DH:(hd + 1) * DH],
                                                start=(b == 0), stop=(b == len(blocks) - 1))
                last.then_inc(pv_done, 1)

            def qk_transposes(c, tok, pair):
                pe.wait_ge(qkv_out, 6 * pair + 2 * c + tok + 1)
                if pair or c or tok:
                    pe.wait_ge(qkt_out, 4 * pair + 2 * c + tok)
                for g in range(GROUPS):
                    last = nc.tensor.transpose(qkt_bank[:, g * P:(g + 1) * P],
                                               qk[:, c, tok, g * P:(g + 1) * P], ident[:, :])
                last.then_inc(qkt_done, 1)

            def out_transpose(tok, pair):
                pe.wait_ge(o_done, 2 * pair + tok + 1)
                nc.tensor.transpose(pv_bank[:, 0:P], o[:, tok, :], ident[:, :]).then_inc(ot_done, 1)

            def wo_product(n, j, tok, pair):
                s = (pair // 2) * HALF + (pair % 2) * D + j * 512
                return passes(acc[j][tok][:, :], o_hi[:, pair, tok * P:(tok + 1) * P], o_lo[:, pair, tok * P:(tok + 1) * P],
                              w_hi[:, n % 2, s:s + 512], w_lo[:, n % 2, s:s + 512], start=pair == 0, stop=pair == PAIRS - 1)

            def mixer_a(layer, pair):
                n, norm = cnt.n[layer, "mix"], 3 * layer
                for r in range(PAIRS):
                    this, prev = pair + r, pair + r - 1

                    def attention(step):
                        if r and step == 0:
                            scores(2, prev)
                            exp_transposes(0, prev)
                            exp_transposes(1, prev)
                        if r and step == 2:
                            weighted_values(0, prev)
                            exp_transposes(2, prev)
                            scores(3, prev)
                        if r and step == 3:
                            out_transpose(0, prev)
                        if r and step == 4:
                            exp_transposes(3, prev)
                        if r and step == 6:
                            weighted_values(1, prev)
                        if r and step == 8:
                            out_transpose(1, prev)
                        steps = (3, 5, 7, 9) if r else (5, 6, 7, 9)
                        if step in steps:
                            c, tok = divmod(steps.index(step), 2)
                            qk_transposes(c, tok, this)
                        if step == 11:
                            scores(0, this)
                            scores(1, this)
                        if (layer, r) == (0, 0) and step in (2, 3, 4):
                            bias_vectors(step - 2)

                    for b in range(6):
                        c, tok = b // 2, b % 2
                        attention(2 * b)
                        if r or c:
                            pe.wait_ge(qkv_out, 6 * this + b - 1)
                        first = r == 0 and c == 0
                        mid = {KT // 2: lambda: attention(2 * b + 1)}
                        if first and tok == 0:
                            if layer == 0:
                                mid[1] = lambda: quarter(layer, "mix", 2)
                            mid[6 if layer else 2] = lambda: quarter(layer, "mix", 3)
                        product(n + 3 * r + c, tok, KT, QW, xt(norm), 0, acc[0][tok][:, 0:QW],
                                waits=x_waits(layer, "mix", tok) if first else {}, mid=mid)

                w, last_pair = n + 3 * PAIRS, pair + PAIRS - 1
                filling = iter([(j, tok, k) for j, tok in ((0, 0), (1, 0), (0, 1)) for k in range(PAIRS - 1)])

                def fill(count):
                    for _ in range(count):
                        wo_product(w, *next(filling))

                scores(2, last_pair)
                exp_transposes(0, last_pair)
                exp_transposes(1, last_pair)
                pe.wait_ge(lo_done, 4 * w + 4)
                pe.wait_ge(ot_lo, 2 * last_pair)
                pe.wait_ge(qkv_out, 6 * last_pair + 5)
                pe.wait_ge(qkt_out, 4 * last_pair + 4)
                fill(3)
                scores(3, last_pair)
                weighted_values(0, last_pair)
                exp_transposes(2, last_pair)
                fill(1)
                out_transpose(0, last_pair)
                fill(2)
                exp_transposes(3, last_pair)
                pe.wait_ge(ot_lo, 2 * last_pair + 1)
                wo_product(w, 0, 0, PAIRS - 1)
                wo_product(w, 1, 0, PAIRS - 1).then_inc(blk, 1)
                weighted_values(1, last_pair)
                quarter(layer, "ffn", 0)
                quarter(layer, "ffn", 1)
                out_transpose(1, last_pair)
                fill(3)
                pe.wait_ge(ot_lo, 2 * last_pair + 2)
                wo_product(w, 0, 1, PAIRS - 1)
                for k in range(PAIRS):
                    last = wo_product(w, 1, 1, k)
                    if k == 1:
                        last.then_inc(half_used, 1)
                last.then_inc(blk, 1)

            def bias_vectors(g):
                t = 5 + g
                if g == 0:
                    pe.wait_ge(table_in, 32)
                    pe.wait_ge(table_one, 1)
                pe.wait_ge(t_free, t - 1)
                nc.tensor.matmul(tbank[t % 2][0:HEADS, 0:SKEW], table[:, g * HEADS:(g + 1) * HEADS],
                                 buckets[:, g, :], start=True, stop=True).then_inc(t_done, 1)

            def mixer_out(layer, n, act, waits):
                for j in range(2):
                    for tok in range(2):
                        product(n + j, tok, KT, 512, act, 0, acc[j][tok][:, :], waits=waits[tok] if j == 0 else {},
                                mid=early_quarters(layer, "ffn", tok) if j else {})

            def mixer_b(layer):
                n, norm = cnt.n[layer, "mix"], 3 * layer
                for j in range(2):
                    for tok in range(2):
                        product(n + j, tok, KT, 512, xt(norm), 0, acc[j][tok][:, :],
                                waits=x_waits(layer, "mix", tok) if j == 0 else {},
                                mid={6: lambda: quarter(layer, "mix", 3)} if j == tok == 0 else {})
                pe.wait_ge(part_in, 16)
                for u in range(4):
                    pe.wait_ge(y_out, 2 if u < 2 else 4)
                    for c in range(2):
                        f = 2 * u + c
                        dst = zbank[u][:, c * SEQ:(c + 1) * SEQ]
                        nc.tensor.matmul(dst, y[:, 0, f * P:(f + 1) * P], pool_w[:, u, 0:SEQ],
                                         start=True, stop=False)
                        last = nc.tensor.matmul(dst[:, P:SEQ], y[:, 1, f * P:(f + 1) * P], pool_w[:, u, SEQ:SEQ + P],
                                                start=False, stop=True)
                    last.then_inc(z_done, 1)
                for g in range(4):
                    pe.wait_ge(lo_done, 4 * (n + 2) + (2 if g < 2 else 4))
                    pe.wait_ge(z_lo_done, g + 1)
                    for eh in range(2):
                        dst = zbank[g][:, eh * SEQ:(eh + 1) * SEQ]
                        for c in range(2):
                            wg_hi, wg_lo = (kt_slice(n % 2, 2 * g + c, KT, SEQ, b)[:, eh * P:(eh + 1) * P] for b in (w_hi, w_lo))
                            last = passes(dst, wg_hi, wg_lo, z_hi[:, 2 * g + c, :], z_lo[:, 2 * g + c, :],
                                          start=c == 0, stop=c == 1)
                            if (g, eh, c) == (2, 0, 0):
                                last.then_inc(half_used, 1)
                    last.then_inc(blk if g % 2 else z_done, 1)
                by_group = {2 * g: (z_lo_done, 5 + g) for g in range(4)}
                mixer_out(layer, n + 3, (u_hi, u_lo), [by_group, by_group])

            def mixer_c(layer):
                n, t0, norm = cnt.n[layer, "mix"], cnt.t[layer, "mix"], 3 * layer
                y0 = 4

                def block_in(s, tok):
                    if s >= 2:
                        pe.wait_ge(y_out, y0 + 2 * (s - 2) + tok + 1)
                    product(n + s, tok, KT, 512, xt(norm), 0, acc[s % 2][tok][:, :],
                            waits=x_waits(layer, "mix", tok) if s == 0 else {},
                            mid={6: lambda: quarter(layer, "mix", 3)} if s == tok == 0 else {})

                def spatial(j, tok):
                    pe.wait_ge(v_done, tok + 1)
                    if j:
                        pe.wait_ge(gate_out, tok + 1)
                    for s in range(2):
                        g = 2 * j + s
                        last = nc.tensor.matmul(sbank[tok][:, s * SEQ:(s + 1) * SEQ], w_st[:, g, :],
                                                gv[:, tok, g * SEQ:(g + 1) * SEQ], start=True, stop=True)
                    last.then_inc(sp_done, 1)

                def gated_quarter(q):
                    tok, j = q % 2, q // 2
                    t = t0 + 1 + q
                    pe.wait_ge(gate_out, q + 1)
                    pe.wait_ge(t_free, t - 1)
                    for c in range(4):
                        last = nc.tensor.transpose(tbank[t % 2][:, c * P:(c + 1) * P],
                                                   gu[:, tok, (4 * j + c) * P:(4 * j + c + 1) * P], ident[:, :])
                    last.then_inc(t_done, 1)

                for s in range(3):
                    for tok in range(2):
                        block_in(s, tok)
                pe.wait_ge(masked, 1)
                pe.wait_ge(t_free, t0 - 1)
                for g in range(4):
                    last = nc.tensor.transpose(tbank[t0 % 2][:, g * P:(g + 1) * P], w_s[:, g, :], ident[:, :])
                last.then_inc(t_done, 1)
                block_in(3, 0)
                pe.wait_ge(t_free, t0 + 1)
                spatial(0, 0)
                spatial(0, 1)
                block_in(3, 1)
                gated_quarter(0)
                gated_quarter(1)
                spatial(1, 0)
                spatial(1, 1)
                gated_quarter(2)
                gated_quarter(3)
                mixer_out(layer, n + 4, (c_hi, c_lo),
                          [{4 * j: (t_free, t0 + 1 + 2 * j + tok + 1) for j in range(2)} for tok in range(2)])

            def ffn(layer):
                n, t0, hid0, norm = cnt.n[layer, "ffn"], cnt.t[layer, "ffn"], cnt.hid[layer, "ffn"], 3 * layer + 1

                def hidden_transposes(b, bank_, i=None):
                    pe.wait_ge(hid_done, at(hid0 + 2 * b + 2, i, 4))
                    pe.wait_ge(t_free, at(t0 + b - 1, i, 2))
                    for c in range(2):
                        for tok in range(2):
                            last = nc.tensor.transpose(tbank[bank_][:, (2 * c + tok) * P:(2 * c + tok + 1) * P],
                                                       prod[:, tok, c * P:(c + 1) * P], ident[:, :])
                    last.then_inc(t_done, 1)

                late = {6: lambda: quarter(layer, "ffn", 3)}
                if MIXERS[layer] == 0:
                    late[2] = lambda: quarter(layer, "ffn", 2)
                for tok in range(2):
                    product(n, tok, KT, 512, xt(norm), 0, acc[0][tok][:, :], waits=x_waits(layer, "ffn", tok),
                            mid={} if tok else late)
                with pe.Fori(0, (HB - 1) // 2, 1) as i:
                    for s in range(2):
                        for tok in range(2):
                            pe.wait_ge(hid_done, at(hid0 + 2 * (s - 1) + tok + 1, i, 4))
                            product(n + 1 + s, tok, KT, 512, xt(norm), 0, acc[(1 + s) % 2][tok][:, :], i, 2)
                            if tok == 0:
                                hidden_transposes(s, (t0 + s) % 2, i)

                n, hb, td = cnt.n[layer, "down"], cnt.h[layer, "down"], cnt.t[layer, "down"]
                for j in range(2):
                    for s, (k0, kt) in enumerate(((0, 8), (8, 8), (16, 6))):
                        for tok in range(2):
                            if (j, s) == (0, 0):
                                pe.wait_ge(hid_done, hid0 + 2 * (HB - 1) + tok + 1)
                            if (j, s, tok) == (0, 2, 0):
                                pe.wait_ge(t_free, t0 + HB)
                            product(n, tok, kt, 512, (hid_hi, hid_lo), k0, acc[j][tok][:, :], start=s == 0, stop=s == 2,
                                    mid={3: lambda: quarter(layer, "ple", 2)} if (j, s, tok) == (1, 2, 1) else {})
                            if (j, s, tok) == (0, 0, 0):
                                hidden_transposes(HB - 1, (t0 + HB - 1) % 2)
                            if (j, s, tok) == (1, 0, 0):
                                quarter(layer, "ple", 0)
                                quarter(layer, "ple", 1)
                            if (j, s, tok) == (1, 1, 0):
                                pe.wait_ge(p_in, 16 * (layer + 1))
                                pe.wait_ge(t_free, td + 1)
                                for k in range(2):
                                    for tk in range(2):
                                        last = nc.tensor.transpose(tbank[(td + 2) % 2][:, (2 * k + tk) * P:(2 * k + tk + 1) * P],
                                                                   p_rows[:, tk, k * P:(k + 1) * P], ident[:, :])
                                last.then_inc(t_done, 1)
                        n += 1

                pe.wait_ge(lo_done, 4 * n + 4)
                pe.wait_ge(t_free, td + 3)
                for tok in range(2):
                    pe.wait_ge(h_done, hb + 2 + tok + 1)
                    for j in range(2):
                        for k in range(2):
                            w_k = [b[:, n % 2, k * HALF + j * 512:k * HALF + (j + 1) * 512] for b in (w_hi, w_lo)]
                            last = passes(acc[j][tok][:, :], p_hi[:, k, tok * P:(tok + 1) * P],
                                          p_lo[:, k, tok * P:(tok + 1) * P], *w_k, start=k == 0, stop=k == 1)
                            if (tok, j, k) == (1, 1, 0):
                                last.then_inc(half_used, 1)
                    last.then_inc(blk, 1)
                    if tok == 0:
                        quarter(layer, "ple", 3)
                for j in range(2):
                    for tok in range(2):
                        if j:
                            pe.wait_ge(gate_done, 26 * layer + 2 * HB + tok + 1)
                        product(n + 1 + j, tok, KT, 512, xt(3 * layer + 2), 0, sbank[tok][:, :],
                                waits=x_waits(layer, "ple", tok) if j == 0 else {},
                                mid=early_quarters(layer + 1, "mix", tok) if j and layer < last_layer else {})

            pe.wait_ge(id_in, 16)
            pe.wait_ge(rows_in, 16)
            nc.tensor.transpose(tbank[0][:, 0:13 * KT + 4], rows[:, :], ident[0:13 * KT + 4, 0:13 * KT + 4]).then_inc(t_done, 1)
            quarter(0, "mix", 0)
            quarter(0, "mix", 1)
            pair = 0
            for layer, kind in enumerate(MIXERS):
                if kind == 0:
                    mixer_a(layer, pair)
                    pair += PAIRS
                elif kind == 1:
                    mixer_b(layer)
                else:
                    mixer_c(layer)
                ffn(layer)

        def panel_quarter(n, s):
            q = cnt.half[n] // 2
            a, half = (s % 2) * q, s // 2
            return raw[:, 2 * (n % 2) + half, a:a + q], [b[:, n % 2, half * HALF + a:half * HALF + a + q] for b in (w_hi, w_lo)]

        def hi_index(layer, part, q):
            if part == "mix" and layer == 0:
                return q + 1
            if part == "mix":
                return cnt.hi[layer - 1, "ple"] + q + 1
            if part == "ffn":
                return cnt.hi[layer, "ffn"] - 4 + q + 1
            return cnt.hi[layer, "down"] + (1, 2, 4, 5)[q]

        def norm_of(layer, part):
            return 3 * layer + ("mix", "ffn", "ple").index(part)

        def r_index(norm, tok):
            return 2 * norm + tok + 1 + (2 if norm > 6 else 0)

        def two_late(layer, part):
            return part == "ffn" and MIXERS[layer] == 0

        def row_done(layer, part):
            return 2 if two_late(layer, part) else 3

        def quarter_view(buf, tok, j):
            return buf[:, 4 * j:4 * j + 4, tok * P:(tok + 1) * P]

        def head_rows(bank_, hd):
            return bank_[hd * DH:(hd + 1) * DH, 0:QW].rearrange("p (g x) -> p g x", g=GROUPS)

        def four(ap):
            return ap.rearrange("p (c x) -> p c x", c=4)

        @block.scalar
        def _(act):
            def split(n, i=None, m=0, which=range(4)):
                for s in which:
                    if s == 0 and n >= 2:
                        act.wait_ge(half_used, at(n - 1, i, m))
                    if s == 2 and n >= 2:
                        act.wait_ge(blk, at(2 * n - 2, i, 2 * m))
                    if s % 2 == 0:
                        step = 16 * (cnt.landed[n + m] - cnt.landed[n]) if m else 0
                        act.wait_ge(raw_in[2 * (n % 2) + s // 2], at(16 * cnt.landed[n], i, step))
                    src, (hi, _) = panel_quarter(n, s)
                    nc.scalar.copy(hi, src).then_inc(hi_done, 1)

            def quarter_hi(layer, part, q):
                order, uses, _ = quarters(layer, part)
                tok, j = order[q]
                act.wait_ge(t_free, uses[q] + 1)
                nc.scalar.copy(quarter_view(x_hi[:, norm_of(layer, part) % 2], tok, j), four(xf[:, q % 2, :])
                               ).then_inc(t_hi, 1)

            def sum_squares(norm, tok, ready):
                act.wait_ge(h_done, ready)
                if norm or tok:
                    act.wait_ge(ssq_done, 2 * norm + tok)
                nc.scalar.activation(squares[:, :], h[:, tok, :], ACT.Square,
                                     accum_out=ssq[:, 2 * norm + tok:2 * norm + tok + 1]).then_inc(ssq_done, 1)

            def late_half(layer, part, n, between=lambda: None):
                norm, (_, _, h0) = norm_of(layer, part), quarters(layer, part)
                between()
                split(n, which=(0,))
                if two_late(layer, part):
                    quarter_hi(layer, part, 2)
                split(n, which=(1, 2))
                sum_squares(norm, 0, h0 + row_done(layer, part))
                quarter_hi(layer, part, 3)
                split(n, which=(3,))
                sum_squares(norm, 1, h0 + 4)

            def rows_out_of_psum(layer, n, c, tok, pair):
                act.wait_ge(blk, 2 * (n + c) + tok + 1)
                if c == 2 and pair:
                    act.wait_ge(pv_done, 2 * pair)
                dst = v[:, tok, :, :].rearrange("p g x -> p (g x)") if c == 2 else qk[:, c, tok, :]
                scale = rinv8[:, tok:tok + 1] if c == 0 else rinv[:, 6 * layer + tok:6 * layer + tok + 1]
                nc.scalar.activation(dst, acc[0][tok][:, 0:QW], ACT.Copy, scale=scale).then_inc(qkv_out, 1)

            def qk_hi(c, tok, pair):
                act.wait_ge(qkt_done, 4 * pair + 2 * c + tok + 1)
                dst = (q2, k2)[c]
                places = [(hd, hd) for hd in range(2)] + [(1 - hd, hd) for hd in range(2)] * c
                for half_, hd in places:
                    last = nc.scalar.copy(dst[half_ * DH:(half_ + 1) * DH, hd, :, tok * P:(tok + 1) * P],
                                          head_rows(qkt_bank, hd))
                last.then_inc(qkt_hi, 1)

            def exponentials(u, pair):
                act.wait_ge(top_done, 4 * pair + u + 1)
                width = QW * (u // 2 + 1)
                nc.scalar.activation(e[:, u % 2, 0:width], e[:, u % 2, 0:width], ACT.Exp,
                                     bias=neg_top[:, u:u + 1], accum_out=den[:, u:u + 1]).then_inc(exp_done, 1)

            def exp_out_of_psum(u, pair):
                qt, hd = u // 2, u % 2
                act.wait_ge(et_done, 4 * pair + u + 1)
                if pair or qt:
                    act.wait_ge(pv_done, 2 * pair + qt)
                if qt == 0:
                    nc.scalar.copy(e_t[:, hd, 0:QW], tbank[hd][:, 0:QW]).then_inc(et_out, 1)
                else:
                    nc.scalar.copy(e_t[:, hd, 0:512], tbank[0][:, :])
                    nc.scalar.copy(e_t[:, hd, 512:2 * QW], tbank[1][:, 0:2 * QW - 512]).then_inc(et_out, 1)

            def out_hi(tok, r, pair):
                act.wait_ge(ot_done, 2 * pair + tok + 1)
                nc.scalar.copy(o_hi[:, r, tok * P:(tok + 1) * P], pv_bank[:, 0:P]).then_inc(ot_hi, 1)

            def mixer_a(layer, pair, ready):
                norm = 3 * layer
                if layer == 0:
                    sum_squares(0, 0, 2)
                    split(1, which=(0, 1))
                    sum_squares(0, 1, 4)
                    split(1, which=(2, 3))
                else:
                    late_half(layer, "mix", cnt.n[layer, "mix"] + 1, ready)
                act.wait_ge(r_done, r_index(norm, 1))
                for r in range(PAIRS):
                    n, this, prev = cnt.n[layer, "mix"] + 3 * r, pair + r, pair + r - 1
                    if r:
                        rows_out_of_psum(layer, n - 3, 2, 1, prev)
                        exp_out_of_psum(0, prev)
                        exp_out_of_psum(1, prev)
                        split(n + 1, which=(0, 1))
                        exponentials(2, prev)
                    rows_out_of_psum(layer, n, 0, 0, this)
                    if r:
                        exp_out_of_psum(2, prev)
                        exponentials(3, prev)
                        split(n + 1, which=(2,))
                        out_hi(0, r - 1, prev)
                        qk_hi(0, 0, this)
                        split(n + 1, which=(3,))
                    rows_out_of_psum(layer, n, 0, 1, this)
                    if r:
                        exp_out_of_psum(3, prev)
                    else:
                        qk_hi(0, 0, this)
                    split(n + 2, which=(0,))
                    qk_hi(0, 1, this)
                    split(n + 2, which=(1,))
                    rows_out_of_psum(layer, n, 1, 0, this)
                    split(n + 2, which=(2,))
                    qk_hi(1, 0, this)
                    split(n + 2, which=(3,))
                    rows_out_of_psum(layer, n, 1, 1, this)
                    if r:
                        out_hi(1, r - 1, prev)
                    split(n + 3, which=(0,))
                    qk_hi(1, 1, this)
                    rows_out_of_psum(layer, n, 2, 0, this)
                    split(n + 3, which=(1, 2, 3))
                    exponentials(0, this)
                    exponentials(1, this)
                f, last_pair = n + 4, this
                rows_out_of_psum(layer, n, 2, 1, last_pair)
                exp_out_of_psum(0, last_pair)
                exp_out_of_psum(1, last_pair)
                exponentials(2, last_pair)
                split(f, which=(0,))
                exponentials(3, last_pair)
                exp_out_of_psum(2, last_pair)
                out_hi(0, PAIRS - 1, last_pair)
                split(f, which=(1,))
                exp_out_of_psum(3, last_pair)
                split(f, which=(2, 3))
                quarter_hi(layer, "ffn", 0)
                out_hi(1, PAIRS - 1, last_pair)
                quarter_hi(layer, "ffn", 1)
                late_half(layer, "ffn", f + 1)

            def steps_before(layer, part, n, evacuate=lambda tok, j: None):
                evacuate(1, 0)
                split(n, which=(0,))
                quarter_hi(layer, part, 0)
                split(n, which=(1,))
                quarter_hi(layer, part, 1)
                split(n, which=(2,))
                evacuate(0, 1)
                quarter_hi(layer, part, 2)
                split(n, which=(3,))

            def mixer_b(layer, ready):
                n, norm = cnt.n[layer, "mix"], 3 * layer

                def y_rows(j, tok):
                    act.wait_ge(blk, 2 * (n + j) + tok + 1)
                    nc.scalar.activation(y[:, tok, j * 512:(j + 1) * 512], acc[j][tok][:, :], ACT.Copy,
                                         scale=rinv[:, 2 * norm + tok:2 * norm + tok + 1]).then_inc(y_out, 1)

                late_half(layer, "mix", n + 1, ready)
                act.wait_ge(r_done, r_index(norm, 1))
                y_rows(0, 0)
                y_rows(0, 1)
                split(n + 2)
                y_rows(1, 0)
                y_rows(1, 1)
                for u in range(4):
                    act.wait_ge(z_done, u + 1)
                    nc.scalar.copy(z_hi[:, 2 * u:2 * u + 2, :].rearrange("p c x -> p (c x)"), zbank[u][:, :]
                                   ).then_inc(z_hi_done, 1)
                    split(n + 3, which=(u,))
                for g in range(4):
                    act.wait_ge(*((blk, 2 * (n + 2) + g // 2 + 1) if g % 2 else (z_done, 5 + g // 2)))
                    for eh in range(2):
                        k = 2 * g + eh
                        last = nc.scalar.activation(u_hi[:, k, :], zbank[g][:, eh * SEQ:(eh + 1) * SEQ], ACT.Copy,
                                                    scale=cols[:, BSCALE + k:BSCALE + k + 1])
                    last.then_inc(z_hi_done, 1)
                split(n + 4)
                steps_before(layer, "ffn", n + 5)
                late_half(layer, "ffn", n + 6)

            def mixer_c(layer, ready):
                n, norm, t0 = cnt.n[layer, "mix"], 3 * layer, cnt.t[layer, "mix"]

                def gelu_rows(s, tok):
                    act.wait_ge(blk, 2 * (n + s) + tok + 1)
                    dst = (gv, gu)[s // 2][:, tok, (s % 2) * 512:(s % 2 + 1) * 512]
                    nc.scalar.activation(dst, acc[s % 2][tok][:, :], ACT.Gelu_apprx_tanh,
                                         scale=rinv[:, 2 * norm + tok:2 * norm + tok + 1]).then_inc(y_out, 1)

                late_half(layer, "mix", n + 1, ready)
                act.wait_ge(r_done, r_index(norm, 1))
                for s in range(4):
                    gelu_rows(s, 0)
                    gelu_rows(s, 1)
                    if s < 3:
                        split(n + 2 + s)
                for q in range(4):
                    act.wait_ge(t_done, t0 + 1 + q + 1)
                    nc.scalar.copy(quarter_view(c_hi, q % 2, q // 2), four(tbank[(t0 + 1 + q) % 2][:, :])).then_inc(t_hi, 1)
                split(n + 5)
                steps_before(layer, "ffn", n + 6)
                late_half(layer, "ffn", n + 7)

            def ffn(layer):
                n, t0, hid0, norm = cnt.n[layer, "ffn"], cnt.t[layer, "ffn"], cnt.hid[layer, "ffn"], 3 * layer + 1

                def silu(b, s, tok, i=None):
                    act.wait_ge(blk, at(2 * (n + b) + tok + 1, i, 4))
                    if b:
                        act.wait_ge(hid_done, at(hid0 + 2 * (b - 1) + tok + 1, i, 4))
                    nc.scalar.activation(gated[:, tok, 0:SEQ], acc[s][tok][:, 0:SEQ], ACT.Silu,
                                         scale=rinv[:, 2 * norm + tok:2 * norm + tok + 1]).then_inc(gate_done, 1)

                def hidden_hi(b, bank_, i=None):
                    act.wait_ge(t_done, at(t0 + b + 1, i, 2))
                    k0 = 2 * b if i is None else i * 4 + 2 * b
                    nc.scalar.copy(hid_hi[:, bass.ds(k0, 2), :], tbank[bank_][:, :].rearrange("p (c x) -> p c x", c=2)
                                   ).then_inc(t_hi, 1)

                act.wait_ge(r_done, r_index(norm, 1))
                silu(0, 0, 0)
                with act.Fori(0, (HB - 1) // 2, 1) as i:
                    for s in range(2):
                        silu(s, s, 1, i)
                        split(n + 2 + s, i, 2)
                        hidden_hi(s, (t0 + s) % 2, i)
                        silu(s + 1, (s + 1) % 2, 0, i)
                silu(HB - 1, 0, 1)
                d = cnt.n[layer, "down"]
                split(d + 1)
                hidden_hi(HB - 1, (t0 + HB - 1) % 2)
                split(d + 2)
                split(d + 3)
                split(d + 4, which=(0, 1))
                quarter_hi(layer, "ple", 0)
                quarter_hi(layer, "ple", 1)
                split(d + 4, which=(2, 3))
                split(d + 5, which=(0, 1))
                td = cnt.t[layer, "down"]
                act.wait_ge(t_done, td + 3)
                nc.scalar.copy(p_hi[:, :, :].rearrange("p k x -> p (k x)"), tbank[(td + 2) % 2][:, :]).then_inc(t_hi, 1)
                split(d + 5, which=(2, 3))
                g = cnt.n[layer, "ple"]
                split(g)
                quarter_hi(layer, "ple", 2)
                late_half(layer, "ple", g + 1)
                norm += 1

                def tanh(j, tok):
                    act.wait_ge(blk, 2 * (g + 1 + j) + tok + 1)
                    if j:
                        act.wait_ge(h_done, cnt.h[layer, "ple"] + tok + 1)
                    nc.scalar.activation(gated[:, tok, :], sbank[tok][:, :], ACT.Tanh,
                                         scale=half_r[:, tok:tok + 1]).then_inc(gate_done, 1)

                act.wait_ge(r_done, r_index(norm, 1))
                split(g + 2)
                tanh(0, 0)
                if layer < last_layer:
                    steps_before(layer + 1, "mix", g + 3, lambda tok, j: tanh(j, tok))
                else:
                    tanh(0, 1)
                    tanh(1, 0)
                    sum_squares(12, 0, cnt.h[layer, "ple"] + 3)
                return lambda: tanh(1, 1)

            split(0, which=(0,))
            quarter_hi(0, "mix", 0)
            split(0, which=(1,))
            quarter_hi(0, "mix", 1)
            split(0, which=(2, 3))
            quarter_hi(0, "mix", 2)
            quarter_hi(0, "mix", 3)
            pair = 0
            ready = lambda: None
            for layer, kind in enumerate(MIXERS):
                if kind == 0:
                    mixer_a(layer, pair, ready)
                    pair += PAIRS
                elif kind == 1:
                    mixer_b(layer, ready)
                else:
                    mixer_c(layer, ready)
                ready = ffn(layer)
            ready()
            sum_squares(12, 1, cnt.h[last_layer, "ple"] + 4)

        @block.vector
        def _(dve):
            TT, TS, STT = nc.vector.tensor_tensor, nc.vector.tensor_scalar, nc.vector.scalar_tensor_tensor

            def split(n, i=None, m=0, which=range(4)):
                for s in which:
                    dve.wait_ge(hi_done, at(4 * n + s + 1, i, 4 * m))
                    src, (hi, lo) = panel_quarter(n, s)
                    TT(lo, src, hi.bitcast(F32), ALU.subtract).then_inc(lo_done, 1)

            def quarter_scale(layer, part, q):
                order, uses, _ = quarters(layer, part)
                (tok, j), t = order[q], uses[q]
                c0 = gain_col(norm_of(layer, part), 4 * j)
                gains = bass.AP(tensor=cols[:, :].tensor, offset=c0, ap=[[13 * KT + 4, P], [1, 4], [0, P]])
                before = cnt.x[layer, part] - 4 + q - 1
                if before >= 1:
                    dve.wait_ge(x_done, before)
                dve.wait_ge(t_done, t + 1)
                TT(four(xf[:, q % 2, :]), four(tbank[t % 2][:, :]), gains, ALU.mult).then_inc(t_free, 1)

            def quarter_lo(layer, part, q):
                tok, j = quarters(layer, part)[0][q]
                par = norm_of(layer, part) % 2
                dve.wait_ge(t_hi, hi_index(layer, part, q))
                TT(quarter_view(x_lo[:, par], tok, j), four(xf[:, q % 2, :]),
                   quarter_view(x_hi[:, par], tok, j).bitcast(F32), ALU.subtract).then_inc(x_done, 1)

            def late_half(layer, part, n, update):
                update(1, 1)
                split(n, which=(0,))
                if two_late(layer, part):
                    quarter_scale(layer, part, 2)
                    quarter_lo(layer, part, 2)
                split(n, which=(1,))
                quarter_scale(layer, part, 3)
                split(n, which=(2,))
                quarter_lo(layer, part, 3)
                split(n, which=(3,))

            def steps_before(layer, part, n, update):
                update(1, 0)
                quarter_scale(layer, part, 0)
                split(n, which=(0,))
                quarter_scale(layer, part, 1)
                quarter_lo(layer, part, 0)
                split(n, which=(1,))
                quarter_lo(layer, part, 1)
                update(0, 1)
                quarter_scale(layer, part, 2)
                split(n, which=(2,))
                quarter_lo(layer, part, 2)
                split(n, which=(3,))

            def add_product(n, tok, j):
                dve.wait_ge(blk, 2 * n + tok + 1)
                hj = h[:, tok, j * 512:(j + 1) * 512]
                TT(hj, acc[j][tok][:, :], hj, ALU.add).then_inc(h_done, 1)

            def biased_scores(u, pair):
                qt, hd = u // 2, u % 2
                dve.wait_ge(s_done, 4 * pair + u + 1)
                if u == 0:
                    dve.wait_ge(bias_in, 32 * pair + 32)
                if pair or qt:
                    dve.wait_ge(et_done, 4 * pair + 2 * qt)
                if qt == 0:
                    parts = [(sbank[hd][:, 0:QW].rearrange("p (g x) -> p g x", g=GROUPS), bias[:, hd, :, P:SEQ],
                              e[:, hd, 0:QW].rearrange("p (g x) -> p g x", g=GROUPS))]
                else:
                    parts = [(sbank[0][:, :], bias[:, hd, 0:2, :].rearrange("p g x -> p (g x)"), e[:, hd, 0:512]),
                             (sbank[1][:, 0:SEQ], bias[:, hd, 2, :], e[:, hd, 512:2 * QW])]
                for b, (s_, b_, e_) in enumerate(parts):
                    nc.vector.tensor_tensor_reduce(out=e_, in0=s_, in1=b_, scale=1.0, scalar=-3e38, op0=ALU.add,
                                                   op1=ALU.max, accum_out=tops[:, u, b:b + 1]).then_inc(max_done, 1)
                dve.wait_ge(max_done, 6 * pair + (1, 2, 4, 6)[u])
                TS(neg_top[:, u:u + 1], tops[:, u, 0:1], tops[:, u, qt:qt + 1], -1.0, ALU.max, ALU.mult).then_inc(top_done, 1)

            def qk_lo(c, tok, pair):
                dve.wait_ge(qkt_hi, 4 * pair + 2 * c + tok + 1)
                tokens = slice(tok * P, (tok + 1) * P)
                for hd in range(2):
                    own, other = (slice(x_ * DH, (x_ + 1) * DH) for x_ in (hd, 1 - hd))
                    dst = k_lo[own, :, tokens] if c else q2[other, hd, :, tokens]
                    last = TT(dst, head_rows(qkt_bank, hd), (q2, k2)[c][own, hd, :, tokens].bitcast(F32), ALU.subtract)
                last.then_inc(qkt_out, 1)

            def normalised(qt, pair):
                dve.wait_ge(pv_done, 2 * pair + qt + 1)
                nc.vector.reciprocal(rden[:, 2 * qt:2 * qt + 2], den[:, 2 * qt:2 * qt + 2]).then_inc(rden_done, 1)
                dve.wait_ge(rden_done, 2 * pair + qt + 1)
                for hd in range(2):
                    last = TS(o[:, qt, hd * DH:(hd + 1) * DH], pv_bank[:, hd * DH:(hd + 1) * DH],
                              rden[:, 2 * qt + hd:2 * qt + hd + 1], None, ALU.mult)
                last.then_inc(o_done, 1)

            def out_lo(tok, r, pair):
                dve.wait_ge(ot_hi, 2 * pair + tok + 1)
                TT(o_lo[:, r, tok * P:(tok + 1) * P], pv_bank[:, 0:P], o_hi[:, r, tok * P:(tok + 1) * P].bitcast(F32),
                   ALU.subtract).then_inc(ot_lo, 1)

            def mixer_a(layer, pair, update):
                if layer:
                    late_half(layer, "mix", cnt.n[layer, "mix"] + 1, update)
                else:
                    split(1, which=(0,))
                    for g in range(GROUPS):
                        split(1, which=(g + 1,))
                        dve.wait_ge(t_done, 5 + g + 1)
                        nc.vector.tensor_copy(offsets[:, g, :], tbank[(5 + g) % 2][0:HEADS, 0:SKEW]).then_inc(t_free, 1)
                for r in range(PAIRS):
                    n, this, prev = cnt.n[layer, "mix"] + 3 * r, pair + r, pair + r - 1
                    if r:
                        split(n + 1, which=(0,))
                        biased_scores(2, prev)
                        split(n + 1, which=(1,))
                        normalised(0, prev)
                        biased_scores(3, prev)
                        split(n + 1, which=(2,))
                        out_lo(0, r - 1, prev)
                    qk_lo(0, 0, this)
                    if r:
                        split(n + 1, which=(3,))
                    split(n + 2, which=(0,))
                    qk_lo(0, 1, this)
                    split(n + 2, which=(1,))
                    if r:
                        normalised(1, prev)
                    split(n + 2, which=(2,))
                    qk_lo(1, 0, this)
                    split(n + 2, which=(3,))
                    if r:
                        out_lo(1, r - 1, prev)
                    split(n + 3, which=(0,))
                    qk_lo(1, 1, this)
                    split(n + 3, which=(1,))
                    biased_scores(0, this)
                    biased_scores(1, this)
                    split(n + 3, which=(2, 3))
                w, f, last_pair = n + 3, n + 4, this
                biased_scores(2, last_pair)
                biased_scores(3, last_pair)
                normalised(0, last_pair)
                split(f, which=(0,))
                out_lo(0, PAIRS - 1, last_pair)
                split(f, which=(1,))
                add_product(w, 0, 0)
                add_product(w, 0, 1)
                split(f, which=(2,))
                normalised(1, last_pair)
                quarter_scale(layer, "ffn", 0)
                quarter_scale(layer, "ffn", 1)
                quarter_lo(layer, "ffn", 0)
                out_lo(1, PAIRS - 1, last_pair)
                quarter_lo(layer, "ffn", 1)
                split(f, which=(3,))
                add_product(w, 1, 0)
                add_product(w, 1, 1)
                late_half(layer, "ffn", f + 1, lambda tok, j: None)

            def mixer_b(layer, update):
                n = cnt.n[layer, "mix"]
                late_half(layer, "mix", n + 1, update)
                split(n + 2)
                for u in range(4):
                    dve.wait_ge(z_hi_done, u + 1)
                    TT(z_lo[:, 2 * u:2 * u + 2, :].rearrange("p c x -> p (c x)"), zbank[u][:, :],
                       z_hi[:, 2 * u:2 * u + 2, :].rearrange("p c x -> p (c x)").bitcast(F32), ALU.subtract
                       ).then_inc(z_lo_done, 1)
                    split(n + 3, which=(u,))
                for g in range(4):
                    dve.wait_ge(z_hi_done, 5 + g)
                    for eh in range(2):
                        k = 2 * g + eh
                        last = STT(u_lo[:, k, :], zbank[g][:, eh * SEQ:(eh + 1) * SEQ], cols[:, BSCALE + k:BSCALE + k + 1],
                                   u_hi[:, k, :].bitcast(F32), ALU.mult, ALU.subtract)
                    last.then_inc(z_lo_done, 1)
                split(n + 4)
                add_product(n + 3, 0, 0)
                steps_before(layer, "ffn", n + 5, lambda tok, j: add_product(n + 3 + j, tok, j))
                late_half(layer, "ffn", n + 6, lambda tok, j: add_product(n + 3 + j, tok, j))

            def mixer_c(layer, update):
                n, t0 = cnt.n[layer, "mix"], cnt.t[layer, "mix"]
                y0, hi0 = 4, cnt.hi[layer, "mix"]
                late_half(layer, "mix", n + 1, update)
                dve.wait_ge(part_in, 64)
                tril4 = bass.AP(tensor=tril[:, :].tensor, offset=0, ap=[[P, P], [0, 4], [1, P]])
                TT(w_s[:, :, :], w_s[:, :, :], tril4, ALU.mult).then_inc(masked, 1)
                split(n + 2)
                split(n + 3)
                step = 0
                for tok in range(2):
                    dve.wait_ge(y_out, y0 + 2 + tok + 1)
                    for j in range(2):
                        nc.vector.bn_stats(stats[:, tok, j, :], gv[:, tok, j * 512:(j + 1) * 512]).then_inc(dve_step, 1)
                    step += 2
                    dve.wait_ge(dve_step, step)
                    nc.vector.bn_aggr(mv[:, tok, :], stats[:, tok, :, :]).then_inc(ln_stat, 1)
                dve.wait_ge(t_done, t0 + 1)
                nc.vector.tensor_copy(w_st[:, :, :].rearrange("p g x -> p (g x)"), tbank[t0 % 2][:, :]).then_inc(t_free, 1)
                for tok in range(2):
                    dve.wait_ge(ln_stat, tok + 1)
                    dve.wait_ge(r_done, 2 * 7 + tok + 1)
                    TS(gv[:, tok, :], gv[:, tok, :], mv[:, tok, 0:1], rinv[:, 26 + tok:27 + tok],
                       ALU.subtract, ALU.mult).then_inc(dve_step, 1)
                    step += 1
                    dve.wait_ge(dve_step, step)
                    TT(gv[:, tok, :], gv[:, tok, :], gain_v[:, :], ALU.mult).then_inc(v_done, 1)
                split(n + 4)
                for half_ in range(2):
                    for q in (2 * half_, 2 * half_ + 1):
                        tok, j = q % 2, q // 2
                        dve.wait_ge(sp_done, q + 1)
                        dve.wait_ge(y_out, y0 + 4 + q + 1)
                        for s in range(2):
                            g = 2 * j + s
                            gu_ = gu[:, tok, g * SEQ:(g + 1) * SEQ]
                            last = STT(gu_, sbank[tok][:, s * SEQ:(s + 1) * SEQ], cols[:, BSP + g:BSP + g + 1], gu_,
                                       ALU.add, ALU.mult)
                        last.then_inc(gate_out, 1)
                    for q in (2 * half_, 2 * half_ + 1):
                        tok, j = q % 2, q // 2
                        dve.wait_ge(t_hi, hi0 + q + 1)
                        TT(quarter_view(c_lo, tok, j), four(tbank[(t0 + 1 + q) % 2][:, :]),
                           quarter_view(c_hi, tok, j).bitcast(F32), ALU.subtract).then_inc(t_free, 1)
                split(n + 5)
                add_product(n + 4, 0, 0)
                steps_before(layer, "ffn", n + 6, lambda tok, j: add_product(n + 4 + j, tok, j))
                late_half(layer, "ffn", n + 7, lambda tok, j: add_product(n + 4 + j, tok, j))

            def ffn(layer):
                n, t0, norm = cnt.n[layer, "ffn"], cnt.t[layer, "ffn"], 3 * layer + 1
                hi0, g0 = cnt.hi[layer, "ffn"], 26 * layer

                def hidden(b, s, tok, i=None):
                    dve.wait_ge(gate_done, at(g0 + 2 * b + tok + 1, i, 4))
                    STT(prod[:, tok, 0:SEQ], acc[s][tok][:, SEQ:512], rinv[:, 2 * norm + tok:2 * norm + tok + 1],
                        gated[:, tok, 0:SEQ], ALU.mult, ALU.mult).then_inc(hid_done, 1)

                def hidden_lo(b, bank_, i=None):
                    dve.wait_ge(t_hi, at(hi0 + b + 1, i, 2))
                    k0 = 2 * b if i is None else i * 4 + 2 * b
                    TT(hid_lo[:, bass.ds(k0, 2), :], tbank[bank_][:, :].rearrange("p (c x) -> p c x", c=2),
                       hid_hi[:, bass.ds(k0, 2), :].bitcast(F32), ALU.subtract).then_inc(t_free, 1)

                hidden(0, 0, 0)
                with dve.Fori(0, (HB - 1) // 2, 1) as i:
                    for s in range(2):
                        hidden(s, s, 1, i)
                        split(n + 2 + s, i, 2)
                        hidden_lo(s, (t0 + s) % 2, i)
                        hidden(s + 1, (s + 1) % 2, 0, i)
                hidden(HB - 1, 0, 1)
                d = cnt.n[layer, "down"]
                split(d + 1)
                hidden_lo(HB - 1, (t0 + HB - 1) % 2)
                split(d + 2)
                split(d + 3)
                add_product(d + 2, 0, 0)

                def down(tok, j):
                    add_product(d + 2 + 3 * j, tok, j)

                down(1, 0)
                split(d + 4, which=(0, 1))
                for q in range(2):
                    quarter_scale(layer, "ple", q)
                for q in range(2):
                    quarter_lo(layer, "ple", q)
                split(d + 4, which=(2, 3))
                split(d + 5, which=(0, 1))
                td = cnt.t[layer, "down"]
                dve.wait_ge(t_hi, cnt.hi[layer, "down"] + 3)
                TT(p_lo[:, :, :].rearrange("p k x -> p (k x)"), tbank[(td + 2) % 2][:, :],
                   p_hi[:, :, :].rearrange("p k x -> p (k x)").bitcast(F32), ALU.subtract).then_inc(t_free, 1)
                split(d + 5, which=(2, 3))
                g = cnt.n[layer, "ple"]
                split(g)
                down(0, 1)
                quarter_scale(layer, "ple", 2)
                quarter_lo(layer, "ple", 2)
                late_half(layer, "ple", g + 1, down)

                def embed(tok, j):
                    dve.wait_ge(gate_done, g0 + 2 * HB + 2 * j + tok + 1)
                    STT(prod[:, tok, :], gated[:, tok, :], 1.0, acc[j][tok][:, :], ALU.add, ALU.mult).then_inc(embed_step, 1)
                    dve.wait_ge(embed_step, 4 * layer + 2 * j + tok + 1)
                    hj = h[:, tok, j * 512:(j + 1) * 512]
                    STT(hj, prod[:, tok, :], 0.5, hj, ALU.mult, ALU.add).then_inc(h_done, 1)

                split(g + 2)
                embed(0, 0)
                if layer < last_layer:
                    steps_before(layer + 1, "mix", g + 3, embed)
                else:
                    embed(1, 0)
                    embed(0, 1)
                return embed

            dve.sem_inc(hid_done, 2)
            nc.vector.memset(expo[:, :], -0.5).then_inc(expo_set, 1)
            nc.vector.memset(table[32:33, :], 1.0).then_inc(table_one, 1)
            dve.wait_ge(x_in[0], 16)
            dve.sem_inc(h_done, 2)
            dve.wait_ge(t_done, 1)
            nc.vector.tensor_copy(cols[:, :], tbank[0][:, 0:13 * KT + 4]).then_inc(t_free, 1)
            dve.wait_ge(t_free, 1)
            quarter_scale(0, "mix", 0)
            quarter_scale(0, "mix", 1)
            split(0, which=(0,))
            quarter_lo(0, "mix", 0)
            split(0, which=(1,))
            quarter_lo(0, "mix", 1)
            split(0, which=(2,))
            dve.wait_ge(x_in[1], 16)
            dve.sem_inc(h_done, 2)
            quarter_scale(0, "mix", 2)
            split(0, which=(3,))
            quarter_scale(0, "mix", 3)
            quarter_lo(0, "mix", 2)
            quarter_lo(0, "mix", 3)
            update = lambda tok, j: None
            pair = 0
            for layer, kind in enumerate(MIXERS):
                if kind == 0:
                    mixer_a(layer, pair, update)
                    pair += PAIRS
                elif kind == 1:
                    mixer_b(layer, update)
                else:
                    mixer_c(layer, update)
                update = ffn(layer)
            dve.wait_ge(part_in, 80)
            for tok in range(2):
                if tok:
                    update(1, 1)
                dve.wait_ge(r_done, r_index(12, tok))
                for j in range(2):
                    c = slice(j * 512, (j + 1) * 512)
                    STT(result[:, tok, c], h[:, tok, c], rinv[:, 24 + tok:25 + tok], gain_f[:, c],
                        ALU.mult, ALU.mult).then_inc(result_done, 1)

        @block.gpsimd
        def _(pool):
            steps = [0]

            def chained(ins):
                steps[0] += 1
                ins.then_inc(r_step, 1)
                pool.wait_ge(r_step, steps[0])

            def inverse_root(col, src, scale):
                m = mean_sq[:, col:col + 1]
                chained(nc.gpsimd.tensor_scalar(m, src, scale, EPS, ALU.mult, ALU.add))
                return nc.gpsimd.tensor_tensor(rinv[:, col:col + 1], m, expo[:, :], ALU.pow)

            def inverse_rms(norm):
                for tok in range(2):
                    col = 2 * norm + tok
                    pool.wait_ge(ssq_done, col + 1)
                    ins = inverse_root(col, ssq[:, col:col + 1], 1.0 / D)
                    scaled, by = {0: (rinv8, 1 / 8), 2: (half_r, 0.5)}.get(norm % 3, (None, None))
                    if norm < 12 and scaled is not None:
                        chained(ins)
                        ins = nc.gpsimd.tensor_scalar(scaled[:, tok:tok + 1], rinv[:, col:col + 1], by, None, ALU.mult)
                    ins.then_inc(r_done, 1)

            skewed = bass.AP(tensor=bias_skew.tensor, offset=P - 1,
                             ap=[[2 * P * SKEW, PAIRS], [P * SKEW, 2], [SKEW - 1, P], [HEADS * P * SKEW, GROUPS], [1, SEQ]])

            skew_rows = bias_skew.rearrange("(g n) p u -> g n p u", g=GROUPS)

            def load_bias(pair, i=None):
                for hd in range(2):
                    pool.dma_start(bias[:, hd, :, :], skewed[pair if i is None else i + pair, hd]).then_inc(bias_in, 16)

            pool.wait_ge(expo_set, 1)
            done = 0
            for layer, kind in enumerate(MIXERS):
                if layer == 0:
                    inverse_rms(0)
                    pool.wait_ge(t_free, 8)
                    pool.dma_start(bias_rows.rearrange("(g n) u -> n g u", g=GROUPS), offsets).then_inc(rows_out, 16)
                    pool.wait_ge(rows_out, 16)
                    for hd in range(2):
                        pool.dma_start(skew_rows[:, hd], bass.AP(tensor=bias_rows.tensor, offset=hd * SKEW,
                                       ap=[[HEADS * SKEW, GROUPS], [0, P], [1, SKEW]])).then_inc(rows_out, 16)
                    pool.wait_ge(rows_out, 48)
                else:
                    inverse_rms(3 * layer)
                if kind == 0:
                    load_bias(0)
                    if layer == 0:
                        for g in range(GROUPS):
                            pool.dma_start(skew_rows[g, 2:HEADS], bass.AP(tensor=bias_rows.tensor, offset=(g * HEADS + 2) * SKEW,
                                           ap=[[SKEW, HEADS - 2], [0, P], [1, SKEW]])).then_inc(rows_out, 16)
                        pool.wait_ge(rows_out, 96)
                    with pool.Fori(0, PAIRS - 1, 1) as i:
                        pool.wait_ge(top_done, at(4 * done + 4, i, 4))
                        load_bias(1, i)
                    done += PAIRS
                if kind == 2:
                    for tok in range(2):
                        pool.wait_ge(ln_stat, tok + 1)
                        inverse_root(26 + tok, mv[:, tok, 1:2], 1.0).then_inc(r_done, 1)
                inverse_rms(3 * layer + 1)
                inverse_rms(3 * layer + 2)
            inverse_rms(12)


_INS = ["x", "p", "rel_table", "final_norm", "a_w_qkv", "a_w_o", "b_w_in", "b_w_grp", "b_w_out",
        "c_w_in", "c_v_gain", "c_w_s", "c_w_out", "vectors", "ffn_w_gate", "ffn_w_up", "ffn_w_down",
        "ple_w_gate", "ple_w_proj"]
_VECTORS = ["norm_mix", "norm_ffn", "norm_ple", "b_scale", "c_b_s"]
_CONSTS = ["identity", "bucket_of", "pool_of", "lower"]
_OUTS = [((1, SEQ, D), "float32")]


def constants():
    f32 = np.float32
    bucket_of = np.zeros((33, GROUPS, SKEW), f32)
    for g, d in enumerate((1, 4, 16)):
        n = SEQ - 1 - np.arange(SKEW)
        near = np.maximum(n, 1).astype(f32)
        large = 16 + (np.log(near / 16) / np.log(2048 / 16) * 16).astype(np.int32)
        bucket = np.where(n < 16, n, np.minimum(large, 31))
        seen = (n >= 0) & (n % d == 0) & (n <= 128 * d)
        bucket_of[bucket[seen], g, np.flatnonzero(seen)] = 1.0
        bucket_of[32, g, ~seen] = NEG
    full = np.zeros((4, SEQ, SEQ), f32)
    for g, win in enumerate((2, 4, 8, 16)):
        for s in range(SEQ):
            full[g, max(0, s - win + 1):s + 1, s] = f32(1.0) / f32(min(s + 1, win))
            full[g, s, s] -= f32(1.0)
    pool_of = np.concatenate([full[:, :P, :], full[:, P:, P:]], axis=2).transpose(1, 0, 2)
    return {"identity": np.eye(P, dtype=f32), "bucket_of": bucket_of,
            "pool_of": np.ascontiguousarray(pool_of), "lower": np.tril(np.ones((P, P), f32))}


def kernel(**inputs):
    import concourse.bacc as _bacc
    from concourse.bass_utils import run_bass_kernel_spmd as _run

    nc = _bacc.Bacc("TRN2", target_bir_lowering=False, num_devices=1)
    const = constants()
    inputs["vectors"] = np.concatenate([np.asarray(inputs[name]).reshape(-1, P) for name in _VECTORS])
    arrays, args = {}, []
    for name in _INS + _CONSTS:
        a = np.ascontiguousarray(inputs[name] if name in _INS else const[name])
        arrays[f"in_{name}_dram"] = a
        args.append(nc.dram_tensor(f"in_{name}_dram", a.shape, mybir.dt.from_np(a.dtype), kind="ExternalInput").ap())
    for i, (shape, dtype) in enumerate(_OUTS):
        args.append(nc.dram_tensor(f"out_{i}_dram", shape, mybir.dt.from_np(np.dtype(dtype)), kind="ExternalOutput").ap())
    trunk(nc, *args)
    r = _run(nc, [arrays], core_ids=[0])
    return r.results[0]["out_0_dram"]
```
